# Optimizing a Trainium2 kernel written in Bass

```python
import math
import jax, jax.numpy as jnp
from jax import lax
import numpy as np

D_MODEL = 1024
BATCH = 1
SEQ = 1024
DEPTH = 1
DEC_BATCH = 8
DEC_SEQ = 4
PAST_LEN = 8192
PAGE_SIZE = 128

MIX_WIDTH = D_MODEL
CONV_CH = MIX_WIDTH // 2
CONV_K = 3
N_HEADS = 4
V_HEAD = (MIX_WIDTH - CONV_CH) // N_HEADS
QK_HEAD = V_HEAD // 2
ROT_DIM = QK_HEAD // 4
ROPE_THETA = 500000.0
D_FF = -(-8 * D_MODEL // (3 * 256)) * 256
Q_BLOCK = 128
N_MOD = 6
ALPHA = (2.0 * DEPTH) ** 0.25
BETA = (8.0 * DEPTH) ** -0.25
LN_EPS = 1e-5
SPLITS = (CONV_CH, CONV_CH, CONV_CH, N_HEADS * 2 * QK_HEAD, N_HEADS * 2 * QK_HEAD, N_HEADS * V_HEAD)
SPLIT_IDX = tuple(int(i) for i in np.cumsum(SPLITS)[:-1])
IN_WIDTH = sum(SPLITS)

kernel_name = 'hybrid_shortconv_diffattn_step'

def layer_norm(x, g, b):
    xf = x.astype(jnp.float32)
    mu = jnp.mean(xf, -1, keepdims=True)
    var = jnp.mean(jnp.square(xf - mu), -1, keepdims=True)
    return ((xf - mu) * lax.rsqrt(var + LN_EPS) * g.astype(jnp.float32) + b.astype(jnp.float32)).astype(x.dtype)

def rope_tables(pos):
    inv = ROPE_THETA ** (-jnp.arange(0, ROT_DIM, 2, dtype=jnp.float32) / ROT_DIM)
    ang = pos.astype(jnp.float32)[:, None] * inv[None, :]
    return jnp.cos(ang), jnp.sin(ang)

def apply_rope(x, cos, sin):
    c = cos[None, :, None, None, :]
    s = sin[None, :, None, None, :]
    xr = x[..., :ROT_DIM].astype(jnp.float32)
    x1, x2 = xr[..., :ROT_DIM // 2], xr[..., ROT_DIM // 2:]
    rot = jnp.concatenate([x1 * c - x2 * s, x2 * c + x1 * s], axis=-1)
    return jnp.concatenate([rot.astype(x.dtype), x[..., ROT_DIM:]], axis=-1)

def adaln(c, w, b):
    m = jax.nn.silu(c) @ w + b
    return m.reshape(c.shape[0], N_MOD, D_MODEL)

def modulate(x, shift, scale):
    return x * (1 + scale[:, None, :]) + shift[:, None, :]

def mixer_inputs(x, mod, w_in, cos, sin):
    b, t, _ = x.shape
    z = modulate(x, mod[:, 0], mod[:, 1]) @ w_in
    h, gb, gc, q, k, v = jnp.split(z, SPLIT_IDX, axis=-1)
    q = apply_rope(q.reshape(b, t, N_HEADS, 2, QK_HEAD), cos, sin)
    k = apply_rope(k.reshape(b, t, N_HEADS, 2, QK_HEAD), cos, sin)
    v = v.reshape(b, t, N_HEADS, V_HEAD)
    return h, gb, gc, q, k, v

def short_conv(u_ext, w):
    t = u_ext.shape[1] - (CONV_K - 1)
    return sum(w[j] * u_ext[:, j:j + t] for j in range(CONV_K))

def diff_attend(q, q_pos, k, v, k_pos, lam):
    s = jnp.einsum('bqhcd,bkhcd->bhcqk', q, k).astype(jnp.float32) * (QK_HEAD ** -0.5)
    mask = k_pos[None, :] <= q_pos[:, None]
    s = jnp.where(mask, s, -jnp.inf)
    p = jax.nn.softmax(s, axis=-1)
    a = p[:, :, 0] - lam * p[:, :, 1]
    return jnp.einsum('bhqk,bkhd->bqhd', a, v.astype(jnp.float32))

def head_out(o, g, lam_init, dtype):
    o = o * lax.rsqrt(jnp.mean(jnp.square(o), -1, keepdims=True) + LN_EPS) * g.astype(jnp.float32)
    o = o * (1.0 - lam_init)
    b, t = o.shape[:2]
    return o.reshape(b, t, N_HEADS * V_HEAD).astype(dtype)

def finish(x, y_mix, mod, w_out, ln1_g, ln1_b, w_gate, w_up, w_down, ln2_g, ln2_b):
    x = layer_norm(ALPHA * x + mod[:, 2][:, None, :] * (y_mix @ w_out), ln1_g, ln1_b)
    hf = modulate(x, mod[:, 3], mod[:, 4])
    f = (jax.nn.silu(hf @ w_gate) * (hf @ w_up)) @ w_down
    return layer_norm(ALPHA * x + mod[:, 5][:, None, :] * f, ln2_g, ln2_b)

def setup_inputs(seed: int = 0) -> dict:
    key = jax.random.key(seed)
    ks = jax.random.split(key, 26)
    f32 = jnp.float32
    n_pages = PAST_LEN // PAGE_SIZE
    n_used = DEC_BATCH * n_pages
    n_pool = (5 * n_used + 3) // 4

    def nrm(k, shape, s):
        return jax.random.normal(k, shape, f32) * s

    sd = D_MODEL ** -0.5
    v_col = jnp.concatenate([jnp.ones((IN_WIDTH - N_HEADS * V_HEAD,), f32),
                             jnp.full((N_HEADS * V_HEAD,), BETA, f32)])
    page_table = jax.random.permutation(ks[7], n_pool)[:n_used].reshape(DEC_BATCH, n_pages).astype(jnp.int32)
    return dict(
        x_prompt=nrm(ks[0], (BATCH, SEQ, D_MODEL), 1.0),
        x_sample=nrm(ks[1], (DEC_BATCH, DEC_SEQ, D_MODEL), 1.0),
        c_prompt=nrm(ks[2], (BATCH, D_MODEL), 1.0),
        c_sample=nrm(ks[3], (DEC_BATCH, D_MODEL), 1.0),
        cache_k=nrm(ks[4], (DEPTH, n_pool, PAGE_SIZE, N_HEADS, 2 * QK_HEAD), 1.0),
        cache_v=nrm(ks[5], (DEPTH, n_pool, PAGE_SIZE, N_HEADS, V_HEAD), 1.0),
        state_conv=nrm(ks[6], (DEPTH, DEC_BATCH, CONV_K - 1, CONV_CH), 1.0),
        page_table=page_table,
        w_ada=nrm(ks[8], (DEPTH, D_MODEL, N_MOD * D_MODEL), 0.5 * sd),
        b_ada=nrm(ks[9], (DEPTH, N_MOD * D_MODEL), 0.01),
        w_in=nrm(ks[10], (DEPTH, D_MODEL, IN_WIDTH), sd) * v_col,
        conv_w=nrm(ks[11], (DEPTH, CONV_K, CONV_CH), CONV_K ** -0.5),
        lambda_q1=nrm(ks[12], (DEPTH, QK_HEAD), 0.1),
        lambda_k1=nrm(ks[13], (DEPTH, QK_HEAD), 0.1),
        lambda_q2=nrm(ks[14], (DEPTH, QK_HEAD), 0.1),
        lambda_k2=nrm(ks[15], (DEPTH, QK_HEAD), 0.1),
        subln_g=1.0 + nrm(ks[16], (DEPTH, V_HEAD), 0.02),
        w_out=nrm(ks[17], (DEPTH, MIX_WIDTH, D_MODEL), BETA * MIX_WIDTH ** -0.5),
        ln1_g=1.0 + nrm(ks[18], (DEPTH, D_MODEL), 0.02),
        ln1_b=nrm(ks[19], (DEPTH, D_MODEL), 0.02),
        w_gate=nrm(ks[20], (DEPTH, D_MODEL, D_FF), sd),
        w_up=nrm(ks[21], (DEPTH, D_MODEL, D_FF), sd),
        w_down=nrm(ks[22], (DEPTH, D_FF, D_MODEL), BETA * D_FF ** -0.5),
        ln2_g=1.0 + nrm(ks[23], (DEPTH, D_MODEL), 0.02),
        ln2_b=nrm(ks[24], (DEPTH, D_MODEL), 0.02),
    )

def reference(x_prompt, x_sample, c_prompt, c_sample, cache_k, cache_v, state_conv, page_table,
              w_ada, b_ada, w_in, conv_w, lambda_q1, lambda_k1, lambda_q2, lambda_k2, subln_g,
              w_out, ln1_g, ln1_b, w_gate, w_up, w_down, ln2_g, ln2_b):
    bp, s_len = x_prompt.shape[0], x_prompt.shape[1]
    bs, t_len = x_sample.shape[0], x_sample.shape[1]
    past = page_table.shape[1] * cache_k.shape[2]
    n_blk = s_len // Q_BLOCK

    pos_p = jnp.arange(s_len)
    cos_p, sin_p = rope_tables(pos_p)
    q_pos_s = past + jnp.arange(t_len)
    cos_s, sin_s = rope_tables(q_pos_s)
    k_pos_s = jnp.arange(past + t_len)
    q_pos_blocks = pos_p.reshape(n_blk, Q_BLOCK)

    xp, xs = x_prompt, x_sample
    kp_l, vp_l, cp_l, ks_l, vs_l, cs_l = [], [], [], [], [], []
    for l in range(DEPTH):
        lam_init = 0.8 - 0.6 * math.exp(-0.3 * l)
        lam = (jnp.exp(jnp.sum(lambda_q1[l].astype(jnp.float32) * lambda_k1[l].astype(jnp.float32)))
               - jnp.exp(jnp.sum(lambda_q2[l].astype(jnp.float32) * lambda_k2[l].astype(jnp.float32)))
               + lam_init)

        mod_p = adaln(c_prompt, w_ada[l], b_ada[l])
        h, gb, gc, q, k, v = mixer_inputs(xp, mod_p, w_in[l], cos_p, sin_p)
        u_ext = jnp.concatenate([jnp.zeros((bp, CONV_K - 1, CONV_CH), h.dtype), gc * h], axis=1)
        y_conv = gb * short_conv(u_ext, conv_w[l])
        qb = jnp.moveaxis(q.reshape(bp, n_blk, Q_BLOCK, N_HEADS, 2, QK_HEAD), 1, 0)
        ob = lax.map(lambda a: diff_attend(a[0], a[1], k, v, pos_p, lam), (qb, q_pos_blocks))
        o = jnp.moveaxis(ob, 0, 1).reshape(bp, s_len, N_HEADS, V_HEAD)
        y_attn = head_out(o, subln_g[l], lam_init, xp.dtype)
        xp = finish(xp, jnp.concatenate([y_conv, y_attn], axis=-1), mod_p, w_out[l],
                    ln1_g[l], ln1_b[l], w_gate[l], w_up[l], w_down[l], ln2_g[l], ln2_b[l])
        kp_l.append(k.reshape(bp, s_len, N_HEADS, 2 * QK_HEAD))
        vp_l.append(v)
        cp_l.append(u_ext[:, -(CONV_K - 1):])

        mod_s = adaln(c_sample, w_ada[l], b_ada[l])
        h, gb, gc, q, k, v = mixer_inputs(xs, mod_s, w_in[l], cos_s, sin_s)
        u_ext = jnp.concatenate([state_conv[l].astype(h.dtype), gc * h], axis=1)
        y_conv = gb * short_conv(u_ext, conv_w[l])
        k_past = cache_k[l, page_table].reshape(bs, past, N_HEADS, 2, QK_HEAD)
        v_past = cache_v[l, page_table].reshape(bs, past, N_HEADS, V_HEAD)
        k_all = jnp.concatenate([k_past.astype(k.dtype), k], axis=1)
        v_all = jnp.concatenate([v_past.astype(v.dtype), v], axis=1)
        o = diff_attend(q, q_pos_s, k_all, v_all, k_pos_s, lam)
        y_attn = head_out(o, subln_g[l], lam_init, xs.dtype)
        xs = finish(xs, jnp.concatenate([y_conv, y_attn], axis=-1), mod_s, w_out[l],
                    ln1_g[l], ln1_b[l], w_gate[l], w_up[l], w_down[l], ln2_g[l], ln2_b[l])
        ks_l.append(k.reshape(bs, t_len, N_HEADS, 2 * QK_HEAD))
        vs_l.append(v)
        cs_l.append(u_ext[:, -(CONV_K - 1):])

    return (xp, xs, jnp.stack(kp_l), jnp.stack(vp_l), jnp.stack(cp_l),
            jnp.stack(ks_l), jnp.stack(vs_l), jnp.stack(cs_l))


_drawn_inputs = setup_inputs


def setup_inputs(seed=0):
    import zlib

    import numpy as np

    out = dict(_drawn_inputs(seed))
    spreads = {}
    factors = {'b_ada': 3.093,
     'lambda_q1': 8.0,
     'lambda_k1': 4.502,
     'lambda_q2': 64.0,
     'lambda_k2': 7.251,
     'subln_g': 34.607,
     'ln1_g': 8.009,
     'ln1_b': 7.708,
     'ln2_g': 8.482,
     'ln2_b': 8.291}
    for name, (base, spread) in spreads.items():
        noise = np.random.default_rng([zlib.crc32(name.encode()), seed]).standard_normal(out[name].shape)
        drawn = base * np.exp(spread * noise) if base else spread * noise
        out[name] = __import__('jax').numpy.asarray(drawn.astype(out[name].dtype))
    for name, factor in factors.items():
        out[name] = (out[name] * factor).astype(out[name].dtype)
    return out
```

```python
import math
from contextlib import ExitStack, contextmanager

import numpy as np

import concourse.bass as bass
from concourse import mybir

F32 = mybir.dt.float32
F32R = mybir.dt.float32r
I32 = mybir.dt.int32
ALU = mybir.AluOpType
ACT = mybir.ActivationFunctionType
AX_X = mybir.AxisListType.X
ds = bass.ds

P = 128
QUAD = 32
BANK = 512
ROPE_THETA = 500000.0
LN_EPS = 1e-5
MASKED = -1.0e30


class Shapes:

    def __init__(self, s):
        self.T, self.D = s["x_prompt"][1:]
        self.B, self.S = s["x_sample"][:2]
        self.DEPTH, self.POOL, self.PAGE, self.H, self.HD = s["cache_k"]
        self.PAGES = s["page_table"][1]
        self.F = s["w_gate"][2]
        self.IN = s["w_in"][2]
        self.CC = s["conv_w"][2]
        self.MODS = s["w_ada"][2] // self.D
        self.BS = self.B * self.S
        self.KC = self.D // P
        self.NT = self.T // P
        self.CH = min(BANK, self.T)
        self.NCH = self.T // self.CH
        self.NF = self.F // P
        self.AW = self.H * self.HD
        self.ALPHA = (2.0 * self.DEPTH) ** 0.25
        assert self.DEPTH == 1 and self.PAGE == P and self.HD == P and self.H == 4
        assert self.BS == QUAD and self.KC % 4 == 0 and self.T % (2 * P) == 0 and self.F % 256 == 0
        assert self.PAGES % 16 == 0 and self.CC == self.AW == 512 and self.B == 8 and self.S == 4


def constants(z):
    p = np.arange(P)
    out = {}
    out["ident"] = np.eye(P)
    out["quad_fold"] = (p[:, None] % QUAD == np.arange(QUAD)[None, :])
    out["pick_prompt"] = np.repeat((p % QUAD == 0)[:, None], P, axis=1)
    out["pick_sample"] = (p[:, None] % QUAD == 1 + np.arange(QUAD)[None, :] // z.S)
    h, q = p // QUAD, p % 8
    out["head_fold"] = (h[:, None] == h[None, :]) & (q[:, None] == q[None, :])
    out["causal"] = np.where(p[None, :] <= p[:, None], 0.0, MASKED)
    a, t = (p // 8) % 4, p % z.S
    bb, tt = np.arange(QUAD) // z.S, np.arange(QUAD) % z.S
    ok = (a[:, None, None] == 0) & (np.arange(z.B)[None, :, None] == bb[None, None, :]) & (
        tt[None, None, :] <= t[:, None, None])
    out["new_mask"] = np.where(ok, 0.0, MASKED).reshape(P, -1)
    ht = np.arange(z.H * z.S)
    out["own_head"] = (h[:, None] == ht[None, :] // z.S) & (((p // 8) % 4) == h)[:, None] & (
        t[:, None] == ht[None, :] % z.S)
    out["comp0"] = (q < z.S)[:, None]
    out["comp1"] = (q >= z.S)[:, None]
    out["mean"] = np.full((P, P), 1.0 / P)
    rot = z.HD // 2 // 4
    inv = (np.float32(ROPE_THETA) ** (-np.arange(0, rot, 2, dtype=np.float32) / np.float32(rot))).astype(np.float32)
    pos = np.arange(z.T, dtype=np.float32).reshape(z.NT, P).T
    ang = (pos[:, :, None] * inv).astype(np.float32)
    out["cos_p"], out["sin_p"] = np.cos(ang).reshape(P, -1), np.sin(ang).reshape(P, -1)
    pos = (z.PAGES * z.PAGE + p % z.S).astype(np.float32)
    ang = (pos[:, None] * inv).astype(np.float32)
    out["cos_s"], out["sin_s"] = np.cos(ang), np.sin(ang)
    where, n = {}, 0
    for k, v in out.items():
        where[k] = (n, n + v.shape[1])
        n += v.shape[1]
    return np.ascontiguousarray(np.concatenate([np.asarray(v, np.float32) for v in out.values()], axis=1)), where


def build(nc, z, io, const_at, n_const):
    T, D, B, S, H, HD, F = z.T, z.D, z.B, z.S, z.H, z.HD, z.F
    KC, NT, CH, NCH, NF, BS, AW, CC = z.KC, z.NT, z.CH, z.NCH, z.NF, z.BS, z.AW, z.CC
    QK = HD // 2
    SCORE_SCALE = QK ** -0.5
    WB = 256
    FT = WB // P
    GP, RING = 4, 4
    REVS = z.PAGES // (GP * RING)
    NEW0 = z.PAGES * QUAD
    SC = NEW0 + QUAD
    NADA = z.MODS * D // BANK
    NG = F // WB
    NB_IN, NB_OUT = z.IN // WB, D // WB
    lam_init = 0.8 - 0.6 * math.exp(-0.3 * 0)

    with ExitStack() as ctx:
        base = [16512]

        def place(name, shape, dt, at):
            return nc.alloc_sbuf_tensor_at(name, shape, dt, offset=at)

        def keep(name, shape, dt=F32):
            n = int(np.prod(shape[1:])) * 4
            at = base[0]
            base[0] += -(-n // 32) * 32
            return place(name, shape, dt, at)

        class Area:

            def __init__(self, at):
                self.at = at

            def __call__(self, name, shape, dt=F32):
                n = int(np.prod(shape[1:])) * 4
                t = place(name, shape, dt, self.at)
                self.at += -(-n // 32) * 32
                return t

        psum = ctx.enter_context(nc.psum_tensor("psum", [P, 8, BANK], F32))

        def sem(name):
            return ctx.enter_context(nc.semaphore(name))

        consts = keep("consts", [P, n_const])
        C = lambda name: consts[:, const_at[name][0]:const_at[name][1]]
        ident = C("ident")
        mod_t = keep("mod_t", [P, 4, KC, QUAD])
        gate_p = keep("gate_p", [P, 2, D])
        gate_s = keep("gate_s", [QUAD, 2, D])
        lam_rows = keep("lam_rows", [P, 4, QK])
        small = keep("small", [P, 16])
        NEG_LAM, COEF = small[:, 6:7], small[:, 8:9]
        eps_col = keep("eps_col", [P, 1])
        g_attn = keep("g_attn", [P, 1])
        conv_w_t = keep("conv_w_t", [P, 3, CC // P])
        q_all = keep("q_all", [P, 4 * H, BS])
        q_blocks = keep("q_blocks", [P, H, 4, QUAD])
        k_new_t = keep("k_new_t", [P, AW])
        v_new = keep("v_new", [P, AW])
        o_t_all = keep("o_t_all", [P, B, H * S])
        xs_rows = keep("xs_rows", [QUAD, D])
        y_conv_at = base[0]
        y_conv = keep("y_conv", [P, CC // P, T])
        base[0] = max(base[0], y_conv_at + 16 * D, y_conv_at + 8 * FT * T)
        y_s_at = base[0]
        y_s = keep("y_s", [QUAD, CC])
        stage0 = base[0]

        ar = Area(stage0)
        c_rows = ar("c_rows", [16, D])
        silu_t = ar("silu_t", [P, KC, QUAD])
        ada_w = ar("ada_w", [P, 2, KC, BANK])
        ada_bias = ar("ada_bias", [P, z.MODS * D])
        ada_out = ar("ada_out", [P, z.MODS * D])

        ar = Area(stage0)
        x_hi = ar("x_hi", [P, KC, T], F32R)
        x_lo = ar("x_lo", [P, KC, T], F32R)
        w_raw = ar("w_raw", [P, 2, KC, WB])
        w_hi = ar("w_hi", [P, 2, KC, WB], F32R)
        w_lo = ar("w_lo", [P, 2, KC, WB], F32R)
        x_t_s = ar("x_t_s", [P, KC, QUAD])
        s_quads = ar("s_quads", [P, 2, WB])
        rings = (2 * RING + 2) * GP * AW + B * z.PAGES
        dense_end = max(ar.at, stage0 + 4 * (rings + SC + z.PAGES * QUAD + 512),
                        stage0 + 4 * (rings + NT * AW + 2 * NT * HD + 2 * T + 8))
        ar.at = dense_end
        u_conv = ar("u_conv", [P, CC // P, T + 2])
        ar.at = max(ar.at, dense_end + 8 * NT * WB, dense_end + 8192 + 4 * CC)
        x_rows = place("x_rows", [P, 2, D], F32, ar.at)
        x_mod = place("x_mod", [P, 2, D], F32, ar.at + 8 * D)
        x_end = ar.at + 16 * D
        z_s = ar("z_s", [QUAD, z.IN])
        z_rows = place("z_rows", [P, 2, NT, WB], F32, dense_end)
        rope_p = ar("rope_p", [P, 4, NT * 32])
        ar.at = max(ar.at, x_end)
        rope_s = ar("rope_s", [QUAD, 4, 4 * H * 8])
        q_wide = place("q_wide", [QUAD, 4 * H, 4, QUAD], F32, dense_end)
        u_s = place("u_s", [QUAD, CC], F32, dense_end + 8192)

        ar = Area(stage0)
        k_ring = ar("k_ring", [P, RING, GP, AW])
        v_ring = ar("v_ring", [P, RING, GP, AW])
        k_turned = place("k_turned", [P, 2, GP, AW], F32, ar.at)
        conv_s = ar("conv_s", [QUAD, 7, CC])
        ar.at += 2 * GP * AW * 4 - 7 * CC * 4
        page_row = ar("page_row", [1, B * z.PAGES], mybir.dt.int32)
        dec0 = ar.at
        v_rows = ar("v_rows", [P, NT, AW])
        k_rows = ar("k_rows", [P, NT, HD])
        q_rows = ar("q_rows", [P, NT, HD])
        k_t = ar("k_t", [P, T])
        a_rows = ar("a_rows", [P, T])
        soft = ar("soft", [P, 8])
        ar = Area(max(ar.at, dense_end))
        o_rows = place("o_rows", [P, NT, AW], F32, dense_end)
        ar = Area(max(ar.at, dense_end + 4 * NT * AW))
        q_zero = ar("q_zero", [P, 2, T])
        e_rows = ar("e_rows", [P, 2, T])
        a_t = ar("a_t", [P, T])
        ar = Area(dec0)
        s_rows = ar("s_rows", [P, SC])
        p_t = ar("p_t", [P, z.PAGES, QUAD])
        p_new = ar("p_new", [P, QUAD])
        max_row = ar("max_row", [1, 2, P])
        dec = ar("dec", [P, 16])
        o_scaled = ar("o_scaled", [P, P])
        assert ar.at <= dense_end

        sq_rows = place("sq_rows", [P, NT, AW], F32, dense_end + 4 * NT * AW)
        ar = Area(dense_end)
        x1 = ar("x1", [P, NT, D])
        stats = ar("stats", [P, 32])
        rstd = ar("rstd", [P, 64])
        gate_act_s = place("gate_act_s", [QUAD, WB], F32, y_s_at)
        h_s = place("h_s", [QUAD, WB], F32, y_s_at + 4 * WB)
        h_t_s_at = ar.at
        h_t_s = ar("h_t_s", [P, NF, QUAD])
        on_y_conv = y_conv_at
        h_out = place("h_out", [P, FT, T], F32, on_y_conv)
        ln_rows = place("ln_rows", [P, 2, D], F32, on_y_conv)
        x1_mod = place("x1_mod", [P, 2, D], F32, on_y_conv + 8 * D)

        ar = Area(stage0)
        h_all = ar("h_all", [P, NF, T])
        h_hi = ar("h_hi", [P, 2, T], F32R)
        h_lo = ar("h_lo", [P, 2, T], F32R)
        d_raw = ar("d_raw", [P, 2, 2, WB])
        d_hi = ar("d_hi", [P, 2, WB], F32R)
        d_lo = ar("d_lo", [P, 2, WB], F32R)
        o_t_sq = place("o_t_sq", [P, B * H * S], F32, h_t_s_at)
        row_tmp = place("row_tmp", [P, 2, WB], F32, on_y_conv + 8 * D)

        q_store = nc.dram_tensor("q_store", (T, AW), F32, kind="Internal").ap()
        u_ext = nc.dram_tensor("u_ext", (B, S + 2, CC), F32, kind="Internal").ap()
        h_store = nc.dram_tensor("h_store", (F, T), F32, kind="Internal").ap()
        k_out = io["new_k_prompt"].rearrange("l b t h d -> (l b t) (h d)")
        v_out = io["new_v_prompt"].rearrange("l b t h d -> (l b t) (h d)")
        k_pages = io["cache_k"].rearrange("l n p h d -> (l n) p (h d)")
        v_pages = io["cache_v"].rearrange("l n p h d -> (l n) p (h d)")
        x_dram = io["x_prompt"].rearrange("b t d -> (b t) d")
        y_dram = io["y_prompt"].rearrange("b t d -> (b t) d")
        xs_dram = io["x_sample"].rearrange("b t d -> (b t) d")
        ys_dram = io["y_sample"].rearrange("b t d -> (b t) d")
        by_rows = lambda w: w[0].rearrange("(k p) n -> p k n", p=P)
        w_ada, w_in, w_out = by_rows(io["w_ada"]), by_rows(io["w_in"]), by_rows(io["w_out"])
        w_gate, w_up, w_down = by_rows(io["w_gate"]), by_rows(io["w_up"]), by_rows(io["w_down"])
        row_of = lambda name: io[name].rearrange("l d -> (l d)")

        stage_done = sem("stage_done")
        dve_step = sem("dve_step")
        consts_in, c_in, vectors_in, bias_in = sem("consts_in"), sem("c_in"), sem("vectors_in"), sem("bias_in")
        bias_zeroed, silu_zeroed, c_turned, silu_ready = (
            sem("bias_zeroed"), sem("silu_zeroed"), sem("c_turned"), sem("silu_ready"))
        ada_in = [sem("ada_in0"), sem("ada_in1")]
        ada_done, ada_banks_free = sem("ada_done"), sem("ada_banks_free")
        mod_done, mod_kept, gates_done, gates_kept = (
            sem("mod_done"), sem("mod_kept"), sem("gates_done"), sem("gates_kept"))
        lam_sums, lam_exps = sem("lam_sums"), sem("lam_exps")
        xs_in, x_in = sem("xs_in"), [sem("x_in0"), sem("x_in1")]
        x_turned, x_banks_free, x_hi_done, x_split = sem("x_turned"), sem("x_banks_free"), sem("x_hi_done"), sem("x_split")
        xs_turned, xs_ready = sem("xs_turned"), sem("xs_ready")
        w_in_sem = [sem("w_landed0"), sem("w_landed1")]
        w_hi_done, w_lo_done = sem("w_hi_done"), sem("w_lo_done")
        s_done, s_quads_free, s_folded, s_fold_free = (
            sem("s_done"), sem("s_quads_free"), sem("s_folded"), sem("s_fold_free"))
        fm_done, fm_free, tm_done, tm_free = sem("fm_done"), sem("fm_free"), sem("tm_done"), sem("tm_free")
        conv_ready, conv_stored, roped, z_stored = (
            sem("conv_ready"), sem("conv_stored"), sem("roped"), [sem("z_stored0"), sem("z_stored1")])
        s_conv_ready, s_roped, s_stored, u_ext_in = (
            sem("s_conv_ready"), sem("s_roped"), sem("s_stored"), sem("u_ext_in"))
        q_wide_ready, q_all_done, q_all_kept = sem("q_wide_ready"), sem("q_all_done"), sem("q_all_kept")
        conv_s_in, v_in_rows, qk_in = sem("conv_s_in"), sem("v_in_rows"), sem("qk_in")
        q_zeroed, rows_turned, head_ready = sem("q_zeroed"), sem("rows_turned"), sem("head_ready")
        scores_done, neg_max, score_banks_free = sem("scores_done"), sem("neg_max"), sem("score_banks_free")
        a_ready, a_turned, a_t_ready = sem("a_ready"), sem("a_turned"), sem("a_t_ready")
        pv_done, o_free = sem("pv_done"), sem("o_free")
        k_in = [sem(f"k_in{g}") for g in range(RING)]
        v_in = [sem(f"v_in{g}") for g in range(RING)]
        pages_in = sem("pages_in")
        k_free, v_free, scored, s_bank_free = sem("k_free"), sem("v_free"), sem("scored"), sem("s_bank_free")
        q_ready, new_scored, max_ready, max_turned = (
            sem("q_ready"), sem("new_scored"), sem("max_ready"), sem("max_turned"))
        max_spread, max_back, negmax_ready, exp_done = (
            sem("max_spread"), sem("max_back"), sem("negmax_ready"), sem("exp_done"))
        p_turned, p_by_act, p_by_dve = sem("p_turned"), sem("p_by_act"), sem("p_by_dve")
        o_scaled_ready, o_t_done, o_t_kept = (
            sem("o_scaled_ready"), sem("o_t_done"), sem("o_t_kept"))
        sq_ready, sq_root, o_normed, o_turned, o_hi_done, o_banks_free = (
            sem("sq_ready"), sem("sq_root"), sem("o_normed"), sem("o_turned"), sem("o_hi_done"), sem("o_banks_free"))
        os_sq, os_mean, os_root, ys_turned = sem("os_sq"), sem("os_mean"), sem("os_root"), sem("ys_turned")
        y_hi_done = sem("y_hi_done")
        x1_in, ln_in, var_ready, root_ready, x1_ready = (
            sem("x1_in"), sem("ln_in"), sem("var_ready"), sem("root_ready"), sem("x1_ready"))
        gate_free, up_free, gs_taken, hs_ready, hs_turned, us_taken = (
            sem("gate_free"), sem("up_free"), sem("gs_taken"), sem("hs_ready"), sem("hs_turned"), sem("us_taken"))
        h_stored = sem("h_stored")
        h_in = [sem(f"h_in{j}") for j in range(NF // 2)]
        d_in = [sem("d_in0"), sem("d_in1")]
        d_hi_done, d_split, d_used, down_done, down_free = (
            sem("d_hi_done"), sem("d_split"), sem("d_used"), sem("down_done"), sem("down_free"))
        y_ready, y_stored = sem("y_ready"), sem("y_stored")

        PAIRS = NF // 2
        TB = min(4, NT)
        DB = NT // 2
        MIX0, FF0 = NB_IN, NB_IN + NB_OUT

        cols_of = "cchhbb"
        in_cols = [2 * CC, 2 * CC + WB, 0, WB, CC, CC + WB] + [3 * CC + WB * j for j in range(6)]

        def stage_end(eng, n):
            eng.drain().then_inc(stage_done, 1)
            eng.wait_ge(stage_done, 4 * n)

        def chain(eng, steps):
            count = [0, 0]

            def link(ins):
                count[1] += 1
                ins.then_inc(steps, 1)
                eng.wait_ge(steps, count[0] + count[1])

            @contextmanager
            def loop(turns, links):
                first = count[0] + count[1]
                with eng.Fori(0, turns) as i:
                    count[0], count[1] = first + i * links, 0
                    yield i
                    assert count[1] == links, (count[1], links)
                count[0], count[1] = first + turns * links, 0

            return link, loop

        def regroup(copy, j):
            got = psum[QUAD * j:QUAD * (j + 1), 4:4 + REVS, :].rearrange("p r n -> p (r n)").rearrange(
                "p (g h a q) -> p g h a q", h=H, a=4, q=8)
            to = p_t[:].rearrange("p (g j) (h q) -> p g j h q", j=4, q=8)
            for a in range(4):
                last = copy(to[QUAD * a:QUAD * (a + 1), :, j], got[:, :, :, a, :])
            return last

        def rope(x1_, x2_, cos, sin, tmp, link, done):
            v = nc.vector
            v.tensor_tensor(tmp[0], x1_, cos, ALU.mult)
            v.tensor_tensor(tmp[1], x2_, sin, ALU.mult)
            v.tensor_tensor(tmp[2], x2_, cos, ALU.mult)
            link(v.tensor_tensor(tmp[3], x1_, sin, ALU.mult))
            v.tensor_tensor(x1_, tmp[0], tmp[1], ALU.subtract)
            v.tensor_tensor(x2_, tmp[2], tmp[3], ALU.add).then_inc(done, 1)

        block = ctx.enter_context(nc.Block())

        def load_pages(eng, pages, ring, landed, free):
            with eng.Fori(0, B * REVS) as r:
                for g in range(RING):
                    at = r * (RING * GP) + g * GP
                    for j in range(GP):
                        page = eng.value_load(page_row[0:1, ds(at + j, 1)], min_val=0, max_val=z.POOL - 1)
                        if j == 0:
                            eng.wait_ge(free, r * RING + g + 1)
                        eng.dma_start(ring[:, g, j, :], pages[ds(page, 1)].rearrange("o p d -> p (o d)")
                                      ).then_inc(landed[g], 16)

        @block.sync
        def _(sp):
            sp.dma_start(consts[:], io["consts"]).then_inc(consts_in, 16)
            sp.dma_start(c_rows[0:1, :], io["c_prompt"]).then_inc(c_in, 16)
            sp.dma_start(c_rows[1:1 + B, :], io["c_sample"]).then_inc(c_in, 16)

            def load_ada(s, n):
                sp.dma_start(ada_w[:, s], w_ada[:, :, ds(n * BANK, BANK)]).then_inc(ada_in[s], 16)

            load_ada(0, 0)
            load_ada(1, 1)
            for j, name in enumerate(("lambda_q1", "lambda_k1", "lambda_q2", "lambda_k2")):
                sp.dma_start(lam_rows[:, j, :], row_of(name).partition_broadcast(P)).then_inc(vectors_in, 16)
            with nc.allow_non_contiguous_dma(reason="a few vectors by feature"):
                sp.dma_start(g_attn[:], io["subln_g"].rearrange("l d -> d l")).then_inc(vectors_in, 16)
                for j in range(3):
                    sp.dma_start(conv_w_t[:, j, :], io["conv_w"][0, j].rearrange("(f p) -> p f", p=P)).then_inc(vectors_in, 16)
            sp.wait_ge(bias_zeroed, 1)
            sp.dma_start(ada_bias[0:QUAD, :], row_of("b_ada").partition_broadcast(QUAD)).then_inc(bias_in, 16)
            with sp.Fori(1, NADA // 2) as i:
                for s in range(2):
                    sp.wait_ge(ada_done, 2 * i + s - 1)
                    load_ada(s, 2 * i + s)
            stage_end(sp, 1)

            sp.dma_start(xs_rows[:], xs_dram).then_inc(xs_in, 16)
            for t in range(NT):
                if t >= 2:
                    sp.wait_ge(x_turned, t - 1)
                sp.dma_start(x_rows[:, t % 2], x_dram[t * P:(t + 1) * P, :]).then_inc(x_in[t % 2], 16)

            def load_w(n, w, col):
                if not isinstance(n, int) or n >= 2:
                    sp.wait_ge(s_folded, n - 1)
                s = n % 2 if isinstance(n, int) else None
                sp.dma_start(w_raw[:, s], w[:, :, ds(col, WB)]).then_inc(w_in_sem[s], 16)

            def store_z(m):
                if m < 4:
                    sp.wait_ge(roped, m + 1)
                else:
                    sp.wait_ge(tm_free, TB + NT * (m + 1))
                to = (q_store, k_out, v_out)[m // 2]
                sp.dma_start(to[:, (m % 2) * WB:(m % 2 + 1) * WB].rearrange("(t p) n -> p t n", p=P),
                             z_rows[:, m % 2]).then_inc(z_stored[m % 2], 16)

            for n in range(NB_IN):
                load_w(n, w_in, in_cols[n])
                if n == 6:
                    sp.wait_ge(conv_ready, 1)
                    with nc.allow_non_contiguous_dma(reason="two tokens' rows by feature"):
                        for f in range(CC // P):
                            sp.dma_start(io["new_conv_prompt"][0, 0][:, f * P:(f + 1) * P].rearrange("j p -> p j"),
                                         u_conv[:, f, T:T + 2]).then_inc(conv_stored, 16)
                if n - 2 >= 6:
                    store_z(n - 8)
            store_z(4)
            store_z(5)
            sp.wait_ge(s_conv_ready, 1)
            sp.dma_start(u_ext[:, 2:2 + S, :].rearrange("b t c -> b t c"), u_s[:]).then_inc(u_ext_in, 16)
            sp.dma_start(u_ext[:, 0:2, :], io["state_conv"][0]).then_inc(u_ext_in, 16)
            sp.wait_ge(s_roped, 1)
            sp.dma_start(io["new_k_sample"].rearrange("l b t h d -> (l b t) (h d)"), z_s[:, 3 * CC + AW:3 * CC + 2 * AW]).then_inc(s_stored, 16)
            sp.dma_start(io["new_v_sample"].rearrange("l b t h d -> (l b t) (h d)"), z_s[:, 3 * CC + 2 * AW:]).then_inc(s_stored, 16)
            sp.wait_ge(u_ext_in, 32)
            sp.dma_start(io["new_conv_sample"][0], u_ext[:, S:S + 2, :]).then_inc(s_stored, 16)
            sp.wait_ge(s_stored, 48)
            sp.wait_ge(conv_stored, 16 * (CC // P))
            for s in range(2):
                sp.wait_ge(z_stored[s], 48)
            stage_end(sp, 2)

            for j in range(3):
                sp.dma_start(conv_s[:, j, :], u_ext[:, j:j + S, :]).then_inc(conv_s_in, 16)
            for j in range(3):
                sp.dma_start(conv_s[:, 4 + j, :], io["conv_w"][0, j].partition_broadcast(QUAD)).then_inc(conv_s_in, 16)
            sp.dma_start(page_row[:], io["page_table"].rearrange("b n -> (b n)").rearrange("(o n) -> o n", o=1)).then_inc(pages_in, 16)
            sp.sem_inc(stage_done, 1)
            sp.wait_ge(pages_in, 16)
            load_pages(sp, k_pages, k_ring, k_in, k_free)
            stage_end(sp, 4)
            stage_end(sp, 5)

            sp.dma_start(x1[:], x_dram.rearrange("(t p) d -> p t d", p=P)).then_inc(x1_in, 16)
            for j, name in enumerate(("ln1_g", "ln1_b")):
                sp.dma_start(ln_rows[:, j, :], row_of(name).partition_broadcast(P)).then_inc(ln_in, 16)
            for j in range(NB_OUT):
                load_w(MIX0 + j, w_out, j * WB)
            stage_end(sp, 6)

            def load_ff(i, which):
                sp.wait_ge(s_folded, FF0 - 1 + which + 2 * i)
                sp.dma_start(w_raw[:, which], (w_gate, w_up)[which][:, :, ds(i * WB, WB)]).then_inc(w_in_sem[which], 16)

            sp.sem_inc(h_stored, 16)
            load_ff(0, 0)
            load_ff(0, 1)

            def store_h(i):
                sp.wait_ge(up_free, 2 + FT + i * FT)
                sp.dma_start(h_store[ds(i * WB, WB), :].rearrange("(f p) t -> p f t", p=P), h_out[:]).then_inc(h_stored, 16)

            with sp.Fori(0, NG - 1) as i:
                load_ff(i + 1, 0)
                load_ff(i + 1, 1)
                store_h(i)
            store_h(NG - 1)
            sp.wait_ge(h_stored, 16 * (NG + 1))
            stage_end(sp, 7)

            for j, name in enumerate(("ln2_g", "ln2_b")):
                sp.dma_start(ln_rows[:, j, :], row_of(name).partition_broadcast(P)).then_inc(ln_in, 16)

            def load_d(nb, pp):
                sp.wait_ge(d_used, 2 + nb * NF + 2 * max(pp - 1, 0))
                sp.dma_start(d_raw[:, pp % 2], w_down[:, 2 * pp:2 * pp + 2, ds(nb * WB, WB)]).then_inc(d_in[pp % 2], 16)

            h_view = h_store.rearrange("(k p) t -> p k t", p=P)
            for pp in range(PAIRS):
                sp.dma_start(h_all[:, 2 * pp:2 * pp + 2, :], h_view[:, 2 * pp:2 * pp + 2, :]).then_inc(h_in[pp], 16)
                load_d(0, pp)
            with sp.Fori(1, D // WB) as nb:
                for pp in range(PAIRS):
                    load_d(nb, pp)
            for t in range(NT):
                sp.wait_ge(y_ready, t + 1)
                sp.dma_start(y_dram[t * P:(t + 1) * P, :], x1[:, t, :]).then_inc(y_stored, 16)
            sp.wait_ge(y_ready, NT + 1)
            sp.dma_start(ys_dram, xs_rows[:]).then_inc(y_stored, 16)
            sp.wait_ge(y_stored, 16 * (NT + 1))

        @block.gpsimd
        def _(pool):
            pool.wait_ge(stage_done, 8)
            pool.dma_start(v_rows[:], v_out.rearrange("(t p) n -> p t n", p=P)).then_inc(v_in_rows, 16)
            for h in range(H):
                if h:
                    pool.wait_ge(rows_turned, h)
                for rows, src in ((k_rows, k_out), (q_rows, q_store)):
                    pool.dma_start(rows[:], src[:, h * HD:(h + 1) * HD].rearrange("(t p) n -> p t n", p=P)
                                   ).then_inc(qk_in, 16)
            pool.wait_ge(pages_in, 16)
            load_pages(pool, v_pages, v_ring, v_in, v_free)

        @block.tensor
        def _(pe):
            mm, turn = nc.tensor.matmul, nc.tensor.transpose

            pe.wait_ge(consts_in, 16)
            pe.wait_ge(c_in, 32)
            for k in range(KC):
                last = turn(psum[:, 0, 16 * k:16 * k + 1 + B], c_rows[0:1 + B, k * P:(k + 1) * P], ident[0:1 + B, 0:1 + B])
            last.then_inc(c_turned, 1)
            pe.wait_ge(silu_ready, 1)
            with pe.Fori(0, NADA // 2) as i:
                for s in range(2):
                    pe.wait_ge(ada_in[s], 16 * i + 16)
                    pe.wait_ge(ada_banks_free, 2 * i + s + 1)
                    for k in range(KC):
                        q = QUAD * (k % 4)
                        last = mm(psum[q:q + QUAD, 1 + s, :], silu_t[:, k, :], ada_w[:, s, k, :],
                                  start=k < 4, stop=k >= KC - 4)
                    last.then_inc(ada_done, 1)
            pe.wait_ge(ada_banks_free, 2 + NADA)
            for m, part in enumerate((0, 1, 3, 4)):
                for k in range(KC):
                    at = part * D + k * P
                    last = mm(psum[:, m // 2, (m % 2) * 256 + k * QUAD:(m % 2) * 256 + (k + 1) * QUAD],
                              ada_out[:, at:at + P], C("quad_fold"), start=True, stop=True)
            last.then_inc(mod_done, 1)
            for g, part in enumerate((2, 5)):
                for j in range(D // BANK):
                    mm(psum[:, 2 + 2 * g + j, :], C("pick_prompt"), ada_out[:, part * D + j * BANK:part * D + (j + 1) * BANK],
                       start=True, stop=True).then_inc(gates_done, 1)
            pe.wait_ge(gates_kept, 4)
            for g, part in enumerate((2, 5)):
                for j in range(D // BANK):
                    mm(psum[0:QUAD, 2 + 2 * g + j, :], C("pick_sample"), ada_out[:, part * D + j * BANK:part * D + (j + 1) * BANK],
                       start=True, stop=True).then_inc(gates_done, 1)
            stage_end(pe, 1)

            with pe.Fori(0, NT // 2) as i:
                for s in range(2):
                    pe.wait_ge(x_in[s], 16 * i + 16)
                    pe.wait_ge(x_banks_free, 2 * i + s + 1)
                    for k in range(KC):
                        last = turn(psum[:, 2 * s + k // 4, (k % 4) * P:(k % 4 + 1) * P], x_rows[:, s, k * P:(k + 1) * P], ident)
                    last.then_inc(x_turned, 1)

            def turn_sample():
                for k in range(KC):
                    last = turn(psum[:, 4, k * QUAD:(k + 1) * QUAD], xs_rows[:, k * P:(k + 1) * P], ident[0:QUAD, 0:QUAD])
                last.then_inc(xs_turned, 1)

            pe.wait_ge(xs_in, 16)
            turn_sample()
            pe.wait_ge(x_split, 2 + NT)
            pe.wait_ge(xs_ready, 1)

            def sample_product(n, s):
                pe.wait_ge(w_lo_done, n + 1)
                pe.wait_ge(s_quads_free, n + 1)
                for k in range(KC):
                    q = QUAD * (k % 4)
                    last = mm(psum[q:q + QUAD, 4 + s, 0:WB], x_t_s[:, k, :], w_raw[:, s, k, :],
                              start=k < 4, stop=k >= KC - 4)
                last.then_inc(s_done, 1)

            def sample_fold(n, s, free, value):
                pe.wait_ge(s_quads_free, n + 3)
                pe.wait_ge(free, value)
                mm(psum[0:QUAD, 6 + s, 0:WB], C("quad_fold"), s_quads[:, s, :],
                   start=True, stop=True).then_inc(s_folded, 1)

            PARTS = ((w_hi, x_hi), (w_hi, x_lo), (w_lo, x_hi))

            def by_feature(s, ft):
                for k in range(KC):
                    for j, (w, x) in enumerate(PARTS):
                        for c in range(NCH):
                            last = mm(psum[:, 2 * ft + c, 0:CH], w[:, s, k, ft * P:(ft + 1) * P], x[:, k, c * CH:(c + 1) * CH],
                                      start=k == 0 and j == 0, stop=k == KC - 1 and j == 2)
                return last

            def by_token(s, t):
                for k in range(KC):
                    for j, (w, x) in enumerate(PARTS):
                        last = mm(psum[:, t % TB, 0:WB], x[:, k, t * P:(t + 1) * P], w[:, s, k, :],
                                  start=k == 0 and j == 0, stop=k == KC - 1 and j == 2)
                return last

            with pe.Fori(0, 3) as i:
                for s in range(2):
                    n = 2 * i + s
                    sample_product(n, s)
                    for ft in range(FT):
                        pe.wait_ge(fm_free, FT * n + ft + 1)
                        by_feature(s, ft).then_inc(fm_done, 1)
                    sample_fold(n, s, s_fold_free, n + 1)

            def token_blocks(first, count, tm_before):
                with pe.Fori(0, count // 2) as i:
                    for s in range(2):
                        n = first + 2 * i + s
                        sample_product(n, s)
                        for t in range(NT):
                            pe.wait_ge(tm_free, tm_before + (2 * i + s) * NT + t + 1)
                            by_token(s, t).then_inc(tm_done, 1)
                        sample_fold(n, s, s_fold_free, n + 1)

            pe.wait_ge(fm_free, 2 + 6 * FT)
            token_blocks(6, 6, 0)
            pe.wait_ge(q_wide_ready, 1)
            for hb in range(4 * H):
                last = mm(psum[:, 7, hb * BS:(hb + 1) * BS], q_wide[:, hb].rearrange("p a j -> p (a j)"),
                          ident[0:QUAD, 0:QUAD], start=True, stop=True)
            last.then_inc(q_all_done, 1)
            stage_end(pe, 2)

            pe.sem_inc(v_free, RING)
            pe.wait_ge(v_in_rows, 16)
            with pe.Fori(0, H) as h:
                pe.wait_ge(qk_in, 32 * h + 32)
                pe.wait_ge(a_t_ready, h * NT + 1)
                pe.wait_ge(o_free, h * NT + 2)
                for bank, rows in ((4, k_rows), (6, q_rows)):
                    for t in range(NT):
                        last = turn(psum[:, bank + t // 4, (t % 4) * P:(t % 4 + 1) * P], rows[:, t, :], ident)
                last.then_inc(rows_turned, 1)
                pe.wait_ge(head_ready, h + 1)

                def scores(i):
                    for c in range(2):
                        pe.wait_ge(score_banks_free, h * (2 * NT) + 2 * i + c + 1)
                        for k0 in range(0, (i + 1) * P, BANK):
                            w = min(BANK, (i + 1) * P - k0)
                            last = mm(psum[:, 2 * c + k0 // BANK, 0:w], q_zero[:, c, i * P:(i + 1) * P], k_t[:, k0:k0 + w],
                                      start=True, stop=True)
                        last.then_inc(scores_done, 1)

                scores(0)
                for i in range(NT):
                    if i + 1 < NT:
                        scores(i + 1)
                    pe.wait_ge(a_ready, h * NT + i + 2)
                    pe.wait_ge(a_t_ready, h * NT + i + 1)
                    for j in range(i + 1):
                        last = turn(psum[:, 4 + j // 4, (j % 4) * P:(j % 4 + 1) * P], a_rows[:, j * P:(j + 1) * P], ident)
                    last.then_inc(a_turned, 1)
                    pe.wait_ge(a_t_ready, h * NT + i + 2)
                    pe.wait_ge(o_free, h * NT + i + 1)
                    for j in range(i + 1):
                        last = mm(psum[:, 6 + i % 2, 0:P], a_t[:, j * P:(j + 1) * P],
                                  v_rows[:, j, ds(h * HD, HD)], start=j == 0, stop=j == i)
                    last.then_inc(pv_done, 1)
            stage_end(pe, 3)

            def new_keys(b):
                pe.wait_ge(q_ready, b + 1)
                for h in range(H):
                    for d in range(4):
                        last = mm(psum[QUAD * h:QUAD * (h + 1), 3, 416:416 + QUAD], q_blocks[:, h, d, :],
                                  k_new_t[:, h * HD + d * QUAD:h * HD + (d + 1) * QUAD], start=d == 0, stop=d == 3)
                last.then_inc(new_scored, 1)

            def key_group(b, r, g):
                n = (b * REVS + r) * RING + g
                pe.wait_ge(k_free, RING + 1 + n)
                pe.wait_ge(s_bank_free, n + 1)
                for h in range(H):
                    for d in range(4):
                        last = mm(psum[QUAD * h:QUAD * (h + 1), g % 2, 0:GP * QUAD], q_blocks[:, h, d, :],
                                  k_turned[:, g % 2, :, h * HD + d * QUAD:h * HD + (d + 1) * QUAD],
                                  start=d == 0, stop=d == 3)
                last.then_inc(scored, 1)

            def value_group(b, r, g, stop):
                pe.wait_ge(v_in[g], (b * REVS + r + 1) * (16 * GP))
                for j in range(GP):
                    for h in range(H):
                        last = mm(psum[QUAD * h:QUAD * (h + 1), 2, 0:P], p_t[:, (r * RING + g) * GP + j, :],
                                  v_ring[:, g, j, h * HD:(h + 1) * HD], start=False, stop=stop and j == GP - 1)
                last.then_inc(v_free, 1)

            def softmax(b):
                pe.wait_ge(max_ready, b + 1)
                pe.wait_ge(o_t_kept, b + 1)
                turn(psum[0:1, 3, 0:P], dec[:, 0:1], ident).then_inc(max_turned, 1)
                pe.wait_ge(max_spread, b + 1)
                mm(psum[:, 3, 256:257], max_row[0:1, 1, :], ident[0:1, 0:1], start=True, stop=True).then_inc(max_back, 1)
                for r in range(REVS):
                    pe.wait_ge(exp_done, b * (REVS + 1) + r + 1)
                    for g in range(4):
                        last = turn(psum[:, 4 + r, g * P:(g + 1) * P], s_rows[:, r * BANK + g * P:r * BANK + (g + 1) * P], ident)
                pe.wait_ge(exp_done, (b + 1) * (REVS + 1))
                mm(psum[:, 3, 384:384 + REVS + 1], C("head_fold"), dec[:, 2:3 + REVS], start=True, stop=True)
                turn(psum[0:QUAD, 3, P:2 * P], s_rows[:, NEW0:SC], ident).then_inc(p_turned, 1)
                pe.wait_ge(p_by_act, b + 1)
                pe.wait_ge(p_by_dve, b + 1)
                for h in range(H):
                    mm(psum[QUAD * h:QUAD * (h + 1), 2, 0:P], p_new[:], v_new[:, h * HD:(h + 1) * HD], start=True, stop=False)

            def by_query(b):
                pe.wait_ge(o_scaled_ready, b + 1)
                mm(psum[:, 3, 448:448 + H * S], o_scaled[:], C("own_head"), start=True, stop=True).then_inc(o_t_done, 1)

            new_keys(0)
            with pe.Fori(0, REVS) as r:
                for g in range(RING):
                    key_group(0, r, g)
            with pe.Fori(0, B - 1) as b:
                softmax(b)
                new_keys(b + 1)
                for r in range(REVS):
                    for g in range(RING):
                        key_group(b + 1, r, g)
                        value_group(b, r, g, (r, g) == (REVS - 1, RING - 1))
                by_query(b)
            softmax(B - 1)
            for r in range(REVS):
                for g in range(RING):
                    value_group(B - 1, r, g, (r, g) == (REVS - 1, RING - 1))
            by_query(B - 1)
            stage_end(pe, 4)

            pe.wait_ge(o_normed, 1)
            for t in range(NT):
                if t >= 4:
                    pe.wait_ge(o_banks_free, t - 3)
                for h in range(H):
                    last = turn(psum[:, t % 4, h * P:(h + 1) * P], o_rows[:, t, h * HD:(h + 1) * HD], ident)
                last.then_inc(o_turned, 1)
            pe.wait_ge(os_sq, 1)
            mm(psum[:, 4, 0:B * H * S], C("mean"), o_t_sq[:], start=True, stop=True).then_inc(os_mean, 1)
            for k in range(CC // P):
                last = turn(psum[:, 5, k * QUAD:(k + 1) * QUAD], y_s[:, k * P:(k + 1) * P], ident[0:QUAD, 0:QUAD])
            last.then_inc(ys_turned, 1)
            stage_end(pe, 5)
            token_blocks(MIX0, NB_OUT, 6 * NT)
            for t in range(NT):
                pe.wait_ge(x1_ready, t + 1)
                pe.wait_ge(x_banks_free, NT + t + 1)
                s = t % 2
                for k in range(KC):
                    last = turn(psum[:, 2 * s + k // 4, (k % 4) * P:(k % 4 + 1) * P], x1[:, t, k * P:(k + 1) * P], ident)
                last.then_inc(x_turned, 1)
            pe.wait_ge(x1_ready, NT + 1)
            turn_sample()
            stage_end(pe, 6)

            with pe.Fori(0, NG) as i:
                for s in range(2):
                    n = FF0 + 2 * i + s
                    sample_product(n, s)
                    for ft in range(FT):
                        if s == 0:
                            pe.wait_ge(up_free, i * FT + ft + 1)
                        else:
                            pe.wait_ge(gate_free, i * FT + ft + 1)
                        by_feature(s, ft).then_inc(fm_done, 1)
                    sample_fold(n, s, (gs_taken, us_taken)[s], i + 1)
                pe.wait_ge(consts_in, 16)
                pe.wait_ge(hs_ready, i + 1)
                for ft in range(FT):
                    last = turn(psum[:, 7, WB + ft * QUAD:WB + (ft + 1) * QUAD], h_s[:, ft * P:(ft + 1) * P], ident[0:QUAD, 0:QUAD])
                last.then_inc(hs_turned, 1)
            stage_end(pe, 7)

            with pe.Fori(0, D // WB) as nb:
                for k in range(NF):
                    pe.wait_ge(d_split, nb * NF + (k + 3))
                    s = k % 2
                    for t in range(NT):
                        if k == 0 and t % 2 == 0:
                            pe.wait_ge(down_free, nb * DB + t // 2 + 1)
                        for j, (x, w) in enumerate(((h_hi, d_hi), (h_hi, d_lo), (h_lo, d_hi))):
                            last = mm(psum[:, t // 2, (t % 2) * WB:(t % 2 + 1) * WB], x[:, s, t * P:(t + 1) * P], w[:, s, :],
                                      start=k == 0 and j == 0 and t % 2 == 0, stop=k == NF - 1 and j == 2,
                                      skip_group_check=True)
                    if k == 0:
                        pe.wait_ge(s_quads_free, FF0 + 2 * NG + nb + 2)
                    q = QUAD * (k % 4)
                    last = mm(psum[q:q + QUAD, 4, 0:WB], h_t_s[:, k, :], d_raw[:, (k // 2) % 2, k % 2, :],
                              start=k < 4, stop=k >= NF - 4)
                    last.then_inc(d_used, 1)
                pe.wait_ge(s_quads_free, FF0 + 2 * NG + nb + 3)
                mm(psum[0:QUAD, 5, 0:WB], C("quad_fold"), s_quads[:, 0, :], start=True, stop=True).then_inc(s_folded, 1)

        @block.scalar
        def _(act):
            go, copy = nc.scalar.activation, nc.scalar.copy

            act.wait_ge(c_turned, 1)
            act.wait_ge(silu_zeroed, 1)
            go(silu_t[:, :, 0:1 + B], psum[:, 0, 0:16 * KC].rearrange("p (k c) -> p k c", c=16)[:, :, 0:1 + B],
               ACT.Silu).then_inc(silu_ready, 1)
            act.wait_ge(lam_sums, 1)
            go(small[:, 2:4], small[:, 0:2], ACT.Exp).then_inc(lam_exps, 1)
            for part, gates in enumerate((gate_p, gate_s)):
                rows = (P, QUAD)[part]
                for j in range(4):
                    act.wait_ge(gates_done, 4 * part + j + 1)
                    copy(gates[:, j // 2, (j % 2) * BANK:(j % 2 + 1) * BANK], psum[0:rows, 2 + j, :]).then_inc(gates_kept, 1)
            stage_end(act, 1)

            act.sem_inc(x_banks_free, 2)

            def modulate(t, s, at, x, shift, scale):
                act.wait_ge(x_turned, t + 1)
                act.wait_ge(x_split, t + 1)
                for k in range(KC):
                    last = go(x[:, k * P:(k + 1) * P], psum[:, 2 * s + k // 4, (k % 4) * P:(k % 4 + 1) * P],
                              ACT.Identity, bias=mod_t[:, shift, k, 0:1], scale=mod_t[:, scale, k, 0:1])
                last.then_inc(x_banks_free, 1)
                act.wait_ge(x_banks_free, t + 3)
                copy(x_hi[:, :, at], x.rearrange("p (k n) -> p k n", n=P)).then_inc(x_hi_done, 1)

            with act.Fori(0, NT // 2) as i:
                for s in range(2):
                    modulate(2 * i + s, s, ds((2 * i + s) * P, P), x_mod[:, s, :], 0, 1)

            def w_high(n, s, fills):
                act.wait_ge(w_in_sem[s], 16 * fills)
                if not isinstance(n, int) or n >= 2:
                    act.wait_ge(s_folded, n - 1)
                copy(w_hi[:, s], w_raw[:, s]).then_inc(w_hi_done, 1)

            w_high(0, 0, 1)
            for n in range(NB_IN):
                if n + 1 < NB_IN:
                    w_high(n + 1, (n + 1) % 2, (n + 1) // 2 + 1)
                if n >= 6:
                    m = n - 6
                    if m == 0:
                        act.wait_ge(fm_free, 2 + 6 * FT)
                        act.wait_ge(conv_stored, 16 * (CC // P))
                    if m >= 2:
                        act.wait_ge(z_stored[m % 2], 16 * (m // 2))
                    for t in range(NT):
                        act.wait_ge(tm_done, m * NT + t + 1)
                        copy(z_rows[:, m % 2, t, :], psum[:, t % TB, 0:WB]).then_inc(tm_free, 1)
            act.wait_ge(q_all_done, 1)
            copy(q_all[:].rearrange("p h b -> p (h b)"), psum[:, 7, :]).then_inc(q_all_kept, 1)
            stage_end(act, 2)

            act.sem_inc(score_banks_free, 2)
            act.sem_inc(a_t_ready, 1)
            act.wait_ge(q_zeroed, 1)
            with act.Fori(0, H) as h:
                act.wait_ge(rows_turned, h + 1)
                copy(k_t[:], psum[:, 4:4 + -(-T // BANK), 0:CH].rearrange("p c n -> p (c n)"))
                for c in range(2):
                    r = slice(c * QK, (c + 1) * QK)
                    last = nc.scalar.mul(q_zero[r, c, :], psum[r, 6:6 + -(-T // BANK), 0:CH].rearrange("p c n -> p (c n)"), SCORE_SCALE)
                last.then_inc(head_ready, 1)

                def exps(i):
                    w = (i + 1) * P
                    for c in range(2):
                        act.wait_ge(neg_max, h * (2 * NT) + 2 * i + c + 1)
                        act.wait_ge(a_ready, h * NT + i + 1)
                        go(e_rows[:, c, 0:w], psum[:, 2 * c:2 * c + 2, :].rearrange("p c n -> p (c n)")[:, 0:w], ACT.Exp,
                           bias=soft[:, 2 + c:3 + c], accum_out=soft[:, 4 + c:5 + c]).then_inc(score_banks_free, 1)

                exps(0)
                for i in range(NT):
                    if i + 1 < NT:
                        exps(i + 1)
                    w = (i + 1) * P
                    act.wait_ge(a_turned, h * NT + i + 2)
                    act.wait_ge(pv_done, h * NT + i + 1)
                    copy(a_t[:, 0:w], psum[:, 4:6, :].rearrange("p c n -> p (c n)")[:, 0:w]).then_inc(a_t_ready, 1)
            stage_end(act, 3)

            act.sem_inc(s_bank_free, 2)
            act.sem_inc(o_t_kept, 1)

            def take_scores(b):
                with act.Fori(0, REVS) as r:
                    for g in range(RING):
                        n = (b * REVS + r) * RING + g
                        act.wait_ge(scored, 3 + n)
                        copy(s_rows[:, ds((r * RING + g) * (GP * QUAD), GP * QUAD)], psum[:, g % 2, 0:GP * QUAD]).then_inc(s_bank_free, 1)

            def softmax(b):
                act.wait_ge(negmax_ready, b + 1)
                for r in range(REVS + 1):
                    part = s_rows[:, r * BANK:(r + 1) * BANK] if r < REVS else s_rows[:, NEW0:SC]
                    go(part, part, ACT.Exp, bias=dec[:, 1:2], accum_out=dec[:, 2 + r:3 + r]).then_inc(exp_done, 1)
                act.wait_ge(p_turned, b + 1)
                for j in range(0, 2):
                    last = regroup(copy, j)
                last.then_inc(p_by_act, 1)

            def keep_output(b):
                act.wait_ge(o_t_done, b + 1)
                copy(o_t_all[:, ds(b, 1), :], psum[:, 3, 448:448 + H * S].rearrange("p (o n) -> p o n", o=1)).then_inc(o_t_kept, 1)

            take_scores(0)
            with act.Fori(0, B - 1) as b:
                softmax(b)
                take_scores(b + 1)
                keep_output(b)
            softmax(B - 1)
            keep_output(B - 1)
            stage_end(act, 4)

            act.wait_ge(sq_ready, 1)
            go(rstd[:, 0:NT * H], stats[:, 0:NT * H], ACT.Sqrt, bias=eps_col[:], scale=1.0 / HD).then_inc(sq_root, 1)
            copy(x_hi[:, 0:CC // P, :], y_conv[:]).then_inc(y_hi_done, 1)
            for t in range(NT):
                act.wait_ge(o_turned, t + 1)
                go(x_hi[:, CC // P:, t * P:(t + 1) * P], psum[:, t % 4, :].rearrange("p (h n) -> p h n", n=P), ACT.Copy,
                   scale=g_attn[:, 0:1]).then_inc(o_hi_done, 1)
            act.wait_ge(os_mean, 1)
            go(o_t_sq[:], psum[:, 4, 0:B * H * S], ACT.Sqrt, bias=eps_col[:]).then_inc(os_root, 1)
            stage_end(act, 5)
            FILLS = NB_IN // 2
            w_high(MIX0, 0, FILLS + 1)
            for j in range(NB_OUT - 1):
                w_high(MIX0 + j + 1, (j + 1) % 2, FILLS + (j + 1) // 2 + 1)

            def roots(count):
                act.wait_ge(var_ready, count)
                var = rstd[:, 0:2 * NT].rearrange("p (t j) -> p t j", j=2)[:, :, 1]
                go(var, var, ACT.Sqrt, bias=eps_col[:])
                var = rstd[0:QUAD, 2 * NT + 1:2 * NT + 2]
                go(var, var, ACT.Sqrt, bias=eps_col[0:QUAD]).then_inc(root_ready, 1)

            roots(1)
            for t in range(NT):
                modulate(NT + t, t % 2, slice(t * P, (t + 1) * P), x1_mod[:, t % 2, :], 2, 3)
            stage_end(act, 6)

            FILLS = (NB_IN + NB_OUT) // 2
            w_high(FF0, 0, FILLS + 1)

            def gate_up(i, more):
                w_high(FF0 + 1 + 2 * i, 1, FILLS + 1 + i)
                act.wait_ge(h_stored, 16 * i + 16)
                for ft in range(FT):
                    act.wait_ge(fm_done, 6 * FT + 2 * FT * i + ft + 1)
                    go(h_out[:, ft, :], psum[:, 2 * ft:2 * ft + NCH, 0:CH].rearrange("p c n -> p (c n)"), ACT.Silu).then_inc(gate_free, 1)
                act.wait_ge(s_folded, FF0 + 1 + 2 * i)
                act.wait_ge(us_taken, i + 1)
                go(gate_act_s[:], psum[0:QUAD, 6, 0:WB], ACT.Silu).then_inc(gs_taken, 1)
                if more:
                    w_high(FF0 + 2 + 2 * i, 0, FILLS + 2 + i)

            with act.Fori(0, NG - 1) as i:
                gate_up(i, True)
            gate_up(NG - 1, False)
            stage_end(act, 7)

            with act.Fori(0, D // WB) as nb:
                for k in range(NF):
                    pp, s = k // 2, k % 2
                    if s == 0:
                        fills = (PAIRS + 1 - pp % 2) // 2
                        act.wait_ge(d_in[pp % 2], 16 * (nb * fills + (pp // 2 + 1)))
                    if pp < PAIRS:
                        act.wait_ge(h_in[pp], 16)
                    act.wait_ge(d_used, nb * NF + (k + 1))
                    copy(h_hi[:, s, :], h_all[:, k, :])
                    copy(d_hi[:, s, :], d_raw[:, pp % 2, s, :]).then_inc(d_hi_done, 1)
            roots(2)

        @block.vector
        def _(dve):
            v = nc.vector
            link, linked_loop = chain(dve, dve_step)

            v.memset(ada_bias[:], 0.0).then_inc(bias_zeroed, 1)
            v.memset(silu_t[:], 0.0).then_inc(silu_zeroed, 1)
            dve.sem_inc(ada_banks_free, 2)
            v.memset(k_new_t[:], 0.0)
            v.memset(v_new[:], 0.0)
            v.memset(q_blocks[:], 0.0)
            link(v.memset(eps_col[:], LN_EPS))
            dve.wait_ge(vectors_in, 16 * 8)
            for j in range(2):
                link(v.tensor_tensor(lam_rows[:, 2 * j, :], lam_rows[:, 2 * j, :], lam_rows[:, 2 * j + 1, :], ALU.mult))
            link(v.tensor_reduce(small[:, 0:1], lam_rows[:, 0, :], AX_X, ALU.add))
            v.tensor_reduce(small[:, 1:2], lam_rows[:, 2, :], AX_X, ALU.add).then_inc(lam_sums, 1)
            dve.wait_ge(lam_exps, 1)
            link(v.tensor_tensor(small[:, 5:6], small[:, 3:4], small[:, 2:3], ALU.subtract))
            link(v.tensor_scalar(NEG_LAM, small[:, 5:6], -lam_init, None, ALU.add))
            dve.wait_ge(consts_in, 16)
            link(v.tensor_scalar(small[:, 7:8], C("comp1"), NEG_LAM, None, ALU.mult))
            link(v.tensor_tensor(COEF, small[:, 7:8], C("comp0"), ALU.add))
            link(v.tensor_scalar(g_attn[:], g_attn[:], 1.0 - lam_init, None, ALU.mult))
            dve.wait_ge(bias_in, 16)
            with dve.Fori(0, NADA // 2) as i:
                for s in range(2):
                    dve.wait_ge(ada_done, 2 * i + s + 1)
                    at = ds((2 * i + s) * BANK, BANK)
                    v.tensor_tensor(ada_out[:, at], psum[:, 1 + s, :], ada_bias[:, at], ALU.add).then_inc(ada_banks_free, 1)
            dve.wait_ge(mod_done, 1)
            for m in range(4):
                last = v.tensor_scalar(mod_t[:, m].rearrange("p k c -> p (k c)"), psum[:, m // 2, (m % 2) * 256:(m % 2) * 256 + KC * QUAD],
                                       float(m % 2), None, ALU.add)
            link(last)
            stage_end(dve, 1)

            dve.sem_inc(x_split, 2)
            dve.sem_inc(s_quads_free, 2)
            dve.sem_inc(s_fold_free, 2)
            dve.sem_inc(fm_free, 2)
            dve.sem_inc(tm_free, TB)
            link(v.memset(u_conv[:, :, 0:2], 0.0))

            def split(t, at, x):
                dve.wait_ge(x_hi_done, t + 1)
                v.tensor_tensor(x_lo[:, :, at], x.rearrange("p (k n) -> p k n", n=P), x_hi[:, :, at], ALU.subtract
                                ).then_inc(x_split, 1)

            def modulate_sample(shift, scale):
                per_token = lambda m: mod_t[:, m, :, 1:1 + B].unsqueeze(3).to_broadcast([P, KC, B, S])
                out = x_t_s[:].rearrange("p k (b t) -> p k b t", t=S)
                link(v.tensor_tensor(out, psum[:, 4, 0:KC * QUAD].rearrange("p (k b t) -> p k b t", b=B, t=S), per_token(scale), ALU.mult))
                v.tensor_tensor(out, out, per_token(shift), ALU.add).then_inc(xs_ready, 1)

            with dve.Fori(0, NT // 2) as i:
                for s in range(2):
                    split(2 * i + s, ds((2 * i + s) * P, P), x_mod[:, s, :])
            dve.wait_ge(xs_turned, 1)
            modulate_sample(0, 1)

            def w_low(n, s):
                dve.wait_ge(w_hi_done, n + 1)
                v.tensor_tensor(w_lo[:, s], w_raw[:, s], w_hi[:, s], ALU.subtract).then_inc(w_lo_done, 1)

            def take_quads(n, s):
                dve.wait_ge(s_done, n + 1)
                v.tensor_copy(s_quads[:, s, :], psum[:, 4 + s, 0:WB]).then_inc(s_quads_free, 1)

            w_low(0, 0)
            for n in range(NB_IN):
                s = n % 2
                if n + 1 < NB_IN:
                    w_low(n + 1, 1 - s)
                take_quads(n, s)
                for ft in range(FT):
                    if n >= 6:
                        break
                    f = (n % 2) * FT + ft
                    dve.wait_ge(fm_done, FT * n + ft + 1)
                    got = psum[:, 2 * ft:2 * ft + NCH, 0:CH].rearrange("p c n -> p (c n)")
                    u = u_conv[:, f, 2:2 + T]
                    y = y_conv[:, f, :]
                    if cols_of[n] == "c":
                        v.tensor_copy(u, got).then_inc(fm_free, 1)
                    elif cols_of[n] == "h":
                        v.tensor_tensor(u, got, u, ALU.mult).then_inc(fm_free, 1)
                        dve.wait_ge(fm_free, 3 + FT * n + ft)
                        link(v.tensor_scalar(y, u_conv[:, f, 0:T], conv_w_t[:, 0, f:f + 1], None, ALU.mult))
                        link(v.scalar_tensor_tensor(y, u_conv[:, f, 1:1 + T], conv_w_t[:, 1, f:f + 1], y, ALU.mult, ALU.add))
                        if f == CC // P - 1:
                            v.scalar_tensor_tensor(y, u, conv_w_t[:, 2, f:f + 1], y, ALU.mult, ALU.add).then_inc(conv_ready, 1)
                            dve.wait_ge(conv_ready, 1)
                        else:
                            link(v.scalar_tensor_tensor(y, u, conv_w_t[:, 2, f:f + 1], y, ALU.mult, ALU.add))
                    else:
                        v.tensor_tensor(y, got, y, ALU.mult).then_inc(fm_free, 1)
                if 6 <= n < 10:
                    m = n - 6
                    dve.wait_ge(tm_free, TB + (m + 1) * NT)
                    pair = z_rows[:, m % 2].rearrange("p t (g d) -> p t g d", d=QK)
                    cos = C("cos_p").rearrange("p (t d) -> p t d", d=8).unsqueeze(2).to_broadcast([P, NT, 4, 8])
                    sin = C("sin_p").rearrange("p (t d) -> p t d", d=8).unsqueeze(2).to_broadcast([P, NT, 4, 8])
                    rope(pair[:, :, :, 0:8], pair[:, :, :, 8:16], cos, sin,
                         [rope_p[:, j, :].rearrange("p (t g d) -> p t g d", g=4, d=8) for j in range(4)], link, roped)
                    dve.wait_ge(roped, m + 1)
                dve.wait_ge(s_folded, n + 1)
                v.tensor_copy(z_s[:, in_cols[n]:in_cols[n] + WB], psum[0:QUAD, 6 + s, 0:WB]).then_inc(s_fold_free, 1)
            dve.wait_ge(s_fold_free, 2 + NB_IN)
            for s in range(2):
                dve.wait_ge(z_stored[s], 48)
            v.tensor_copy(y_s[:], z_s[:, CC:2 * CC])
            v.tensor_tensor(u_s[:], z_s[:, 2 * CC:3 * CC], z_s[:, 0:CC], ALU.mult).then_inc(s_conv_ready, 1)
            qk = z_s[:, 3 * CC:3 * CC + 2 * AW].rearrange("p (g d) -> p g d", d=QK)
            cos = C("cos_s")[0:QUAD].unsqueeze(1).to_broadcast([QUAD, 4 * H, 8])
            sin = C("sin_s")[0:QUAD].unsqueeze(1).to_broadcast([QUAD, 4 * H, 8])
            rope(qk[:, :, 0:8], qk[:, :, 8:16], cos, sin,
                 [rope_s[:, j, :].rearrange("p (g d) -> p g d", d=8) for j in range(4)], link, s_roped)
            dve.wait_ge(s_roped, 1)
            v.transpose(k_new_t[0:QUAD, :], z_s[:, 3 * CC + AW:3 * CC + 2 * AW])
            link(v.tensor_copy(v_new[0:QUAD, :], z_s[:, 3 * CC + 2 * AW:]))
            v.tensor_scalar(q_wide[:], z_s[:, 3 * CC:3 * CC + AW].rearrange("p (g j) -> p g j", j=QUAD).unsqueeze(2)
                            .to_broadcast([QUAD, 4 * H, 4, QUAD]), SCORE_SCALE, None, ALU.mult).then_inc(q_wide_ready, 1)
            stage_end(dve, 2)

            dve.sem_inc(k_free, RING)
            dve.sem_inc(a_ready, 1)
            dve.sem_inc(a_turned, 1)
            dve.sem_inc(pv_done, 1)
            dve.sem_inc(o_free, 2)
            v.memset(q_zero[:], 0.0).then_inc(q_zeroed, 1)
            dve.wait_ge(conv_s_in, 96)
            for j in range(3):
                link(v.tensor_tensor(conv_s[:, j, :], conv_s[:, j, :], conv_s[:, 4 + j, :], ALU.mult))
            link(v.tensor_tensor(conv_s[:, 0, :], conv_s[:, 0, :], conv_s[:, 1, :], ALU.add))
            link(v.tensor_tensor(conv_s[:, 0, :], conv_s[:, 0, :], conv_s[:, 2, :], ALU.add))
            link(v.tensor_tensor(y_s[:], y_s[:], conv_s[:, 0, :], ALU.mult))
            with linked_loop(H, 2 * NT * 2 + 3 * NT) as h:
                def maxima(i):
                    w = (i + 1) * P
                    for c in range(2):
                        dve.wait_ge(scores_done, h * (2 * NT) + 2 * i + c + 1)
                        diag = psum[:, 2 * c + i // 4, (i % 4) * P:(i % 4 + 1) * P]
                        link(v.tensor_tensor(diag, diag, C("causal"), ALU.add))
                        link(v.tensor_reduce(soft[:, c:c + 1], psum[:, 2 * c:2 * c + 2, :].rearrange("p c n -> p (c n)")[:, 0:w], AX_X, ALU.max))
                        v.tensor_scalar(soft[:, 2 + c:3 + c], soft[:, c:c + 1], -1.0, None, ALU.mult).then_inc(neg_max, 1)

                def take_o(i):
                    dve.wait_ge(pv_done, h * NT + i + 2)
                    v.tensor_copy(o_rows[:, i, ds(h * HD, HD)], psum[:, 6 + i % 2, 0:P]).then_inc(o_free, 1)

                maxima(0)
                for i in range(NT):
                    if i + 1 < NT:
                        maxima(i + 1)
                    w = (i + 1) * P
                    dve.wait_ge(score_banks_free, 2 + h * (2 * NT) + 2 * i + 2)
                    link(v.reciprocal(soft[:, 6:8], soft[:, 4:6]))
                    link(v.tensor_scalar(soft[:, 7:8], soft[:, 7:8], NEG_LAM, None, ALU.mult))
                    dve.wait_ge(a_turned, h * NT + i + 1)
                    link(v.tensor_scalar(a_rows[:, 0:w], e_rows[:, 0, 0:w], soft[:, 6:7], None, ALU.mult))
                    v.scalar_tensor_tensor(a_rows[:, 0:w], e_rows[:, 1, 0:w], soft[:, 7:8], a_rows[:, 0:w], ALU.mult, ALU.add
                                           ).then_inc(a_ready, 1)
                    if i:
                        take_o(i - 1)
                take_o(NT - 1)
            stage_end(dve, 3)

            dve.sem_inc(scored, 2)
            link(v.memset(p_new[:], 0.0))
            q_rows_of = q_all[:].rearrange("p (h d) n -> p h d n", d=4)

            def queries(b):
                dve.wait_ge(scored, 2 + b * (REVS * RING))
                for a in range(4):
                    for c in range(2):
                        r = slice(QUAD * a, QUAD * (a + 1))
                        last = v.tensor_copy(q_blocks[r, :, 2 * c:2 * c + 2, a * 8 + c * S:a * 8 + (c + 1) * S],
                                             q_rows_of[r, :, 2 * c:2 * c + 2, ds(b * S, S)])
                last.then_inc(q_ready, 1)
                dve.wait_ge(new_scored, b + 1)
                v.tensor_tensor(s_rows[:, NEW0:SC].rearrange("p (o n) -> p o n", o=1), psum[:, 3, 416:416 + QUAD].rearrange("p (o n) -> p o n", o=1),
                                C("new_mask").rearrange("p (b n) -> p b n", n=QUAD)[:, ds(b, 1), :], ALU.add)

            def turn_keys(b):
                with dve.Fori(0, REVS) as r:
                    for g in range(RING):
                        n = (b * REVS + r) * RING + g
                        dve.wait_ge(k_in[g], (b * REVS + r + 1) * (16 * GP))
                        dve.wait_ge(scored, n + 1)
                        v.transpose(k_turned[:, g % 2].rearrange("p j n -> p (j n)"), k_ring[:, g].rearrange("p j n -> p (j n)")
                                    ).then_inc(k_free, 1)
                dve.wait_ge(k_free, RING + (b + 1) * (REVS * RING))

            def softmax(b):
                dve.wait_ge(s_bank_free, 2 + (b + 1) * (REVS * RING))
                v.tensor_reduce(dec[:, 0:1], s_rows[:], AX_X, ALU.max).then_inc(max_ready, 1)
                dve.wait_ge(max_turned, b + 1)
                link(v.tensor_reduce(max_row[0:1, 0, 0:QUAD].rearrange("p (h q) -> p h q", q=8),
                                     psum[0:1, 3, 0:P].rearrange("p (h a q) -> p h q a", a=4, q=8), AX_X, ALU.max))
                v.tensor_scalar(max_row[0:1, 1, :].rearrange("p (h a q) -> p h a q", a=4, q=8),
                                max_row[0:1, 0, 0:QUAD].rearrange("p (h q) -> p h q", q=8).unsqueeze(2).to_broadcast([1, H, 4, 8]),
                                -1.0, None, ALU.mult).then_inc(max_spread, 1)
                dve.wait_ge(max_back, b + 1)
                v.tensor_copy(dec[:, 1:2], psum[:, 3, 256:257]).then_inc(negmax_ready, 1)
                dve.wait_ge(p_turned, b + 1)
                for j in range(2, 4):
                    regroup(v.tensor_copy, j)
                v.tensor_copy(p_new[0:QUAD, :].rearrange("p (h q) -> p h q", q=8),
                              psum[0:QUAD, 3, P:2 * P].rearrange("p (h a q) -> p h a q", a=4, q=8)[:, :, 0, :]).then_inc(p_by_dve, 1)
                link(v.tensor_reduce(dec[:, 12:13], psum[:, 3, 384:384 + REVS + 1], AX_X, ALU.add))
                link(v.reciprocal(dec[:, 13:14], dec[:, 12:13]))
                link(v.tensor_tensor(dec[:, 14:15], dec[:, 13:14], COEF, ALU.mult))

            def scale_output(b):
                dve.wait_ge(v_free, RING + (b + 1) * (REVS * RING))
                v.tensor_scalar(o_scaled[:], psum[:, 2, 0:P], dec[:, 14:15], None, ALU.mult).then_inc(o_scaled_ready, 1)

            queries(0)
            turn_keys(0)
            with linked_loop(B - 1, 4) as b:
                softmax(b)
                queries(b + 1)
                turn_keys(b + 1)
                scale_output(b)
            softmax(B - 1)
            scale_output(B - 1)
            stage_end(dve, 4)

            rows = o_rows[:].rearrange("p t (h d) -> p (t h) d", d=HD)
            link(v.tensor_tensor(sq_rows[:], o_rows[:], o_rows[:], ALU.mult))
            v.tensor_reduce(stats[:, 0:NT * H], sq_rows[:].rearrange("p t (h d) -> p (t h) d", d=HD), AX_X, ALU.add).then_inc(sq_ready, 1)
            o_t = o_t_all[:].rearrange("p b n -> p (b n)")
            v.tensor_tensor(o_t_sq[:], o_t, o_t, ALU.mult).then_inc(os_sq, 1)
            dve.wait_ge(sq_root, 1)
            link(v.reciprocal(rstd[:, 0:NT * H], rstd[:, 0:NT * H]))
            v.tensor_tensor(rows, rows, rstd[:, 0:NT * H].unsqueeze(2).to_broadcast([P, NT * H, HD]), ALU.mult).then_inc(o_normed, 1)
            dve.wait_ge(y_hi_done, 1)
            v.tensor_tensor(x_lo[:, 0:CC // P, :], y_conv[:], x_hi[:, 0:CC // P, :], ALU.subtract)
            for t in range(NT):
                dve.wait_ge(o_hi_done, t + 1)
                at = slice(t * P, (t + 1) * P)
                for h in range(H):
                    k = CC // P + h
                    last = v.scalar_tensor_tensor(x_lo[:, k, at], psum[:, t % 4, h * P:(h + 1) * P], g_attn[:, 0:1], x_hi[:, k, at],
                                                  ALU.mult, ALU.subtract)
                last.then_inc(o_banks_free, 1)
            dve.wait_ge(os_root, 1)
            link(v.reciprocal(o_t_sq[:], o_t_sq[:]))
            link(v.tensor_tensor(o_t, o_t, o_t_sq[:], ALU.mult))
            v.tensor_scalar(x_t_s[:, CC // P:, :].rearrange("p h (b t) -> p b h t", t=S), o_t_all[:].rearrange("p b (h t) -> p b h t", t=S),
                            g_attn[:, 0:1], None, ALU.mult)
            dve.wait_ge(ys_turned, 1)
            v.tensor_copy(x_t_s[:, 0:CC // P, :].rearrange("p k n -> p (k n)"), psum[:, 5, 0:(CC // P) * QUAD])
            stage_end(dve, 5)

            def residual(x, got, gate, tmp, free):
                ins = v.tensor_tensor(tmp, got, gate, ALU.mult)
                ins.then_inc(free[0], 1)
                dve.wait_ge(free[0], free[1])
                link(v.scalar_tensor_tensor(x, x, z.ALPHA, tmp, ALU.mult, ALU.add))

            dve.wait_ge(x1_in, 16)
            w_low(MIX0, 0)
            for j in range(NB_OUT):
                n, s = MIX0 + j, j % 2
                if j + 1 < NB_OUT:
                    w_low(n + 1, 1 - s)
                take_quads(n, s)
                cols = slice(j * WB, (j + 1) * WB)
                for t in range(NT):
                    dve.wait_ge(tm_done, (6 + j) * NT + t + 1)
                    residual(x1[:, t, cols], psum[:, t % TB, 0:WB], gate_p[:, 0, cols], row_tmp[:, 0, :],
                             (tm_free, TB + (6 + j) * NT + t + 1))
                dve.wait_ge(s_folded, n + 1)
                residual(xs_rows[:, cols], psum[0:QUAD, 6 + s, 0:WB], gate_s[:, 0, cols], row_tmp[0:QUAD, 1, :],
                         (s_fold_free, 3 + n))

            def moments(x, t):
                rows = x.shape[0]
                for j in range(2):
                    last = v.bn_stats(stats[0:rows, 6 * j:6 * j + 6], x[:, j * (D // 2):(j + 1) * (D // 2)])
                link(last)
                link(v.bn_aggr(rstd[0:rows, 2 * t:2 * t + 2], stats[0:rows, 0:12]))

            def normalise(x, t):
                rows = x.shape[0]
                link(v.tensor_scalar(x, x, rstd[0:rows, 2 * t:2 * t + 1], rstd[0:rows, 32 + t:33 + t], ALU.subtract, ALU.mult))
                link(v.tensor_tensor(x, x, ln_rows[0:rows, 0, :], ALU.mult))
                return v.tensor_tensor(x, x, ln_rows[0:rows, 1, :], ALU.add)

            def layer_norms(count, out):
                for t in range(NT):
                    moments(x1[:, t, :], t)
                moments(xs_rows[:], NT)
                dve.drain().then_inc(var_ready, 1)
                dve.wait_ge(root_ready, count)
                var = rstd[:, 0:2 * NT].rearrange("p (t j) -> p t j", j=2)[:, :, 1]
                link(v.reciprocal(rstd[:, 32:32 + NT], var))
                link(v.reciprocal(rstd[0:QUAD, 32 + NT:33 + NT], rstd[0:QUAD, 2 * NT + 1:2 * NT + 2]))
                dve.wait_ge(ln_in, 32 * count)
                for t in range(NT):
                    normalise(x1[:, t, :], t).then_inc(out, 1)
                normalise(xs_rows[:], NT).then_inc(out, 1)

            layer_norms(1, x1_ready)
            for t in range(NT):
                split(NT + t, slice(t * P, (t + 1) * P), x1_mod[:, t % 2, :])
            dve.wait_ge(xs_turned, 2)
            modulate_sample(2, 3)
            stage_end(dve, 6)

            dve.sem_inc(up_free, 2)
            dve.sem_inc(us_taken, 1)
            dve.sem_inc(gs_taken, 1)
            w_low(FF0, 0)

            def gate_up(i, more):
                w_low(FF0 + 1 + 2 * i, 1)
                take_quads(FF0 + 2 * i, 0)
                if more:
                    w_low(FF0 + 2 + 2 * i, 0)
                take_quads(FF0 + 1 + 2 * i, 1)
                for ft in range(FT):
                    dve.wait_ge(fm_done, 6 * FT + 2 * FT * i + (FT + ft + 1))
                    dve.wait_ge(gate_free, FT * i + ft + 1)
                    h = h_out[:, ft, :]
                    v.tensor_tensor(h, psum[:, 2 * ft:2 * ft + NCH, 0:CH].rearrange("p c n -> p (c n)"), h, ALU.mult).then_inc(up_free, 1)
                dve.wait_ge(s_folded, FF0 + 2 + 2 * i)
                dve.wait_ge(gs_taken, i + 2)
                v.tensor_tensor(h_s[:], psum[0:QUAD, 7, 0:WB], gate_act_s[:], ALU.mult).then_inc(us_taken, 1)
                dve.wait_ge(us_taken, i + 2)
                dve.sem_inc(hs_ready, 1)
                dve.wait_ge(hs_turned, i + 1)
                v.tensor_copy(h_t_s[:, ds(FT * i, FT), :], psum[:, 7, WB:WB + FT * QUAD].rearrange("p (f n) -> p f n", n=QUAD))

            with dve.Fori(0, NG - 1) as i:
                gate_up(i, True)
            gate_up(NG - 1, False)
            stage_end(dve, 7)

            dve.sem_inc(d_used, 2)
            dve.sem_inc(d_split, 2)
            dve.sem_inc(down_free, DB)
            N0 = FF0 + 2 * NG
            with linked_loop(D // WB, DB + 1) as nb:
                for k in range(NF):
                    s = k % 2
                    dve.wait_ge(d_hi_done, nb * NF + (k + 1))
                    v.tensor_tensor(h_lo[:, s, :], h_all[:, k, :], h_hi[:, s, :], ALU.subtract)
                    v.tensor_tensor(d_lo[:, s, :], d_raw[:, (k // 2) % 2, s, :], d_hi[:, s, :], ALU.subtract).then_inc(d_split, 1)
                dve.wait_ge(d_used, 2 + (nb + 1) * NF)
                cols = ds(nb * WB, WB)
                for j in range(DB):
                    got = psum[:, j, 0:2 * WB].rearrange("p (t n) -> p t n", n=WB)
                    gate = gate_p[:, 1, cols].unsqueeze(1).to_broadcast([P, 2, WB])
                    residual(x1[:, 2 * j:2 * j + 2, cols], got, gate, row_tmp[:], (down_free, nb * DB + (DB + j + 1)))
                v.tensor_copy(s_quads[:, 0, :], psum[:, 4, 0:WB]).then_inc(s_quads_free, 1)
                dve.wait_ge(s_folded, N0 + nb + 1)
                residual(xs_rows[:, cols], psum[0:QUAD, 5, 0:WB], gate_s[:, 1, cols], row_tmp[0:QUAD, 0, :],
                         (s_fold_free, NB_IN + NB_OUT + 3 + nb))
            layer_norms(2, y_ready)


_NAMES = ["x_prompt", "x_sample", "c_prompt", "c_sample", "cache_k", "cache_v", "state_conv", "page_table",
          "w_ada", "b_ada", "w_in", "conv_w", "lambda_q1", "lambda_k1", "lambda_q2", "lambda_k2", "subln_g",
          "w_out", "ln1_g", "ln1_b", "w_gate", "w_up", "w_down", "ln2_g", "ln2_b"]


def kernel(**inputs):
    import concourse.bacc as bacc
    from concourse.bass_utils import run_bass_kernel_spmd

    nc = bacc.Bacc("TRN2", target_bir_lowering=False, num_devices=1)
    arrays = {n: np.ascontiguousarray(inputs[n]) for n in _NAMES}
    z = Shapes({n: a.shape for n, a in arrays.items()})
    arrays["consts"], const_at = constants(z)
    io = {n: nc.dram_tensor(n, a.shape, mybir.dt.from_np(a.dtype), kind="ExternalInput").ap() for n, a in arrays.items()}
    outs = [("y_prompt", (1, z.T, z.D)), ("y_sample", (z.B, z.S, z.D)),
            ("new_k_prompt", (1, 1, z.T, z.H, z.HD)), ("new_v_prompt", (1, 1, z.T, z.H, z.HD)),
            ("new_conv_prompt", (1, 1, 2, z.CC)),
            ("new_k_sample", (1, z.B, z.S, z.H, z.HD)), ("new_v_sample", (1, z.B, z.S, z.H, z.HD)),
            ("new_conv_sample", (1, z.B, 2, z.CC))]
    for n, shape in outs:
        io[n] = nc.dram_tensor(n, shape, F32, kind="ExternalOutput").ap()
    build(nc, z, io, const_at, arrays["consts"].shape[1])
    r = run_bass_kernel_spmd(nc, [arrays], core_ids=[0])
    return tuple(r.results[0][n] for n, _ in outs)
```

```python
import math
from contextlib import ExitStack, contextmanager

import numpy as np

import concourse.bass as bass
from concourse import mybir

F32 = mybir.dt.float32
F32R = mybir.dt.float32r
I32 = mybir.dt.int32
ALU = mybir.AluOpType
ACT = mybir.ActivationFunctionType
AX_X = mybir.AxisListType.X
ds = bass.ds

P = 128
QUAD = 32
BANK = 512
ROPE_THETA = 500000.0
LN_EPS = 1e-5
MASKED = -1.0e30


class Shapes:

    def __init__(self, s):
        self.T, self.D = s["x_prompt"][1:]
        self.B, self.S = s["x_sample"][:2]
        self.DEPTH, self.POOL, self.PAGE, self.H, self.HD = s["cache_k"]
        self.PAGES = s["page_table"][1]
        self.F = s["w_gate"][2]
        self.IN = s["w_in"][2]
        self.CC = s["conv_w"][2]
        self.MODS = s["w_ada"][2] // self.D
        self.BS = self.B * self.S
        self.KC = self.D // P
        self.NT = self.T // P
        self.CH = min(BANK, self.T)
        self.NCH = self.T // self.CH
        self.NF = self.F // P
        self.AW = self.H * self.HD
        self.ALPHA = (2.0 * self.DEPTH) ** 0.25
        assert self.DEPTH == 1 and self.PAGE == P and self.HD == P and self.H == 4
        assert self.BS == QUAD and self.KC % 4 == 0 and self.T % (2 * P) == 0 and self.F % 256 == 0
        assert self.PAGES % 16 == 0 and self.CC == self.AW == 512 and self.B == 8 and self.S == 4


def constants(z):
    p = np.arange(P)
    out = {}
    out["ident"] = np.eye(P)
    out["quad_fold"] = (p[:, None] % QUAD == np.arange(QUAD)[None, :])
    out["pick_prompt"] = np.repeat((p % QUAD == 0)[:, None], P, axis=1)
    out["pick_sample"] = (p[:, None] % QUAD == 1 + np.arange(QUAD)[None, :] // z.S)
    h, q = p // QUAD, p % 8
    out["head_fold"] = (h[:, None] == h[None, :]) & (q[:, None] == q[None, :])
    out["causal"] = np.where(p[None, :] <= p[:, None], 0.0, MASKED)
    a, t = (p // 8) % 4, p % z.S
    bb, tt = np.arange(QUAD) // z.S, np.arange(QUAD) % z.S
    ok = (a[:, None, None] == 0) & (np.arange(z.B)[None, :, None] == bb[None, None, :]) & (
        tt[None, None, :] <= t[:, None, None])
    out["new_mask"] = np.where(ok, 0.0, MASKED).reshape(P, -1)
    ht = np.arange(z.H * z.S)
    out["own_head"] = (h[:, None] == ht[None, :] // z.S) & (((p // 8) % 4) == h)[:, None] & (
        t[:, None] == ht[None, :] % z.S)
    out["comp0"] = (q < z.S)[:, None]
    out["comp1"] = (q >= z.S)[:, None]
    out["mean"] = np.full((P, P), 1.0 / P)
    rot = z.HD // 2 // 4
    inv = (np.float32(ROPE_THETA) ** (-np.arange(0, rot, 2, dtype=np.float32) / np.float32(rot))).astype(np.float32)
    pos = np.arange(z.T, dtype=np.float32).reshape(z.NT, P).T
    ang = (pos[:, :, None] * inv).astype(np.float32)
    out["cos_p"], out["sin_p"] = np.cos(ang).reshape(P, -1), np.sin(ang).reshape(P, -1)
    pos = (z.PAGES * z.PAGE + p % z.S).astype(np.float32)
    ang = (pos[:, None] * inv).astype(np.float32)
    out["cos_s"], out["sin_s"] = np.cos(ang), np.sin(ang)
    where, n = {}, 0
    for k, v in out.items():
        where[k] = (n, n + v.shape[1])
        n += v.shape[1]
    return np.ascontiguousarray(np.concatenate([np.asarray(v, np.float32) for v in out.values()], axis=1)), where


def build(nc, z, io, const_at, n_const):
    T, D, B, S, H, HD, F = z.T, z.D, z.B, z.S, z.H, z.HD, z.F
    KC, NT, CH, NCH, NF, BS, AW, CC = z.KC, z.NT, z.CH, z.NCH, z.NF, z.BS, z.AW, z.CC
    QK = HD // 2
    SCORE_SCALE = QK ** -0.5
    WB = 256
    FT = WB // P
    GP, RING = 4, 4
    REVS = z.PAGES // (GP * RING)
    NEW0 = z.PAGES * QUAD
    SC = NEW0 + QUAD
    NADA = z.MODS * D // BANK
    NG = F // WB
    NB_IN, NB_OUT = z.IN // WB, D // WB
    lam_init = 0.8 - 0.6 * math.exp(-0.3 * 0)

    with ExitStack() as ctx:
        base = [16512]

        def place(name, shape, dt, at):
            return nc.alloc_sbuf_tensor_at(name, shape, dt, offset=at)

        def keep(name, shape, dt=F32):
            n = int(np.prod(shape[1:])) * 4
            at = base[0]
            base[0] += -(-n // 32) * 32
            return place(name, shape, dt, at)

        class Area:

            def __init__(self, at):
                self.at = at

            def __call__(self, name, shape, dt=F32):
                n = int(np.prod(shape[1:])) * 4
                t = place(name, shape, dt, self.at)
                self.at += -(-n // 32) * 32
                return t

        psum = ctx.enter_context(nc.psum_tensor("psum", [P, 8, BANK], F32))

        def sem(name):
            return ctx.enter_context(nc.semaphore(name))

        consts = keep("consts", [P, n_const])
        C = lambda name: consts[:, const_at[name][0]:const_at[name][1]]
        ident = C("ident")
        mod_t = keep("mod_t", [P, 4, KC, QUAD])
        gate_p = keep("gate_p", [P, 2, D])
        gate_s = keep("gate_s", [QUAD, 2, D])
        lam_rows_at = base[0]
        lam_rows = keep("lam_rows", [P, 4, QK])
        small = keep("small", [P, 16])
        NEG_LAM, COEF = small[:, 6:7], small[:, 8:9]
        ln1_t = keep("ln1_t", [P, 2, KC])
        eps_col = keep("eps_col", [P, 1])
        g_attn = keep("g_attn", [P, 1])
        conv_w_t = keep("conv_w_t", [P, 3, CC // P])
        q_all = keep("q_all", [P, 4 * H, BS])
        q_blocks = keep("q_blocks", [P, H, 4, QUAD])
        k_new_t = keep("k_new_t", [P, AW])
        v_new = keep("v_new", [P, AW])
        o_t_all = keep("o_t_all", [P, B, H * S])
        xs_rows = keep("xs_rows", [QUAD, D])
        y_conv_at = base[0]
        y_conv = keep("y_conv", [P, CC // P, T])
        base[0] = max(base[0], y_conv_at + 16 * D, y_conv_at + 8 * FT * T)
        y_s_at = base[0]
        y_s = keep("y_s", [QUAD, CC])
        stage0 = base[0]

        ar = Area(stage0)
        c_rows = ar("c_rows", [16, D])
        silu_t = ar("silu_t", [P, KC, QUAD])
        ada_w = ar("ada_w", [P, 2, KC, BANK])
        ada_bias = ar("ada_bias", [P, z.MODS * D])
        ada_out = ar("ada_out", [P, z.MODS * D])
        ada_end = ar.at

        ar = Area(stage0)
        x_hi = ar("x_hi", [P, KC, T], F32R)
        x_lo = ar("x_lo", [P, KC, T], F32R)
        w_hi = ar("w_hi", [P, 2, KC, WB], F32R)
        w_lo = ar("w_lo", [P, 2, KC, WB], F32R)
        ar.at = max(ar.at, ada_end)
        w_raw = ar("w_raw", [P, 2, KC, WB])
        x_t_s = ar("x_t_s", [P, KC, QUAD])
        s_quads = ar("s_quads", [P, 2, WB])
        dense_end = max(ar.at, stage0 + 4 * ((2 * RING + 2) * GP * AW + B * z.PAGES + NT * AW + SC + 2 * T + P + 64))
        ar.at = dense_end
        u_conv = ar("u_conv", [P, CC // P, T + 2])
        ar.at = max(ar.at, dense_end + 8 * NT * WB, dense_end + 8192 + 4 * CC)
        x_rows = place("x_rows", [P, NT, D], F32, dense_end)
        x_mod = place("x_mod", [P, 2, CH], F32, dense_end + 4 * NT * D)
        z_s = ar("z_s", [QUAD, z.IN])
        z_rows = place("z_rows", [P, 2, NT, WB], F32, dense_end)
        rope_p = ar("rope_p", [P, 4, NT * 32])
        rope_s = ar("rope_s", [QUAD, 4, 4 * H * 8])
        q_wide = place("q_wide", [QUAD, 4 * H, 4, QUAD], F32, dense_end)
        u_s = place("u_s", [QUAD, CC], F32, dense_end + 8192)

        ar = Area(stage0)
        k_ring = ar("k_ring", [P, RING, GP, AW])
        v_ring = ar("v_ring", [P, RING, GP, AW])
        k_turned = place("k_turned", [P, 2, GP, AW], F32, ar.at)
        conv_s = ar("conv_s", [QUAD, 7, CC])
        ar.at += 2 * GP * AW * 4 - 7 * CC * 4
        page_row = ar("page_row", [1, B * z.PAGES], mybir.dt.int32)
        v_rows = ar("v_rows", [P, NT, AW])
        e_rows = ar("e_rows", [P, 2, T])
        s_rows = ar("s_rows", [P, SC])
        soft = ar("soft", [P, 8])
        dec = ar("dec", [P, 16])
        p_new = ar("p_new", [P, QUAD])
        o_scaled = ar("o_scaled", [P, P])
        assert ar.at <= dense_end
        ar = Area(dense_end)
        o_rows = ar("o_rows", [P, NT, AW])
        q_zero = ar("q_zero", [P, 2, T])
        k_t = ar("k_t", [P, T])
        a_rows = ar("a_rows", [P, T])
        a_t = ar("a_t", [P, T])
        ar = Area(y_conv_at)
        k_rows = ar("k_rows", [P, NT, HD])
        q_rows = ar("q_rows", [P, NT, HD])
        p_t = ar("p_t", [P, z.PAGES, QUAD])
        max_row = place("max_row", [1, 2, P], F32, lam_rows_at)

        sq_rows = place("sq_rows", [P, NT, AW], F32, dense_end + 4 * NT * AW)
        ar = Area(dense_end)
        x1 = ar("x1", [P, NT, D])
        stats = ar("stats", [P, max(NT * H, (NT + 1) * NB_OUT * 6)])
        rstd = ar("rstd", [P, 64])
        gate_act_s = place("gate_act_s", [QUAD, WB], F32, y_s_at)
        h_s = place("h_s", [QUAD, WB], F32, y_s_at + 4 * WB)
        h_t_s_at = ar.at
        h_t_s = ar("h_t_s", [P, NF, QUAD])
        on_y_conv = y_conv_at
        h_out = place("h_out", [P, FT, T], F32, on_y_conv)
        x1_mod = place("x1_mod", [P, 2, CH], F32, on_y_conv)
        row_tmp = place("row_tmp", [P, 2, WB], F32, on_y_conv + 8 * CH)
        ln_rows = place("ln_rows", [P, 2, D], F32, on_y_conv + 8 * D)

        ar = Area(stage0)
        h_all = ar("h_all", [P, NF, T])
        h_hi = ar("h_hi", [P, 3, T], F32R)
        d_raw = ar("d_raw", [P, 4, 2, WB])
        d_hi = ar("d_hi", [P, 3, WB], F32R)
        d_lo = ar("d_lo", [P, 3, WB], F32R)
        assert ar.at <= dense_end
        h_lo = place("h_lo", [P, 3, T], F32R, on_y_conv)
        down_tmp = place("down_tmp", [P, 2, WB], F32, on_y_conv + 12 * D)
        ln2_rows = place("ln2_rows", [P, 2, D], F32, stage0)
        o_t_sq = place("o_t_sq", [P, B * H * S], F32, h_t_s_at)

        q_store = nc.dram_tensor("q_store", (T, AW), F32, kind="Internal").ap()
        y_conv_store = nc.dram_tensor("y_conv_store", (CC, T), F32, kind="Internal").ap()
        u_ext = nc.dram_tensor("u_ext", (B, S + 2, CC), F32, kind="Internal").ap()
        h_store = nc.dram_tensor("h_store", (F, T), F32, kind="Internal").ap()
        k_out = io["new_k_prompt"].rearrange("l b t h d -> (l b t) (h d)")
        v_out = io["new_v_prompt"].rearrange("l b t h d -> (l b t) (h d)")
        k_pages = io["cache_k"].rearrange("l n p h d -> (l n) p (h d)")
        v_pages = io["cache_v"].rearrange("l n p h d -> (l n) p (h d)")
        x_dram = io["x_prompt"].rearrange("b t d -> (b t) d")
        y_dram = io["y_prompt"].rearrange("b t d -> (b t) d")
        xs_dram = io["x_sample"].rearrange("b t d -> (b t) d")
        ys_dram = io["y_sample"].rearrange("b t d -> (b t) d")
        by_rows = lambda w: w[0].rearrange("(k p) n -> p k n", p=P)
        w_ada, w_in, w_out = by_rows(io["w_ada"]), by_rows(io["w_in"]), by_rows(io["w_out"])
        w_gate, w_up, w_down = by_rows(io["w_gate"]), by_rows(io["w_up"]), by_rows(io["w_down"])
        row_of = lambda name: io[name].rearrange("l d -> (l d)")

        stage_done = sem("stage_done")
        dve_step = sem("dve_step")
        consts_in, c_in, vectors_in, bias_in = sem("consts_in"), sem("c_in"), sem("vectors_in"), sem("bias_in")
        bias_zeroed, silu_zeroed, c_turned, silu_ready = (
            sem("bias_zeroed"), sem("silu_zeroed"), sem("c_turned"), sem("silu_ready"))
        ada_in = [sem("ada_in0"), sem("ada_in1")]
        ada_done, ada_banks_free = sem("ada_done"), sem("ada_banks_free")
        mod_done, mod_kept, gates_done, gates_kept = (
            sem("mod_done"), sem("mod_kept"), sem("gates_done"), sem("gates_kept"))
        lam_sums, lam_exps = sem("lam_sums"), sem("lam_exps")
        xs_in, x_in = sem("xs_in"), [sem(f"x_in{c}") for c in range(NCH)]
        x_turned, x_banks_free, x_hi_done, x_split = sem("x_turned"), sem("x_banks_free"), sem("x_hi_done"), sem("x_split")
        xs_turned, xs_ready = sem("xs_turned"), sem("xs_ready")
        w_in_sem = [sem("w_landed0"), sem("w_landed1")]
        w_hi_done, w_lo_done = sem("w_hi_done"), sem("w_lo_done")
        s_done, s_quads_free, s_folded, s_fold_free = (
            sem("s_done"), sem("s_quads_free"), sem("s_folded"), sem("s_fold_free"))
        fm_done, fm_free, tm_done, tm_free = sem("fm_done"), sem("fm_free"), sem("tm_done"), sem("tm_free")
        conv_ready, conv_stored, roped, z_stored = (
            sem("conv_ready"), sem("conv_stored"), sem("roped"), [sem("z_stored0"), sem("z_stored1")])
        s_conv_ready, s_roped, s_stored, u_ext_in = (
            sem("s_conv_ready"), sem("s_roped"), sem("s_stored"), sem("u_ext_in"))
        q_wide_ready, q_all_done, q_all_kept = sem("q_wide_ready"), sem("q_all_done"), sem("q_all_kept")
        conv_s_in, v_in_rows, qk_in = sem("conv_s_in"), sem("v_in_rows"), sem("qk_in")
        y_conv_kept, y_conv_in, k_rows_turned, k_t_ready = (
            sem("y_conv_kept"), sem("y_conv_in"), sem("k_rows_turned"), sem("k_t_ready"))
        q_zeroed, rows_turned, head_ready = sem("q_zeroed"), sem("rows_turned"), sem("head_ready")
        scores_done, neg_max, score_banks_free = sem("scores_done"), sem("neg_max"), sem("score_banks_free")
        a_ready, a_turned, a_t_ready = sem("a_ready"), sem("a_turned"), sem("a_t_ready")
        pv_done, o_free = sem("pv_done"), sem("o_free")
        k_in = [sem(f"k_in{g}") for g in range(RING)]
        v_in = [sem(f"v_in{g}") for g in range(RING)]
        pages_in = sem("pages_in")
        k_free, v_free, scored, s_bank_free = sem("k_free"), sem("v_free"), sem("scored"), sem("s_bank_free")
        q_ready, new_scored, max_ready, max_turned = (
            sem("q_ready"), sem("new_scored"), sem("max_ready"), sem("max_turned"))
        max_spread, max_back, negmax_ready, exp_done = (
            sem("max_spread"), sem("max_back"), sem("negmax_ready"), sem("exp_done"))
        p_turned, p_by_act, p_by_dve = sem("p_turned"), sem("p_by_act"), sem("p_by_dve")
        o_scaled_ready, o_t_done, o_t_kept = (
            sem("o_scaled_ready"), sem("o_t_done"), sem("o_t_kept"))
        sq_ready, sq_root, o_normed, o_turned, o_hi_done, o_banks_free = (
            sem("sq_ready"), sem("sq_root"), sem("o_normed"), sem("o_turned"), sem("o_hi_done"), sem("o_banks_free"))
        os_sq, os_mean, os_root, ys_turned = sem("os_sq"), sem("os_mean"), sem("os_root"), sem("ys_turned")
        y_hi_done = sem("y_hi_done")
        x1_in, ln_in, var_ready, root_ready, norm_ready, x1_ready, x1_scaled, moments_in = (
            sem("x1_in"), sem("ln_in"), sem("var_ready"), sem("root_ready"), sem("norm_ready"), sem("x1_ready"),
            sem("x1_scaled"), sem("moments_in"))
        gate_free, up_free, gs_taken, hs_ready, hs_turned, us_taken = (
            sem("gate_free"), sem("up_free"), sem("gs_taken"), sem("hs_ready"), sem("hs_turned"), sem("us_taken"))
        h_stored, x1_times_g = sem("h_stored"), sem("x1_times_g")
        h_in = [sem(f"h_in{j}") for j in range(NF // 2)]
        d_in = [sem(f"d_in{j}") for j in range(4)]
        d_hi_done, d_split, d_used, down_done, down_free = (
            sem("d_hi_done"), sem("d_split"), sem("d_used"), sem("down_done"), sem("down_free"))
        y_ready, y_stored = sem("y_ready"), sem("y_stored")

        TILES = ([i for i in range(NT) if i % 4 in (0, 3)], [i for i in range(NT) if i % 4 in (1, 2)])
        assert 2 * H == B and NT == 2 * REVS and RING == 4 and REVS <= 4
        MISC, ROWS, OUT = 4, 5, 7
        TPC = CH // P
        UNITS = NCH * KC
        PAIRS = NF // 2
        TB = min(4, NT)
        DB = NT // 2
        MIX0, FF0 = NB_IN, NB_IN + NB_OUT

        cols_of = "cchhbb"
        in_cols = [2 * CC, 2 * CC + WB, 0, WB, CC, CC + WB] + [3 * CC + WB * j for j in range(6)]

        def stage_end(eng, n):
            eng.drain().then_inc(stage_done, 1)
            eng.wait_ge(stage_done, 4 * n)

        def chain(eng, steps):
            count = [0, 0]

            def link(ins):
                count[1] += 1
                ins.then_inc(steps, 1)
                eng.wait_ge(steps, count[0] + count[1])

            @contextmanager
            def loop(turns, links):
                first = count[0] + count[1]
                with eng.Fori(0, turns) as i:
                    count[0], count[1] = first + i * links, 0
                    yield i
                    assert count[1] == links, (count[1], links)
                count[0], count[1] = first + turns * links, 0

            return link, loop

        def regroup(copy, j):
            got = psum[QUAD * j:QUAD * (j + 1), 0:REVS, :].rearrange("p r n -> p (r n)").rearrange(
                "p (g h a q) -> p g h a q", h=H, a=4, q=8)
            to = p_t[:].rearrange("p (g j) (h q) -> p g j h q", j=4, q=8)
            for a in range(4):
                last = copy(to[QUAD * a:QUAD * (a + 1), :, j], got[:, :, :, a, :])
            return last

        def rope(x1_, x2_, cos, sin, tmp, link, done):
            v = nc.vector
            v.tensor_tensor(tmp[0], x1_, cos, ALU.mult)
            v.tensor_tensor(tmp[1], x2_, sin, ALU.mult)
            v.tensor_tensor(tmp[2], x2_, cos, ALU.mult)
            link(v.tensor_tensor(tmp[3], x1_, sin, ALU.mult))
            v.tensor_tensor(x1_, tmp[0], tmp[1], ALU.subtract)
            v.tensor_tensor(x2_, tmp[2], tmp[3], ALU.add).then_inc(done, 1)

        block = ctx.enter_context(nc.Block())

        def load_pages(eng, pages, ring, landed, free):
            with eng.Fori(0, B * REVS) as r:
                for g in range(RING):
                    at = r * (RING * GP) + g * GP
                    for j in range(GP):
                        page = eng.value_load(page_row[0:1, ds(at + j, 1)], min_val=0, max_val=z.POOL - 1)
                        if j == 0:
                            eng.wait_ge(free, r * RING + g + 1)
                        eng.dma_start(ring[:, g, j, :], pages[ds(page, 1)].rearrange("o p d -> p (o d)")
                                      ).then_inc(landed[g], 16)

        def fetch_head(eng, h):
            for rows, src in ((k_rows, k_out), (q_rows, q_store)):
                eng.dma_start(rows[:], src[:, ds(h * HD, HD)].rearrange("(t p) n -> p t n", p=P)).then_inc(qk_in, 16)

        @block.sync
        def _(sp):
            sp.dma_start(consts[:], io["consts"]).then_inc(consts_in, 16)
            sp.dma_start(c_rows[0:1, :], io["c_prompt"]).then_inc(c_in, 16)
            sp.dma_start(c_rows[1:1 + B, :], io["c_sample"]).then_inc(c_in, 16)

            def load_ada(s, n):
                sp.dma_start(ada_w[:, s], w_ada[:, :, ds(n * BANK, BANK)]).then_inc(ada_in[s], 16)

            load_ada(0, 0)
            load_ada(1, 1)
            for j, name in enumerate(("lambda_q1", "lambda_k1", "lambda_q2", "lambda_k2")):
                sp.dma_start(lam_rows[:, j, :], row_of(name).partition_broadcast(P)).then_inc(vectors_in, 16)
            with nc.allow_non_contiguous_dma(reason="a few vectors by feature"):
                sp.dma_start(g_attn[:], io["subln_g"].rearrange("l d -> d l")).then_inc(vectors_in, 16)
                for j, name in enumerate(("ln1_g", "ln1_b")):
                    sp.dma_start(ln1_t[:, j, :], row_of(name).rearrange("(k p) -> p k", p=P)).then_inc(vectors_in, 16)
                for j in range(3):
                    sp.dma_start(conv_w_t[:, j, :], io["conv_w"][0, j].rearrange("(f p) -> p f", p=P)).then_inc(vectors_in, 16)
            sp.wait_ge(bias_zeroed, 1)
            sp.dma_start(ada_bias[0:QUAD, :], row_of("b_ada").partition_broadcast(QUAD)).then_inc(bias_in, 16)
            with sp.Fori(1, NADA // 2) as i:
                for s in range(2):
                    sp.wait_ge(ada_done, 2 * i + s - 1)
                    load_ada(s, 2 * i + s)

            def load_w(n, w, col):
                if not isinstance(n, int) or n >= 2:
                    sp.wait_ge(s_folded, n - 1)
                s = n % 2
                sp.dma_start(w_raw[:, s], w[:, :, ds(col, WB)]).then_inc(w_in_sem[s], 16)

            for c in range(NCH):
                sp.dma_start(x_rows[:, c * TPC:(c + 1) * TPC, :], x_dram[c * CH:(c + 1) * CH, :].rearrange("(t p) d -> p t d", p=P)
                             ).then_inc(x_in[c], 16)
            sp.dma_start(xs_rows[:], xs_dram).then_inc(xs_in, 16)
            for n in range(2):
                load_w(n, w_in, in_cols[n])
            stage_end(sp, 1)

            def store_z(m):
                if m < 4:
                    sp.wait_ge(roped, m + 1)
                else:
                    sp.wait_ge(tm_free, TB + NT * (m + 1))
                to = (q_store, k_out, v_out)[m // 2]
                sp.dma_start(to[:, (m % 2) * WB:(m % 2 + 1) * WB].rearrange("(t p) n -> p t n", p=P),
                             z_rows[:, m % 2]).then_inc(z_stored[m % 2], 16)

            for n in range(2, NB_IN):
                load_w(n, w_in, in_cols[n])
                if n == 6:
                    sp.wait_ge(conv_ready, 1)
                    with nc.allow_non_contiguous_dma(reason="two tokens' rows by feature"):
                        for f in range(CC // P):
                            sp.dma_start(io["new_conv_prompt"][0, 0][:, f * P:(f + 1) * P].rearrange("j p -> p j"),
                                         u_conv[:, f, T:T + 2]).then_inc(conv_stored, 16)
                if n - 2 >= 6:
                    store_z(n - 8)
            sp.wait_ge(fm_free, 2 + 6 * FT)
            sp.dma_start(y_conv_store.rearrange("(f p) t -> p f t", p=P), y_conv[:]).then_inc(y_conv_kept, 16)
            store_z(4)
            store_z(5)
            sp.wait_ge(s_conv_ready, 1)
            sp.dma_start(u_ext[:, 2:2 + S, :].rearrange("b t c -> b t c"), u_s[:]).then_inc(u_ext_in, 16)
            sp.dma_start(u_ext[:, 0:2, :], io["state_conv"][0]).then_inc(u_ext_in, 16)
            sp.wait_ge(s_roped, 1)
            sp.dma_start(io["new_k_sample"].rearrange("l b t h d -> (l b t) (h d)"), z_s[:, 3 * CC + AW:3 * CC + 2 * AW]).then_inc(s_stored, 16)
            sp.dma_start(io["new_v_sample"].rearrange("l b t h d -> (l b t) (h d)"), z_s[:, 3 * CC + 2 * AW:]).then_inc(s_stored, 16)
            sp.wait_ge(u_ext_in, 32)
            sp.dma_start(io["new_conv_sample"][0], u_ext[:, S:S + 2, :]).then_inc(s_stored, 16)
            sp.wait_ge(s_stored, 48)
            sp.wait_ge(conv_stored, 16 * (CC // P))
            for s in range(2):
                sp.wait_ge(z_stored[s], 48)
            sp.wait_ge(y_conv_kept, 16)
            stage_end(sp, 2)

            for j in range(3):
                sp.dma_start(conv_s[:, j, :], u_ext[:, j:j + S, :]).then_inc(conv_s_in, 16)
            for j in range(3):
                sp.dma_start(conv_s[:, 4 + j, :], io["conv_w"][0, j].partition_broadcast(QUAD)).then_inc(conv_s_in, 16)
            sp.dma_start(page_row[:], io["page_table"].rearrange("b n -> (b n)").rearrange("(o n) -> o n", o=1)).then_inc(pages_in, 16)
            sp.wait_ge(pages_in, 16)
            load_pages(sp, k_pages, k_ring, k_in, k_free)
            stage_end(sp, 3)
            sp.dma_start(y_conv[:], y_conv_store.rearrange("(f p) t -> p f t", p=P)).then_inc(y_conv_in, 16)
            stage_end(sp, 4)

            sp.dma_start(x1[:], x_dram.rearrange("(t p) d -> p t d", p=P)).then_inc(x1_in, 16)
            for j, name in enumerate(("ln1_g", "ln1_b")):
                sp.dma_start(ln_rows[:, j, :], row_of(name).partition_broadcast(P)).then_inc(ln_in, 16)
            for j in range(NB_OUT):
                load_w(MIX0 + j, w_out, j * WB)
            stage_end(sp, 5)

            def load_ff(i, which):
                sp.wait_ge(s_folded, FF0 - 1 + which + 2 * i)
                sp.dma_start(w_raw[:, which], (w_gate, w_up)[which][:, :, ds(i * WB, WB)]).then_inc(w_in_sem[which], 16)

            sp.sem_inc(h_stored, 16)
            load_ff(0, 0)
            load_ff(0, 1)

            def store_h(i):
                sp.wait_ge(up_free, 2 + FT + i * FT)
                sp.dma_start(h_store[ds(i * WB, WB), :].rearrange("(f p) t -> p f t", p=P), h_out[:]).then_inc(h_stored, 16)

            with sp.Fori(0, NG - 1) as i:
                load_ff(i + 1, 0)
                load_ff(i + 1, 1)
                store_h(i)
            store_h(NG - 1)
            sp.wait_ge(h_stored, 16 * (NG + 1))
            sp.wait_ge(x1_scaled, NT + 1)
            stage_end(sp, 6)

            def load_d(nb, pp):
                if pp >= 4:
                    sp.wait_ge(d_used, nb * NF + 2 + 2 * (pp - 3))
                elif not isinstance(nb, int):
                    before = max(p for p in range(PAIRS) if p % 4 == pp)
                    sp.wait_ge(d_used, nb * NF - NF + 2 + 2 * (before + 1))
                sp.dma_start(d_raw[:, pp % 4], w_down[:, 2 * pp:2 * pp + 2, ds(nb * WB, WB)]).then_inc(d_in[pp % 4], 16)

            h_view = h_store.rearrange("(k p) t -> p k t", p=P)
            for pp in range(PAIRS):
                sp.dma_start(h_all[:, 2 * pp:2 * pp + 2, :], h_view[:, 2 * pp:2 * pp + 2, :]).then_inc(h_in[pp], 16)
                load_d(0, pp)
            with sp.Fori(1, D // WB) as nb:
                for pp in range(PAIRS):
                    load_d(nb, pp)
            sp.wait_ge(d_used, 2 + (D // WB) * NF)
            for j, name in enumerate(("ln2_g", "ln2_b")):
                sp.dma_start(ln2_rows[:, j, :], row_of(name).partition_broadcast(P)).then_inc(ln_in, 16)
            for t in range(NT):
                sp.wait_ge(y_ready, t + 1)
                sp.dma_start(y_dram[t * P:(t + 1) * P, :], x1[:, t, :]).then_inc(y_stored, 16)
            sp.wait_ge(y_ready, NT + 1)
            sp.dma_start(ys_dram, xs_rows[:]).then_inc(y_stored, 16)
            sp.wait_ge(y_stored, 16 * (NT + 1))

        @block.gpsimd
        def _(pool):
            pool.wait_ge(stage_done, 8)
            pool.dma_start(v_rows[:], v_out.rearrange("(t p) n -> p t n", p=P)).then_inc(v_in_rows, 16)
            pool.wait_ge(pages_in, 16)
            load_pages(pool, v_pages, v_ring, v_in, v_free)

            pool.wait_ge(stage_done, 20)
            pool.wait_ge(ln_in, 32)
            for t in range(NT + 1):
                x, g, b = ((x1[:, t, :], ln_rows[:, 0, :], ln_rows[:, 1, :]) if t < NT
                           else (xs_rows[:], ln_rows[0:QUAD, 0, :], ln_rows[0:QUAD, 1, :]))
                nc.gpsimd.tensor_tensor(x, x, g, ALU.mult).then_inc(x1_times_g, 1)
                pool.wait_ge(x1_times_g, t + 1)
                nc.gpsimd.tensor_tensor(x, x, b, ALU.add).then_inc(x1_scaled, 1)

        @block.tensor
        def _(pe):
            mm, turn = nc.tensor.matmul, nc.tensor.transpose

            pe.wait_ge(consts_in, 16)
            pe.wait_ge(c_in, 32)
            for k in range(KC):
                last = turn(psum[:, 0, 16 * k:16 * k + 1 + B], c_rows[0:1 + B, k * P:(k + 1) * P], ident[0:1 + B, 0:1 + B])
            last.then_inc(c_turned, 1)
            pe.wait_ge(silu_ready, 1)
            with pe.Fori(0, NADA // 2) as i:
                for s in range(2):
                    pe.wait_ge(ada_in[s], 16 * i + 16)
                    pe.wait_ge(ada_banks_free, 2 * i + s + 1)
                    for k in range(KC):
                        q = QUAD * (k % 4)
                        last = mm(psum[q:q + QUAD, 1 + s, :], silu_t[:, k, :], ada_w[:, s, k, :],
                                  start=k < 4, stop=k >= KC - 4)
                    last.then_inc(ada_done, 1)
            pe.wait_ge(ada_banks_free, 2 + NADA)
            for m, part in enumerate((0, 1, 3, 4)):
                for k in range(KC):
                    at = part * D + k * P
                    last = mm(psum[:, m // 2, (m % 2) * 256 + k * QUAD:(m % 2) * 256 + (k + 1) * QUAD],
                              ada_out[:, at:at + P], C("quad_fold"), start=True, stop=True)
            last.then_inc(mod_done, 1)
            for g, part in enumerate((2, 5)):
                for j in range(D // BANK):
                    mm(psum[:, 2 + 2 * g + j, :], C("pick_prompt"), ada_out[:, part * D + j * BANK:part * D + (j + 1) * BANK],
                       start=True, stop=True).then_inc(gates_done, 1)
            pe.wait_ge(gates_kept, 4)
            for g, part in enumerate((2, 5)):
                for j in range(D // BANK):
                    mm(psum[0:QUAD, 2 + 2 * g + j, :], C("pick_sample"), ada_out[:, part * D + j * BANK:part * D + (j + 1) * BANK],
                       start=True, stop=True).then_inc(gates_done, 1)
            stage_end(pe, 1)

            def turn_unit(rows, u, c, k):
                pe.wait_ge(x_banks_free, u + 1)
                for t in range(TPC):
                    last = turn(psum[:, u % 4, t * P:(t + 1) * P], rows[:, c * TPC + t, k * P:(k + 1) * P], ident)
                last.then_inc(x_turned, 1)

            for c in range(NCH):
                pe.wait_ge(x_in[c], 16)
                for k in range(KC):
                    turn_unit(x_rows, c * KC + k, c, k)

            def turn_sample():
                for k in range(KC):
                    last = turn(psum[:, 4, k * QUAD:(k + 1) * QUAD], xs_rows[:, k * P:(k + 1) * P], ident[0:QUAD, 0:QUAD])
                last.then_inc(xs_turned, 1)

            pe.wait_ge(xs_in, 16)
            turn_sample()
            pe.wait_ge(x_split, 2 + UNITS)
            pe.wait_ge(xs_ready, 1)

            def sample_product(n, s):
                pe.wait_ge(w_lo_done, n + 1)
                pe.wait_ge(s_quads_free, n + 1)
                for k in range(KC):
                    q = QUAD * (k % 4)
                    last = mm(psum[q:q + QUAD, 4 + s, 0:WB], x_t_s[:, k, :], w_raw[:, s, k, :],
                              start=k < 4, stop=k >= KC - 4)
                last.then_inc(s_done, 1)

            def sample_fold(n, s, free, value):
                pe.wait_ge(s_quads_free, n + 3)
                pe.wait_ge(free, value)
                mm(psum[0:QUAD, 6 + s, 0:WB], C("quad_fold"), s_quads[:, s, :],
                   start=True, stop=True).then_inc(s_folded, 1)

            PARTS = ((w_hi, x_hi), (w_hi, x_lo), (w_lo, x_hi))

            def by_feature(s, ft):
                for k in range(KC):
                    for j, (w, x) in enumerate(PARTS):
                        for c in range(NCH):
                            last = mm(psum[:, 2 * ft + c, 0:CH], w[:, s, k, ft * P:(ft + 1) * P], x[:, k, c * CH:(c + 1) * CH],
                                      start=k == 0 and j == 0, stop=k == KC - 1 and j == 2)
                return last

            def by_token(s, t):
                for k in range(KC):
                    for j, (w, x) in enumerate(PARTS):
                        last = mm(psum[:, t % TB, 0:WB], x[:, k, t * P:(t + 1) * P], w[:, s, k, :],
                                  start=k == 0 and j == 0, stop=k == KC - 1 and j == 2)
                return last

            with pe.Fori(0, 3) as i:
                for s in range(2):
                    n = 2 * i + s
                    sample_product(n, s)
                    for ft in range(FT):
                        pe.wait_ge(fm_free, FT * n + ft + 1)
                        by_feature(s, ft).then_inc(fm_done, 1)
                    sample_fold(n, s, s_fold_free, n + 1)

            def token_blocks(first, count, tm_before):
                with pe.Fori(0, count // 2) as i:
                    for s in range(2):
                        n = first + 2 * i + s
                        sample_product(n, s)
                        for t in range(NT):
                            pe.wait_ge(tm_free, tm_before + (2 * i + s) * NT + t + 1)
                            by_token(s, t).then_inc(tm_done, 1)
                        sample_fold(n, s, s_fold_free, n + 1)

            pe.wait_ge(fm_free, 2 + 6 * FT)
            token_blocks(6, 6, 0)
            pe.wait_ge(q_wide_ready, 1)
            for hb in range(4 * H):
                last = mm(psum[:, 7, hb * BS:(hb + 1) * BS], q_wide[:, hb].rearrange("p a j -> p (a j)"),
                          ident[0:QUAD, 0:QUAD], start=True, stop=True)
            last.then_inc(q_all_done, 1)
            stage_end(pe, 2)

            pe.sem_inc(v_free, RING)

            def head_start(h):
                pe.wait_ge(qk_in, 32 * h + 32)
                pe.wait_ge(a_t_ready, h * NT + 1)
                for t in range(NT):
                    last = turn(psum[:, ROWS + t // 4, (t % 4) * P:(t % 4 + 1) * P], k_rows[:, t, :], ident)
                last.then_inc(k_rows_turned, 1)
                pe.wait_ge(k_t_ready, h + 1)
                for t in range(NT):
                    last = turn(psum[:, ROWS + t // 4, (t % 4) * P:(t % 4 + 1) * P], q_rows[:, t, :], ident)
                last.then_inc(rows_turned, 1)
                pe.wait_ge(head_ready, h + 1)

            def scores(n, i, c):
                pe.wait_ge(score_banks_free, 2 * n + c + 1)
                pe.wait_ge(a_t_ready, n + 1)
                for k0 in range(0, (i + 1) * P, BANK):
                    w = min(BANK, (i + 1) * P - k0)
                    last = mm(psum[:, ROWS + k0 // BANK, 0:w], q_zero[:, c, i * P:(i + 1) * P], k_t[:, k0:k0 + w],
                              start=True, stop=True)
                last.then_inc(scores_done, 1)

            def turn_rows(n, i):
                pe.wait_ge(a_ready, n + 2)
                for j in range(i + 1):
                    last = turn(psum[:, ROWS + j // 4, (j % 4) * P:(j % 4 + 1) * P], a_rows[:, j * P:(j + 1) * P], ident)
                last.then_inc(a_turned, 1)

            def weigh_rows(h, n, i):
                pe.wait_ge(a_t_ready, n + 2)
                pe.wait_ge(o_free, n + 1)
                for j in range(i + 1):
                    last = mm(psum[:, OUT, 0:P], a_t[:, j * P:(j + 1) * P],
                              v_rows[:, j, ds(h * HD, HD)], start=j == 0, stop=j == i)
                last.then_inc(pv_done, 1)

            def new_keys(b):
                pe.wait_ge(q_ready, b + 1)
                for h in range(H):
                    for d in range(4):
                        last = mm(psum[QUAD * h:QUAD * (h + 1), MISC, 416:416 + QUAD], q_blocks[:, h, d, :],
                                  k_new_t[:, h * HD + d * QUAD:h * HD + (d + 1) * QUAD], start=d == 0, stop=d == 3)
                last.then_inc(new_scored, 1)

            def key_group(b, r, g):
                n = (b * REVS + r) * RING + g
                pe.wait_ge(k_free, RING + 1 + n)
                pe.wait_ge(s_bank_free, n + 1)
                for h in range(H):
                    for d in range(4):
                        last = mm(psum[QUAD * h:QUAD * (h + 1), g % 2, 0:GP * QUAD], q_blocks[:, h, d, :],
                                  k_turned[:, g % 2, :, h * HD + d * QUAD:h * HD + (d + 1) * QUAD],
                                  start=d == 0, stop=d == 3)
                last.then_inc(scored, 1)

            def value_group(b, r, g, stop):
                pe.wait_ge(v_in[g], (b * REVS + r + 1) * (16 * GP))
                for j in range(GP):
                    for h in range(H):
                        last = mm(psum[QUAD * h:QUAD * (h + 1), 2, 0:P], p_t[:, (r * RING + g) * GP + j, :],
                                  v_ring[:, g, j, h * HD:(h + 1) * HD], start=False, stop=stop and j == GP - 1)
                last.then_inc(v_free, 1)

            def softmax(b):
                pe.wait_ge(max_ready, b + 1)
                pe.wait_ge(o_t_kept, b + 1)
                turn(psum[0:1, MISC, 0:P], dec[:, 0:1], ident).then_inc(max_turned, 1)
                pe.wait_ge(max_spread, b + 1)
                mm(psum[:, MISC, 256:257], max_row[0:1, 1, :], ident[0:1, 0:1], start=True, stop=True).then_inc(max_back, 1)
                for r in range(REVS):
                    pe.wait_ge(exp_done, b * (REVS + 1) + r + 1)
                    for g in range(4):
                        last = turn(psum[:, r, g * P:(g + 1) * P], s_rows[:, r * BANK + g * P:r * BANK + (g + 1) * P], ident)
                pe.wait_ge(exp_done, (b + 1) * (REVS + 1))
                mm(psum[:, MISC, 384:384 + REVS + 1], C("head_fold"), dec[:, 2:3 + REVS], start=True, stop=True)
                turn(psum[0:QUAD, MISC, P:2 * P], s_rows[:, NEW0:SC], ident).then_inc(p_turned, 1)
                pe.wait_ge(p_by_act, b + 1)
                pe.wait_ge(p_by_dve, b + 1)
                for h in range(H):
                    mm(psum[QUAD * h:QUAD * (h + 1), 2, 0:P], p_new[:], v_new[:, h * HD:(h + 1) * HD], start=True, stop=False)

            def by_query(b):
                pe.wait_ge(o_scaled_ready, b + 1)
                mm(psum[:, MISC, 448:448 + H * S], o_scaled[:], C("own_head"), start=True, stop=True).then_inc(o_t_done, 1)

            def step(b, h, half, first=False):
                if half == 0:
                    pe.wait_ge(v_in_rows, 16)
                    head_start(h)
                if not first:
                    softmax(b - 1)
                new_keys(b)
                for r in range(REVS):
                    n, i = b * REVS + r, TILES[half][r]
                    for g in range(RING):
                        if g < 2:
                            scores(n, i, g)
                        if g == 3:
                            turn_rows(n, i)
                        key_group(b, r, g)
                        if not first:
                            value_group(b - 1, r, g, (r, g) == (REVS - 1, RING - 1))
                    weigh_rows(h, n, i)
                if not first:
                    by_query(b - 1)

            step(0, 0, 0, first=True)
            with pe.Fori(0, H - 1) as i:
                step(2 * i + 1, i, 1)
                step(2 * i + 2, i + 1, 0)
            step(B - 1, H - 1, 1)
            softmax(B - 1)
            for r in range(REVS):
                for g in range(RING):
                    value_group(B - 1, r, g, (r, g) == (REVS - 1, RING - 1))
            by_query(B - 1)
            stage_end(pe, 3)

            pe.wait_ge(o_normed, 1)
            for t in range(NT):
                if t >= 4:
                    pe.wait_ge(o_banks_free, t - 3)
                for h in range(H):
                    last = turn(psum[:, t % 4, h * P:(h + 1) * P], o_rows[:, t, h * HD:(h + 1) * HD], ident)
                last.then_inc(o_turned, 1)
            pe.wait_ge(os_sq, 1)
            mm(psum[:, 4, 0:B * H * S], C("mean"), o_t_sq[:], start=True, stop=True).then_inc(os_mean, 1)
            for k in range(CC // P):
                last = turn(psum[:, 5, k * QUAD:(k + 1) * QUAD], y_s[:, k * P:(k + 1) * P], ident[0:QUAD, 0:QUAD])
            last.then_inc(ys_turned, 1)
            stage_end(pe, 4)
            token_blocks(MIX0, NB_OUT, 6 * NT)
            for c in range(NCH):
                pe.wait_ge(x1_ready, 1 + (c + 1) * TPC)
                for k in range(KC):
                    turn_unit(x1, UNITS + c * KC + k, c, k)
            pe.wait_ge(x1_ready, NT + 1)
            turn_sample()
            stage_end(pe, 5)

            with pe.Fori(0, NG) as i:
                for s in range(2):
                    n = FF0 + 2 * i + s
                    sample_product(n, s)
                    for ft in range(FT):
                        if s == 0:
                            pe.wait_ge(up_free, i * FT + ft + 1)
                        else:
                            pe.wait_ge(gate_free, i * FT + ft + 1)
                        by_feature(s, ft).then_inc(fm_done, 1)
                    sample_fold(n, s, (gs_taken, us_taken)[s], i + 1)
                pe.wait_ge(consts_in, 16)
                pe.wait_ge(hs_ready, i + 1)
                for ft in range(FT):
                    last = turn(psum[:, 7, WB + ft * QUAD:WB + (ft + 1) * QUAD], h_s[:, ft * P:(ft + 1) * P], ident[0:QUAD, 0:QUAD])
                last.then_inc(hs_turned, 1)
            stage_end(pe, 6)

            with pe.Fori(0, D // WB) as nb:
                for k in range(NF):
                    pe.wait_ge(d_split, nb * NF + (k + 3))
                    s = k % 3
                    for t in range(NT):
                        if k == 0 and t % 2 == 0:
                            pe.wait_ge(down_free, nb * DB + t // 2 + 1)
                        for j, (x, w) in enumerate(((h_hi, d_hi), (h_hi, d_lo), (h_lo, d_hi))):
                            last = mm(psum[:, t // 2, (t % 2) * WB:(t % 2 + 1) * WB], x[:, s, t * P:(t + 1) * P], w[:, s, :],
                                      start=k == 0 and j == 0 and t % 2 == 0, stop=k == NF - 1 and j == 2,
                                      skip_group_check=True)
                    if k == 0:
                        pe.wait_ge(s_quads_free, FF0 + 2 * NG + nb + 2)
                    q = QUAD * (k % 4)
                    last = mm(psum[q:q + QUAD, 4, 0:WB], h_t_s[:, k, :], d_raw[:, (k // 2) % 4, k % 2, :],
                              start=k < 4, stop=k >= NF - 4)
                    last.then_inc(d_used, 1)
                pe.wait_ge(s_quads_free, FF0 + 2 * NG + nb + 3)
                mm(psum[0:QUAD, 5, 0:WB], C("quad_fold"), s_quads[:, 0, :], start=True, stop=True).then_inc(s_folded, 1)

        @block.scalar
        def _(act):
            go, copy = nc.scalar.activation, nc.scalar.copy

            act.wait_ge(c_turned, 1)
            act.wait_ge(silu_zeroed, 1)
            go(silu_t[:, :, 0:1 + B], psum[:, 0, 0:16 * KC].rearrange("p (k c) -> p k c", c=16)[:, :, 0:1 + B],
               ACT.Silu).then_inc(silu_ready, 1)
            act.wait_ge(lam_sums, 1)
            go(small[:, 2:4], small[:, 0:2], ACT.Exp).then_inc(lam_exps, 1)
            for part, gates in enumerate((gate_p, gate_s)):
                rows = (P, QUAD)[part]
                for j in range(4):
                    act.wait_ge(gates_done, 4 * part + j + 1)
                    copy(gates[:, j // 2, (j % 2) * BANK:(j % 2 + 1) * BANK], psum[0:rows, 2 + j, :]).then_inc(gates_kept, 1)
            stage_end(act, 1)

            act.sem_inc(x_banks_free, 4)

            def modulate(u, c, k, x, shift, scale):
                act.wait_ge(x_turned, u + 1)
                act.wait_ge(x_split, u + 1)
                go(x[:, u % 2, :], psum[:, u % 4, 0:CH], ACT.Identity, bias=mod_t[:, shift, k, 0:1],
                   scale=mod_t[:, scale, k, 0:1]).then_inc(x_banks_free, 1)
                act.wait_ge(x_banks_free, u + 5)
                copy(x_hi[:, k, c * CH:(c + 1) * CH], x[:, u % 2, :]).then_inc(x_hi_done, 1)

            for c in range(NCH):
                for k in range(KC):
                    modulate(c * KC + k, c, k, x_mod, 0, 1)

            def w_high(n, s, fills):
                act.wait_ge(w_in_sem[s], 16 * fills)
                if not isinstance(n, int) or n >= 2:
                    act.wait_ge(s_folded, n - 1)
                copy(w_hi[:, s], w_raw[:, s]).then_inc(w_hi_done, 1)

            w_high(0, 0, 1)
            for n in range(NB_IN):
                if n + 1 < NB_IN:
                    w_high(n + 1, (n + 1) % 2, (n + 1) // 2 + 1)
                if n >= 6:
                    m = n - 6
                    if m == 0:
                        act.wait_ge(fm_free, 2 + 6 * FT)
                        act.wait_ge(conv_stored, 16 * (CC // P))
                    if m >= 2:
                        act.wait_ge(z_stored[m % 2], 16 * (m // 2))
                    for t in range(NT):
                        act.wait_ge(tm_done, m * NT + t + 1)
                        copy(z_rows[:, m % 2, t, :], psum[:, t % TB, 0:WB]).then_inc(tm_free, 1)
            act.wait_ge(q_all_done, 1)
            copy(q_all[:].rearrange("p h b -> p (h b)"), psum[:, 7, :]).then_inc(q_all_kept, 1)
            stage_end(act, 2)

            fetch_head(act, 0)
            act.sem_inc(score_banks_free, 1)
            act.sem_inc(a_t_ready, 1)
            act.sem_inc(s_bank_free, 2)
            act.sem_inc(o_t_kept, 1)
            act.wait_ge(q_zeroed, 1)

            def head_start(h):
                both = psum[:, ROWS:ROWS + -(-T // BANK), 0:CH]
                act.wait_ge(k_rows_turned, h + 1)
                copy(k_t[:], both.rearrange("p c n -> p (c n)")).then_inc(k_t_ready, 1)
                act.wait_ge(rows_turned, h + 1)
                for c in range(2):
                    r = slice(c * QK, (c + 1) * QK)
                    last = nc.scalar.mul(q_zero[r, c, :], both[r].rearrange("p c n -> p (c n)"), SCORE_SCALE)
                last.then_inc(head_ready, 1)

            def exps(n, i, c):
                act.wait_ge(neg_max, 2 * n + c + 1)
                act.wait_ge(a_ready, n + 1)
                w = (i + 1) * P
                go(e_rows[:, c, 0:w], psum[:, ROWS:ROWS + 2, :].rearrange("p c n -> p (c n)")[:, 0:w], ACT.Exp,
                   bias=soft[:, 2 + c:3 + c], accum_out=soft[:, 4 + c:5 + c]).then_inc(score_banks_free, 1)

            def keep_turned(n, i):
                act.wait_ge(a_turned, n + 2)
                act.wait_ge(pv_done, n + 1)
                w = (i + 1) * P
                copy(a_t[:, 0:w], psum[:, ROWS:ROWS + 2, :].rearrange("p c n -> p (c n)")[:, 0:w]).then_inc(a_t_ready, 1)

            def take_scores(b, r, g):
                n = (b * REVS + r) * RING + g
                act.wait_ge(scored, 3 + n)
                copy(s_rows[:, (r * RING + g) * (GP * QUAD):(r * RING + g + 1) * (GP * QUAD)], psum[:, g % 2, 0:GP * QUAD]
                     ).then_inc(s_bank_free, 1)

            def softmax(b):
                act.wait_ge(negmax_ready, b + 1)
                for r in range(REVS + 1):
                    part = s_rows[:, r * BANK:(r + 1) * BANK] if r < REVS else s_rows[:, NEW0:SC]
                    go(part, part, ACT.Exp, bias=dec[:, 1:2], accum_out=dec[:, 2 + r:3 + r]).then_inc(exp_done, 1)
                act.wait_ge(p_turned, b + 1)
                for j in range(0, 2):
                    last = regroup(copy, j)
                last.then_inc(p_by_act, 1)

            def keep_output(b):
                act.wait_ge(o_t_done, b + 1)
                copy(o_t_all[:, ds(b, 1), :], psum[:, MISC, 448:448 + H * S].rearrange("p (o n) -> p o n", o=1)).then_inc(o_t_kept, 1)

            def step(b, h, half, first=False):
                if half == 0:
                    head_start(h)
                if not first:
                    softmax(b - 1)
                for r in range(REVS):
                    n, i = b * REVS + r, TILES[half][r]
                    for g in range(RING):
                        if g == 3:
                            keep_turned(n, i)
                        take_scores(b, r, g)
                        if g < 2:
                            exps(n, i, g)
                if not first:
                    keep_output(b - 1)

            step(0, 0, 0, first=True)
            with act.Fori(0, H - 1) as i:
                fetch_head(act, i + 1)
                step(2 * i + 1, i, 1)
                step(2 * i + 2, i + 1, 0)
            step(B - 1, H - 1, 1)
            softmax(B - 1)
            keep_output(B - 1)
            stage_end(act, 3)

            act.wait_ge(sq_ready, 1)
            go(rstd[:, 0:NT * H], stats[:, 0:NT * H], ACT.Sqrt, bias=eps_col[:], scale=1.0 / HD).then_inc(sq_root, 1)
            act.wait_ge(y_conv_in, 16)
            copy(x_hi[:, 0:CC // P, :], y_conv[:]).then_inc(y_hi_done, 1)
            for t in range(NT):
                act.wait_ge(o_turned, t + 1)
                go(x_hi[:, CC // P:, t * P:(t + 1) * P], psum[:, t % 4, :].rearrange("p (h n) -> p h n", n=P), ACT.Copy,
                   scale=g_attn[:, 0:1]).then_inc(o_hi_done, 1)
            act.wait_ge(os_mean, 1)
            go(o_t_sq[:], psum[:, 4, 0:B * H * S], ACT.Sqrt, bias=eps_col[:]).then_inc(os_root, 1)
            stage_end(act, 4)
            FILLS = NB_IN // 2
            w_high(MIX0, 0, FILLS + 1)
            for j in range(NB_OUT - 1):
                w_high(MIX0 + j + 1, (j + 1) % 2, FILLS + (j + 1) // 2 + 1)

            def roots(count):
                act.wait_ge(var_ready, count)
                var = rstd[:, 0:2 * NT].rearrange("p (t j) -> p t j", j=2)[:, :, 1]
                go(var, var, ACT.Sqrt, bias=eps_col[:])
                var = rstd[0:QUAD, 2 * NT + 1:2 * NT + 2]
                go(var, var, ACT.Sqrt, bias=eps_col[0:QUAD]).then_inc(root_ready, 1)

            def normalise(t, x):
                rows = x.shape[0]
                go(x, x, ACT.Identity, bias=rstd[0:rows, 48 + t:49 + t], scale=rstd[0:rows, 32 + t:33 + t]).then_inc(x1_ready, 1)

            roots(1)
            act.wait_ge(norm_ready, 1)
            normalise(NT, xs_rows[:])
            for c in range(NCH):
                for t in range(c * TPC, (c + 1) * TPC):
                    normalise(t, x1[:, t, :])
                for k in range(KC):
                    modulate(UNITS + c * KC + k, c, k, x1_mod, 2, 3)
            stage_end(act, 5)

            FILLS = (NB_IN + NB_OUT) // 2
            w_high(FF0, 0, FILLS + 1)

            def gate_up(i, more):
                w_high(FF0 + 1 + 2 * i, 1, FILLS + 1 + i)
                act.wait_ge(h_stored, 16 * i + 16)
                for ft in range(FT):
                    act.wait_ge(fm_done, 6 * FT + 2 * FT * i + ft + 1)
                    go(h_out[:, ft, :], psum[:, 2 * ft:2 * ft + NCH, 0:CH].rearrange("p c n -> p (c n)"), ACT.Silu).then_inc(gate_free, 1)
                act.wait_ge(s_folded, FF0 + 1 + 2 * i)
                act.wait_ge(us_taken, i + 1)
                go(gate_act_s[:], psum[0:QUAD, 6, 0:WB], ACT.Silu).then_inc(gs_taken, 1)
                if more:
                    w_high(FF0 + 2 + 2 * i, 0, FILLS + 2 + i)

            with act.Fori(0, NG - 1) as i:
                gate_up(i, True)
            gate_up(NG - 1, False)
            stage_end(act, 6)

            with act.Fori(0, D // WB) as nb:
                for k in range(NF):
                    pp, s = k // 2, k % 3
                    if k % 2 == 0:
                        fills = (PAIRS - pp % 4 + 3) // 4
                        act.wait_ge(d_in[pp % 4], 16 * (nb * fills + (pp // 4 + 1)))
                    if k % 2 == 0:
                        act.wait_ge(h_in[pp], 16)
                    if k == 0:
                        act.wait_ge(d_used, nb * NF + 2)
                    elif k >= 3:
                        act.wait_ge(d_used, nb * NF + k)
                    copy(h_hi[:, s, :], h_all[:, k, :])
                    copy(d_hi[:, s, :], d_raw[:, pp % 4, k % 2, :]).then_inc(d_hi_done, 1)
            roots(2)
            act.wait_ge(norm_ready, 2)
            for t in range(NT):
                normalise(t, x1[:, t, :])
            normalise(NT, xs_rows[:])

        @block.vector
        def _(dve):
            v = nc.vector
            link, linked_loop = chain(dve, dve_step)

            v.memset(ada_bias[:], 0.0).then_inc(bias_zeroed, 1)
            v.memset(silu_t[:], 0.0).then_inc(silu_zeroed, 1)
            dve.sem_inc(ada_banks_free, 2)
            v.memset(k_new_t[:], 0.0)
            v.memset(v_new[:], 0.0)
            v.memset(q_blocks[:], 0.0)
            link(v.memset(eps_col[:], LN_EPS))
            dve.wait_ge(vectors_in, 16 * 10)
            for j in range(2):
                link(v.tensor_tensor(lam_rows[:, 2 * j, :], lam_rows[:, 2 * j, :], lam_rows[:, 2 * j + 1, :], ALU.mult))
            link(v.tensor_reduce(small[:, 0:1], lam_rows[:, 0, :], AX_X, ALU.add))
            v.tensor_reduce(small[:, 1:2], lam_rows[:, 2, :], AX_X, ALU.add).then_inc(lam_sums, 1)
            dve.wait_ge(lam_exps, 1)
            link(v.tensor_tensor(small[:, 5:6], small[:, 3:4], small[:, 2:3], ALU.subtract))
            link(v.tensor_scalar(NEG_LAM, small[:, 5:6], -lam_init, None, ALU.add))
            dve.wait_ge(consts_in, 16)
            link(v.tensor_scalar(small[:, 7:8], C("comp1"), NEG_LAM, None, ALU.mult))
            link(v.tensor_tensor(COEF, small[:, 7:8], C("comp0"), ALU.add))
            link(v.tensor_scalar(g_attn[:], g_attn[:], 1.0 - lam_init, None, ALU.mult))
            dve.wait_ge(bias_in, 16)
            with dve.Fori(0, NADA // 2) as i:
                for s in range(2):
                    dve.wait_ge(ada_done, 2 * i + s + 1)
                    at = ds((2 * i + s) * BANK, BANK)
                    v.tensor_tensor(ada_out[:, at], psum[:, 1 + s, :], ada_bias[:, at], ALU.add).then_inc(ada_banks_free, 1)
            dve.wait_ge(mod_done, 1)
            for m in range(4):
                last = v.tensor_scalar(mod_t[:, m].rearrange("p k c -> p (k c)"), psum[:, m // 2, (m % 2) * 256:(m % 2) * 256 + KC * QUAD],
                                       float(m % 2), None, ALU.add)
            link(last)
            wide = lambda j: ln1_t[:, j, :].unsqueeze(2).to_broadcast([P, KC, QUAD])
            link(v.tensor_tensor(silu_t[:], mod_t[:, 3], wide(1), ALU.mult))
            link(v.tensor_tensor(mod_t[:, 2], mod_t[:, 2], silu_t[:], ALU.add))
            link(v.tensor_tensor(mod_t[:, 3], mod_t[:, 3], wide(0), ALU.mult))
            stage_end(dve, 1)

            dve.sem_inc(x_split, 2)
            dve.sem_inc(s_quads_free, 2)
            dve.sem_inc(s_fold_free, 2)
            dve.sem_inc(fm_free, 2)
            dve.sem_inc(tm_free, TB)

            def split(u, c, k, x):
                at = slice(c * CH, (c + 1) * CH)
                dve.wait_ge(x_hi_done, u + 1)
                v.tensor_tensor(x_lo[:, k, at], x[:, u % 2, :], x_hi[:, k, at], ALU.subtract).then_inc(x_split, 1)

            def modulate_sample(shift, scale):
                per_token = lambda m: mod_t[:, m, :, 1:1 + B].unsqueeze(3).to_broadcast([P, KC, B, S])
                out = x_t_s[:].rearrange("p k (b t) -> p k b t", t=S)
                link(v.tensor_tensor(out, psum[:, 4, 0:KC * QUAD].rearrange("p (k b t) -> p k b t", b=B, t=S), per_token(scale), ALU.mult))
                v.tensor_tensor(out, out, per_token(shift), ALU.add).then_inc(xs_ready, 1)

            for c in range(NCH):
                for k in range(KC):
                    split(c * KC + k, c, k, x_mod)
            dve.wait_ge(x_split, 2 + UNITS)
            link(v.memset(u_conv[:, :, 0:2], 0.0))
            dve.wait_ge(xs_turned, 1)
            modulate_sample(0, 1)

            def w_low(n, s):
                dve.wait_ge(w_hi_done, n + 1)
                v.tensor_tensor(w_lo[:, s], w_raw[:, s], w_hi[:, s], ALU.subtract).then_inc(w_lo_done, 1)

            def take_quads(n, s):
                dve.wait_ge(s_done, n + 1)
                v.tensor_copy(s_quads[:, s, :], psum[:, 4 + s, 0:WB]).then_inc(s_quads_free, 1)

            w_low(0, 0)
            for n in range(NB_IN):
                s = n % 2
                if n + 1 < NB_IN:
                    w_low(n + 1, 1 - s)
                take_quads(n, s)
                for ft in range(FT):
                    if n >= 6:
                        break
                    f = (n % 2) * FT + ft
                    dve.wait_ge(fm_done, FT * n + ft + 1)
                    got = psum[:, 2 * ft:2 * ft + NCH, 0:CH].rearrange("p c n -> p (c n)")
                    u = u_conv[:, f, 2:2 + T]
                    y = y_conv[:, f, :]
                    if cols_of[n] == "c":
                        v.tensor_copy(u, got).then_inc(fm_free, 1)
                    elif cols_of[n] == "h":
                        v.tensor_tensor(u, got, u, ALU.mult).then_inc(fm_free, 1)
                        dve.wait_ge(fm_free, 3 + FT * n + ft)
                        link(v.tensor_scalar(y, u_conv[:, f, 0:T], conv_w_t[:, 0, f:f + 1], None, ALU.mult))
                        link(v.scalar_tensor_tensor(y, u_conv[:, f, 1:1 + T], conv_w_t[:, 1, f:f + 1], y, ALU.mult, ALU.add))
                        if f == CC // P - 1:
                            v.scalar_tensor_tensor(y, u, conv_w_t[:, 2, f:f + 1], y, ALU.mult, ALU.add).then_inc(conv_ready, 1)
                            dve.wait_ge(conv_ready, 1)
                        else:
                            link(v.scalar_tensor_tensor(y, u, conv_w_t[:, 2, f:f + 1], y, ALU.mult, ALU.add))
                    else:
                        v.tensor_tensor(y, got, y, ALU.mult).then_inc(fm_free, 1)
                if 6 <= n < 10:
                    m = n - 6
                    dve.wait_ge(tm_free, TB + (m + 1) * NT)
                    pair = z_rows[:, m % 2].rearrange("p t (g d) -> p t g d", d=QK)
                    cos = C("cos_p").rearrange("p (t d) -> p t d", d=8).unsqueeze(2).to_broadcast([P, NT, 4, 8])
                    sin = C("sin_p").rearrange("p (t d) -> p t d", d=8).unsqueeze(2).to_broadcast([P, NT, 4, 8])
                    rope(pair[:, :, :, 0:8], pair[:, :, :, 8:16], cos, sin,
                         [rope_p[:, j, :].rearrange("p (t g d) -> p t g d", g=4, d=8) for j in range(4)], link, roped)
                    dve.wait_ge(roped, m + 1)
                dve.wait_ge(s_folded, n + 1)
                v.tensor_copy(z_s[:, in_cols[n]:in_cols[n] + WB], psum[0:QUAD, 6 + s, 0:WB]).then_inc(s_fold_free, 1)
            dve.wait_ge(s_fold_free, 2 + NB_IN)
            for s in range(2):
                dve.wait_ge(z_stored[s], 48)
            v.tensor_copy(y_s[:], z_s[:, CC:2 * CC])
            v.tensor_tensor(u_s[:], z_s[:, 2 * CC:3 * CC], z_s[:, 0:CC], ALU.mult).then_inc(s_conv_ready, 1)
            qk = z_s[:, 3 * CC:3 * CC + 2 * AW].rearrange("p (g d) -> p g d", d=QK)
            cos = C("cos_s")[0:QUAD].unsqueeze(1).to_broadcast([QUAD, 4 * H, 8])
            sin = C("sin_s")[0:QUAD].unsqueeze(1).to_broadcast([QUAD, 4 * H, 8])
            rope(qk[:, :, 0:8], qk[:, :, 8:16], cos, sin,
                 [rope_s[:, j, :].rearrange("p (g d) -> p g d", d=8) for j in range(4)], link, s_roped)
            dve.wait_ge(s_roped, 1)
            v.transpose(k_new_t[0:QUAD, :], z_s[:, 3 * CC + AW:3 * CC + 2 * AW])
            link(v.tensor_copy(v_new[0:QUAD, :], z_s[:, 3 * CC + 2 * AW:]))
            v.tensor_scalar(q_wide[:], z_s[:, 3 * CC:3 * CC + AW].rearrange("p (g j) -> p g j", j=QUAD).unsqueeze(2)
                            .to_broadcast([QUAD, 4 * H, 4, QUAD]), SCORE_SCALE, None, ALU.mult).then_inc(q_wide_ready, 1)
            stage_end(dve, 2)

            dve.sem_inc(k_free, RING)
            dve.sem_inc(a_ready, 1)
            dve.sem_inc(a_turned, 1)
            dve.sem_inc(pv_done, 1)
            dve.sem_inc(o_free, 1)
            dve.sem_inc(scored, 2)
            v.memset(q_zero[:], 0.0).then_inc(q_zeroed, 1)
            dve.wait_ge(conv_s_in, 96)
            for j in range(3):
                link(v.tensor_tensor(conv_s[:, j, :], conv_s[:, j, :], conv_s[:, 4 + j, :], ALU.mult))
            link(v.tensor_tensor(conv_s[:, 0, :], conv_s[:, 0, :], conv_s[:, 1, :], ALU.add))
            link(v.tensor_tensor(conv_s[:, 0, :], conv_s[:, 0, :], conv_s[:, 2, :], ALU.add))
            link(v.tensor_tensor(y_s[:], y_s[:], conv_s[:, 0, :], ALU.mult))
            link(v.memset(p_new[:], 0.0))

            def maxima(n, i, c):
                w = (i + 1) * P
                dve.wait_ge(scores_done, 2 * n + c + 1)
                diag = psum[:, ROWS + i // 4, (i % 4) * P:(i % 4 + 1) * P]
                link(v.tensor_tensor(diag, diag, C("causal"), ALU.add))
                link(v.tensor_reduce(soft[:, c:c + 1], psum[:, ROWS:ROWS + 2, :].rearrange("p c n -> p (c n)")[:, 0:w], AX_X, ALU.max))
                v.tensor_scalar(soft[:, 2 + c:3 + c], soft[:, c:c + 1], -1.0, None, ALU.mult).then_inc(neg_max, 1)

            def combine(n, i):
                w = (i + 1) * P
                dve.wait_ge(score_banks_free, 2 * n + 3)
                link(v.reciprocal(soft[:, 6:8], soft[:, 4:6]))
                link(v.tensor_scalar(soft[:, 7:8], soft[:, 7:8], NEG_LAM, None, ALU.mult))
                dve.wait_ge(a_turned, n + 1)
                link(v.tensor_scalar(a_rows[:, 0:w], e_rows[:, 0, 0:w], soft[:, 6:7], None, ALU.mult))
                v.scalar_tensor_tensor(a_rows[:, 0:w], e_rows[:, 1, 0:w], soft[:, 7:8], a_rows[:, 0:w], ALU.mult, ALU.add
                                       ).then_inc(a_ready, 1)

            def take_rows(h, n, i):
                dve.wait_ge(pv_done, n + 2)
                v.tensor_copy(o_rows[:, i, ds(h * HD, HD)], psum[:, OUT, 0:P]).then_inc(o_free, 1)

            q_rows_of = q_all[:].rearrange("p (h d) n -> p h d n", d=4)

            def queries(b):
                dve.wait_ge(scored, 2 + b * (REVS * RING))
                for a in range(4):
                    for c in range(2):
                        r = slice(QUAD * a, QUAD * (a + 1))
                        last = v.tensor_copy(q_blocks[r, :, 2 * c:2 * c + 2, a * 8 + c * S:a * 8 + (c + 1) * S],
                                             q_rows_of[r, :, 2 * c:2 * c + 2, ds(b * S, S)])
                last.then_inc(q_ready, 1)
                dve.wait_ge(new_scored, b + 1)
                v.tensor_tensor(s_rows[:, NEW0:SC].rearrange("p (o n) -> p o n", o=1), psum[:, MISC, 416:416 + QUAD].rearrange("p (o n) -> p o n", o=1),
                                C("new_mask").rearrange("p (b n) -> p b n", n=QUAD)[:, ds(b, 1), :], ALU.add)

            def turn_keys(b, r, g):
                n = (b * REVS + r) * RING + g
                dve.wait_ge(k_in[g], (b * REVS + r + 1) * (16 * GP))
                dve.wait_ge(scored, n + 1)
                v.transpose(k_turned[:, g % 2].rearrange("p j n -> p (j n)"), k_ring[:, g].rearrange("p j n -> p (j n)")
                            ).then_inc(k_free, 1)

            def softmax(b):
                dve.wait_ge(s_bank_free, 2 + (b + 1) * (REVS * RING))
                v.tensor_reduce(dec[:, 0:1], s_rows[:], AX_X, ALU.max).then_inc(max_ready, 1)
                dve.wait_ge(max_turned, b + 1)
                link(v.tensor_reduce(max_row[0:1, 0, 0:QUAD].rearrange("p (h q) -> p h q", q=8),
                                     psum[0:1, MISC, 0:P].rearrange("p (h a q) -> p h q a", a=4, q=8), AX_X, ALU.max))
                v.tensor_scalar(max_row[0:1, 1, :].rearrange("p (h a q) -> p h a q", a=4, q=8),
                                max_row[0:1, 0, 0:QUAD].rearrange("p (h q) -> p h q", q=8).unsqueeze(2).to_broadcast([1, H, 4, 8]),
                                -1.0, None, ALU.mult).then_inc(max_spread, 1)
                dve.wait_ge(max_back, b + 1)
                v.tensor_copy(dec[:, 1:2], psum[:, MISC, 256:257]).then_inc(negmax_ready, 1)
                dve.wait_ge(p_turned, b + 1)
                for j in range(2, 4):
                    regroup(v.tensor_copy, j)
                v.tensor_copy(p_new[0:QUAD, :].rearrange("p (h q) -> p h q", q=8),
                              psum[0:QUAD, MISC, P:2 * P].rearrange("p (h a q) -> p h a q", a=4, q=8)[:, :, 0, :]).then_inc(p_by_dve, 1)
                link(v.tensor_reduce(dec[:, 12:13], psum[:, MISC, 384:384 + REVS + 1], AX_X, ALU.add))
                link(v.reciprocal(dec[:, 13:14], dec[:, 12:13]))
                link(v.tensor_tensor(dec[:, 14:15], dec[:, 13:14], COEF, ALU.mult))

            def scale_output(b):
                dve.wait_ge(v_free, RING + (b + 1) * (REVS * RING))
                v.tensor_scalar(o_scaled[:], psum[:, 2, 0:P], dec[:, 14:15], None, ALU.mult).then_inc(o_scaled_ready, 1)

            def step(b, h, half, first=False):
                if not first:
                    softmax(b - 1)
                queries(b)
                for r in range(REVS):
                    n, i = b * REVS + r, TILES[half][r]
                    for g in range(RING):
                        turn_keys(b, r, g)
                        if g < 2:
                            maxima(n, i, g)
                        elif g == 2:
                            combine(n, i)
                        else:
                            take_rows(h, n, i)
                if not first:
                    scale_output(b - 1)

            step(0, 0, 0, first=True)
            with linked_loop(H - 1, 2 * (4 + 7 * REVS)) as i:
                step(2 * i + 1, i, 1)
                step(2 * i + 2, i + 1, 0)
            step(B - 1, H - 1, 1)
            softmax(B - 1)
            scale_output(B - 1)
            stage_end(dve, 3)

            rows = o_rows[:].rearrange("p t (h d) -> p (t h) d", d=HD)
            link(v.tensor_tensor(sq_rows[:], o_rows[:], o_rows[:], ALU.mult))
            v.tensor_reduce(stats[:, 0:NT * H], sq_rows[:].rearrange("p t (h d) -> p (t h) d", d=HD), AX_X, ALU.add).then_inc(sq_ready, 1)
            o_t = o_t_all[:].rearrange("p b n -> p (b n)")
            v.tensor_tensor(o_t_sq[:], o_t, o_t, ALU.mult).then_inc(os_sq, 1)
            dve.wait_ge(sq_root, 1)
            link(v.reciprocal(rstd[:, 0:NT * H], rstd[:, 0:NT * H]))
            v.tensor_tensor(rows, rows, rstd[:, 0:NT * H].unsqueeze(2).to_broadcast([P, NT * H, HD]), ALU.mult).then_inc(o_normed, 1)
            dve.wait_ge(y_hi_done, 1)
            v.tensor_tensor(x_lo[:, 0:CC // P, :], y_conv[:], x_hi[:, 0:CC // P, :], ALU.subtract)
            for t in range(NT):
                dve.wait_ge(o_hi_done, t + 1)
                at = slice(t * P, (t + 1) * P)
                for h in range(H):
                    k = CC // P + h
                    last = v.scalar_tensor_tensor(x_lo[:, k, at], psum[:, t % 4, h * P:(h + 1) * P], g_attn[:, 0:1], x_hi[:, k, at],
                                                  ALU.mult, ALU.subtract)
                last.then_inc(o_banks_free, 1)
            dve.wait_ge(os_root, 1)
            link(v.reciprocal(o_t_sq[:], o_t_sq[:]))
            link(v.tensor_tensor(o_t, o_t, o_t_sq[:], ALU.mult))
            v.tensor_scalar(x_t_s[:, CC // P:, :].rearrange("p h (b t) -> p b h t", t=S), o_t_all[:].rearrange("p b (h t) -> p b h t", t=S),
                            g_attn[:, 0:1], None, ALU.mult)
            dve.wait_ge(ys_turned, 1)
            v.tensor_copy(x_t_s[:, 0:CC // P, :].rearrange("p k n -> p (k n)"), psum[:, 5, 0:(CC // P) * QUAD])
            stage_end(dve, 4)

            def residual(x, got, gate, tmp, free, t, j):
                ins = v.tensor_tensor(tmp, got, gate, ALU.mult)
                ins.then_inc(free[0], 1)
                dve.wait_ge(free[0], free[1])
                link(v.scalar_tensor_tensor(x, x, z.ALPHA, tmp, ALU.mult, ALU.add))
                rows = x.shape[0]
                for i in range(x.shape[1] if len(x.shape) == 3 else 1):
                    at = (t + i) * 6 * NB_OUT + 6 * j
                    v.bn_stats(stats[0:rows, ds(at, 6)], x[:, i, :] if len(x.shape) == 3 else x)

            dve.wait_ge(x1_in, 16)
            w_low(MIX0, 0)
            for j in range(NB_OUT):
                n, s = MIX0 + j, j % 2
                if j + 1 < NB_OUT:
                    w_low(n + 1, 1 - s)
                take_quads(n, s)
                cols = slice(j * WB, (j + 1) * WB)
                for t in range(NT):
                    dve.wait_ge(tm_done, (6 + j) * NT + t + 1)
                    residual(x1[:, t, cols], psum[:, t % TB, 0:WB], gate_p[:, 0, cols], row_tmp[:, 0, :],
                             (tm_free, TB + (6 + j) * NT + t + 1), t, j)
                dve.wait_ge(s_folded, n + 1)
                residual(xs_rows[:, cols], psum[0:QUAD, 6 + s, 0:WB], gate_s[:, 0, cols], row_tmp[0:QUAD, 1, :],
                         (s_fold_free, 3 + n), NT, j)

            def moments(count):
                dve.drain().then_inc(moments_in, 1)
                dve.wait_ge(moments_in, count)
                for t in range(NT + 1):
                    rows = P if t < NT else QUAD
                    v.bn_aggr(rstd[0:rows, 2 * t:2 * t + 2], stats[0:rows, 6 * NB_OUT * t:6 * NB_OUT * (t + 1)])
                dve.drain().then_inc(var_ready, 1)
                dve.wait_ge(root_ready, count)
                pairs = rstd[:, 0:2 * NT].rearrange("p (t j) -> p t j", j=2)
                link(v.reciprocal(rstd[:, 32:32 + NT], pairs[:, :, 1]))
                link(v.reciprocal(rstd[0:QUAD, 32 + NT:33 + NT], rstd[0:QUAD, 2 * NT + 1:2 * NT + 2]))
                link(v.scalar_tensor_tensor(rstd[:, 48:48 + NT], pairs[:, :, 0], -1.0, rstd[:, 32:32 + NT], ALU.mult, ALU.mult))
                v.scalar_tensor_tensor(rstd[0:QUAD, 48 + NT:49 + NT], rstd[0:QUAD, 2 * NT:2 * NT + 1], -1.0,
                                       rstd[0:QUAD, 32 + NT:33 + NT], ALU.mult, ALU.mult).then_inc(norm_ready, 1)

            moments(1)
            for c in range(NCH):
                for k in range(KC):
                    split(UNITS + c * KC + k, c, k, x1_mod)
            dve.wait_ge(xs_turned, 2)
            modulate_sample(2, 3)
            stage_end(dve, 5)

            dve.sem_inc(up_free, 2)
            dve.sem_inc(us_taken, 1)
            dve.sem_inc(gs_taken, 1)
            w_low(FF0, 0)

            def gate_up(i, more):
                w_low(FF0 + 1 + 2 * i, 1)
                take_quads(FF0 + 2 * i, 0)
                if more:
                    w_low(FF0 + 2 + 2 * i, 0)
                take_quads(FF0 + 1 + 2 * i, 1)
                for ft in range(FT):
                    dve.wait_ge(fm_done, 6 * FT + 2 * FT * i + (FT + ft + 1))
                    dve.wait_ge(gate_free, FT * i + ft + 1)
                    h = h_out[:, ft, :]
                    v.tensor_tensor(h, psum[:, 2 * ft:2 * ft + NCH, 0:CH].rearrange("p c n -> p (c n)"), h, ALU.mult).then_inc(up_free, 1)
                dve.wait_ge(s_folded, FF0 + 2 + 2 * i)
                dve.wait_ge(gs_taken, i + 2)
                v.tensor_tensor(h_s[:], psum[0:QUAD, 7, 0:WB], gate_act_s[:], ALU.mult).then_inc(us_taken, 1)
                dve.wait_ge(us_taken, i + 2)
                dve.sem_inc(hs_ready, 1)
                dve.wait_ge(hs_turned, i + 1)
                v.tensor_copy(h_t_s[:, ds(FT * i, FT), :], psum[:, 7, WB:WB + FT * QUAD].rearrange("p (f n) -> p f n", n=QUAD))

            with dve.Fori(0, NG - 1) as i:
                gate_up(i, True)
            gate_up(NG - 1, False)
            stage_end(dve, 6)

            dve.sem_inc(d_used, 2)
            dve.sem_inc(d_split, 2)
            dve.sem_inc(down_free, DB)
            N0 = FF0 + 2 * NG
            with linked_loop(D // WB, DB + 1) as nb:
                for k in range(NF):
                    s = k % 3
                    dve.wait_ge(d_hi_done, nb * NF + (k + 1))
                    v.tensor_tensor(h_lo[:, s, :], h_all[:, k, :], h_hi[:, s, :], ALU.subtract)
                    v.tensor_tensor(d_lo[:, s, :], d_raw[:, (k // 2) % 4, k % 2, :], d_hi[:, s, :], ALU.subtract).then_inc(d_split, 1)
                dve.wait_ge(d_used, 2 + (nb + 1) * NF)
                cols = ds(nb * WB, WB)
                for j in range(DB):
                    got = psum[:, j, 0:2 * WB].rearrange("p (t n) -> p t n", n=WB)
                    gate = gate_p[:, 1, cols].unsqueeze(1).to_broadcast([P, 2, WB])
                    residual(x1[:, 2 * j:2 * j + 2, cols], got, gate, down_tmp[:], (down_free, nb * DB + (DB + j + 1)), 2 * j, nb)
                v.tensor_copy(s_quads[:, 0, :], psum[:, 4, 0:WB]).then_inc(s_quads_free, 1)
                dve.wait_ge(s_folded, N0 + nb + 1)
                residual(xs_rows[:, cols], psum[0:QUAD, 5, 0:WB], gate_s[:, 1, cols], down_tmp[0:QUAD, 0, :],
                         (s_fold_free, NB_IN + NB_OUT + 3 + nb), NT, nb)
            moments(2)
            dve.wait_ge(ln_in, 64)
            for t in range(NT + 1):
                rows = P if t < NT else QUAD
                x = x1[:, t, :] if t < NT else xs_rows[:]
                dve.wait_ge(x1_ready, NT + 1 + t + 1)
                link(v.tensor_tensor(x, x, ln2_rows[0:rows, 0, :], ALU.mult))
                v.tensor_tensor(x, x, ln2_rows[0:rows, 1, :], ALU.add).then_inc(y_ready, 1)


_NAMES = ["x_prompt", "x_sample", "c_prompt", "c_sample", "cache_k", "cache_v", "state_conv", "page_table",
          "w_ada", "b_ada", "w_in", "conv_w", "lambda_q1", "lambda_k1", "lambda_q2", "lambda_k2", "subln_g",
          "w_out", "ln1_g", "ln1_b", "w_gate", "w_up", "w_down", "ln2_g", "ln2_b"]


def kernel(**inputs):
    import concourse.bacc as bacc
    from concourse.bass_utils import run_bass_kernel_spmd

    nc = bacc.Bacc("TRN2", target_bir_lowering=False, num_devices=1)
    arrays = {n: np.ascontiguousarray(inputs[n]) for n in _NAMES}
    z = Shapes({n: a.shape for n, a in arrays.items()})
    arrays["consts"], const_at = constants(z)
    io = {n: nc.dram_tensor(n, a.shape, mybir.dt.from_np(a.dtype), kind="ExternalInput").ap() for n, a in arrays.items()}
    outs = [("y_prompt", (1, z.T, z.D)), ("y_sample", (z.B, z.S, z.D)),
            ("new_k_prompt", (1, 1, z.T, z.H, z.HD)), ("new_v_prompt", (1, 1, z.T, z.H, z.HD)),
            ("new_conv_prompt", (1, 1, 2, z.CC)),
            ("new_k_sample", (1, z.B, z.S, z.H, z.HD)), ("new_v_sample", (1, z.B, z.S, z.H, z.HD)),
            ("new_conv_sample", (1, z.B, 2, z.CC))]
    for n, shape in outs:
        io[n] = nc.dram_tensor(n, shape, F32, kind="ExternalOutput").ap()
    build(nc, z, io, const_at, arrays["consts"].shape[1])
    r = run_bass_kernel_spmd(nc, [arrays], core_ids=[0])
    return tuple(r.results[0][n] for n, _ in outs)
```

```python
import math
from contextlib import ExitStack, contextmanager

import numpy as np

import concourse.bass as bass
from concourse import mybir

F32 = mybir.dt.float32
F32R = mybir.dt.float32r
I32 = mybir.dt.int32
ALU = mybir.AluOpType
ACT = mybir.ActivationFunctionType
AX_X = mybir.AxisListType.X
ds = bass.ds

P = 128
QUAD = 32
BANK = 512
ROPE_THETA = 500000.0
LN_EPS = 1e-5
MASKED = -1.0e30


class Shapes:

    def __init__(self, s):
        self.T, self.D = s["x_prompt"][1:]
        self.B, self.S = s["x_sample"][:2]
        self.DEPTH, self.POOL, self.PAGE, self.H, self.HD = s["cache_k"]
        self.PAGES = s["page_table"][1]
        self.F = s["w_gate"][2]
        self.IN = s["w_in"][2]
        self.CC = s["conv_w"][2]
        self.MODS = s["w_ada"][2] // self.D
        self.BS = self.B * self.S
        self.KC = self.D // P
        self.NT = self.T // P
        self.CH = min(BANK, self.T)
        self.NCH = self.T // self.CH
        self.NF = self.F // P
        self.AW = self.H * self.HD
        self.ALPHA = (2.0 * self.DEPTH) ** 0.25
        assert self.DEPTH == 1 and self.PAGE == P and self.HD == P and self.H == 4
        assert self.BS == QUAD and self.KC % 4 == 0 and self.T % (2 * P) == 0 and self.F % 256 == 0
        assert self.PAGES % 16 == 0 and self.CC == self.AW == 512 and self.B == 8 and self.S == 4


def constants(z):
    p = np.arange(P)
    out = {}
    out["ident"] = np.eye(P)
    out["quad_fold"] = (p[:, None] % QUAD == np.arange(QUAD)[None, :])
    h, q = p // QUAD, p % 8
    out["head_fold"] = (h[:, None] == h[None, :]) & (q[:, None] == q[None, :])
    out["causal"] = np.where(p[None, :] <= p[:, None], 0.0, MASKED)
    a, t = (p // 8) % 4, p % z.S
    bb, tt = np.arange(QUAD) // z.S, np.arange(QUAD) % z.S
    ok = (a[:, None, None] == 0) & (np.arange(z.B)[None, :, None] == bb[None, None, :]) & (
        tt[None, None, :] <= t[:, None, None])
    out["new_mask"] = np.where(ok, 0.0, MASKED).reshape(P, -1)
    ht = np.arange(z.H * z.S)
    out["own_head"] = (h[:, None] == ht[None, :] // z.S) & (((p // 8) % 4) == h)[:, None] & (
        t[:, None] == ht[None, :] % z.S)
    out["comp0"] = (q < z.S)[:, None]
    out["comp1"] = (q >= z.S)[:, None]
    out["mean"] = np.full((P, P), 1.0 / P)
    out["pick_prompt"] = np.repeat((p % QUAD == 0)[:, None], P, axis=1)
    out["pick_sample"] = (p[:, None] % QUAD == 1 + np.arange(QUAD)[None, :] // z.S)
    rot = z.HD // 2 // 4
    inv = (np.float32(ROPE_THETA) ** (-np.arange(0, rot, 2, dtype=np.float32) / np.float32(rot))).astype(np.float32)
    pos = np.arange(z.T, dtype=np.float32).reshape(z.NT, P).T
    ang = (pos[:, :, None] * inv).astype(np.float32)
    out["cos_p"], out["sin_p"] = np.cos(ang).reshape(P, -1), np.sin(ang).reshape(P, -1)
    pos = (z.PAGES * z.PAGE + p % z.S).astype(np.float32)
    ang = (pos[:, None] * inv).astype(np.float32)
    out["cos_s"], out["sin_s"] = np.cos(ang), np.sin(ang)
    where, n = {}, 0
    for k, v in out.items():
        where[k] = (n, n + v.shape[1])
        n += v.shape[1]
    return np.ascontiguousarray(np.concatenate([np.asarray(v, np.float32) for v in out.values()], axis=1)), where


def build(nc, z, io, const_at, n_const):
    T, D, B, S, H, HD, F = z.T, z.D, z.B, z.S, z.H, z.HD, z.F
    KC, NT, CH, NCH, NF, BS, AW, CC = z.KC, z.NT, z.CH, z.NCH, z.NF, z.BS, z.AW, z.CC
    QK = HD // 2
    SCORE_SCALE = QK ** -0.5
    WB = 256
    FT = WB // P
    GP, RING = 4, 4
    REVS = z.PAGES // (GP * RING)
    NEW0 = z.PAGES * QUAD
    SC = NEW0 + QUAD
    assert z.MODS * D // BANK == 2 * z.MODS
    NG = F // WB
    NB_IN, NB_OUT = z.IN // WB, D // WB
    lam_init = 0.8 - 0.6 * math.exp(-0.3 * 0)

    with ExitStack() as ctx:
        base = [16512]

        def place(name, shape, dt, at):
            return nc.alloc_sbuf_tensor_at(name, shape, dt, offset=at)

        def keep(name, shape, dt=F32):
            n = int(np.prod(shape[1:])) * 4
            at = base[0]
            base[0] += -(-n // 32) * 32
            return place(name, shape, dt, at)

        class Area:

            def __init__(self, at):
                self.at = at

            def __call__(self, name, shape, dt=F32):
                n = int(np.prod(shape[1:])) * 4
                t = place(name, shape, dt, self.at)
                self.at += -(-n // 32) * 32
                return t

        psum = ctx.enter_context(nc.psum_tensor("psum", [P, 8, BANK], F32))

        def sem(name):
            return ctx.enter_context(nc.semaphore(name))

        consts_at = base[0]
        consts = keep("consts", [P, n_const])
        C = lambda name: consts[:, const_at[name][0]:const_at[name][1]]
        ident = C("ident")
        o_stats_at = -(-(consts_at + 4 * const_at["pick_prompt"][0]) // 32) * 32
        o_stats = place("o_stats", [P, NT * H * 6], F32, o_stats_at)
        o_moments = place("o_moments", [P, NT * H, 2], F32, o_stats_at + 24 * NT * H)
        assert o_stats_at + 32 * NT * H <= consts_at + 4 * n_const
        mod_t = keep("mod_t", [P, 4, KC, QUAD])
        gate_p_at = base[0]
        gate_p = keep("gate_p", [P, 2, D])
        gate_s = keep("gate_s", [QUAD, 2, D])
        lam_rows_at = base[0]
        lam_rows = keep("lam_rows", [P, 4, QK])
        small = keep("small", [P, 16])
        NEG_LAM, COEF = small[:, 6:7], small[:, 8:9]
        ln1_t = keep("ln1_t", [P, 2, KC])
        eps_col = keep("eps_col", [P, 1])
        g_attn = keep("g_attn", [P, 1])
        conv_w_t = keep("conv_w_t", [P, 3, CC // P])
        queries_at = base[0]
        q_all = keep("q_all", [P, 4 * H, BS])
        q_blocks = keep("q_blocks", [P, H, 4, QUAD])
        k_new_t = keep("k_new_t", [P, AW])
        v_new = keep("v_new", [P, AW])
        queries_end = base[0]
        o_t_all = keep("o_t_all", [P, B, H * S])
        xs_rows = keep("xs_rows", [QUAD, D])
        y_conv_at = base[0]
        y_conv = keep("y_conv", [P, CC // P, T])
        base[0] = max(base[0], y_conv_at + 16 * D, y_conv_at + 8 * FT * T)
        y_s_at = base[0]
        y_s = keep("y_s", [QUAD, CC])
        stage0 = base[0]

        ar = Area(stage0)
        c_rows = ar("c_rows", [16, D])
        silu_t = ar("silu_t", [P, KC, QUAD])
        ada_w = ar("ada_w", [P, 2, KC, BANK])
        ada_bias = ar("ada_bias", [P, z.MODS * D])
        ada_out = ar("ada_out", [P, z.MODS * D])
        ada_end = ar.at

        ar = Area(stage0)
        x_hi = ar("x_hi", [P, KC, T], F32R)
        x_lo = ar("x_lo", [P, KC, T], F32R)
        w_hi = ar("w_hi", [P, 2, KC, WB], F32R)
        w_lo = ar("w_lo", [P, 2, KC, WB], F32R)
        ar.at = max(ar.at, ada_end)
        w_raw = ar("w_raw", [P, 2, KC, WB])
        x_t_s = ar("x_t_s", [P, KC, QUAD])
        s_quads = ar("s_quads", [P, 2, WB])
        dense_end = max(ar.at, stage0 + 4 * ((2 * RING + 2) * GP * AW + B * z.PAGES + NT * AW + SC + 2 * T + P + 64))
        ar.at = dense_end
        u_conv = ar("u_conv", [P, CC // P, T + 2])
        ar.at = max(ar.at, dense_end + 8 * NT * WB, dense_end + 8192 + 4 * CC)
        x_rows = place("x_rows", [P, NT, D], F32, dense_end)
        x_mod = place("x_mod", [P, 2, CH], F32, dense_end + 4 * NT * D)
        z_s = ar("z_s", [QUAD, z.IN])
        z_rows = place("z_rows", [P, 2, NT, WB], F32, dense_end)
        rope_p = ar("rope_p", [P, 4, NT * 32])
        rope_s = ar("rope_s", [QUAD, 4, 4 * H * 8])
        q_wide = place("q_wide", [QUAD, 4 * H, 4, QUAD], F32, dense_end)
        u_s = place("u_s", [QUAD, CC], F32, dense_end + 8192)

        ar = Area(stage0)
        k_ring = ar("k_ring", [P, RING, GP, AW])
        v_ring = ar("v_ring", [P, RING, GP, AW])
        k_turned = place("k_turned", [P, 2, GP, AW], F32, ar.at)
        conv_s = ar("conv_s", [QUAD, 7, CC])
        ar.at += 2 * GP * AW * 4 - 7 * CC * 4
        page_row = ar("page_row", [1, B * z.PAGES], mybir.dt.int32)
        v_rows = ar("v_rows", [P, NT, AW])
        e_rows = ar("e_rows", [P, 2, T])
        s_rows = ar("s_rows", [P, SC])
        soft = ar("soft", [P, 8])
        dec = ar("dec", [P, 16])
        p_new = ar("p_new", [P, QUAD])
        o_scaled = ar("o_scaled", [P, P])
        assert ar.at <= dense_end
        ar = Area(dense_end)
        o_rows = ar("o_rows", [P, NT, AW])
        q_zero = ar("q_zero", [P, 2, T])
        k_t = ar("k_t", [P, T])
        a_rows = ar("a_rows", [P, T])
        a_t = ar("a_t", [P, T])
        ar = Area(y_conv_at)
        k_rows = ar("k_rows", [P, NT, HD])
        q_rows = ar("q_rows", [P, NT, HD])
        p_t = ar("p_t", [P, z.PAGES, QUAD])
        max_row = place("max_row", [1, 2, P], F32, lam_rows_at)

        ar = Area(dense_end)
        x1 = ar("x1", [P, NT, D])
        stats = ar("stats", [P, max(NT * H, (NT + 1) * NB_OUT * 6)])
        rstd = ar("rstd", [P, 64])
        gate_act_s = place("gate_act_s", [QUAD, WB], F32, y_s_at)
        h_s = place("h_s", [QUAD, WB], F32, y_s_at + 4 * WB)
        h_t_s_at = ar.at
        h_t_s = ar("h_t_s", [P, NF, QUAD])
        on_y_conv = y_conv_at
        h_out = place("h_out", [P, FT, T], F32, on_y_conv)
        x1_mod = place("x1_mod", [P, 2, CH], F32, on_y_conv)
        row_tmp = place("row_tmp", [P, 2, WB], F32, on_y_conv + 8 * CH)
        ln_rows = place("ln_rows", [P, 2, D], F32, on_y_conv + 8 * D)

        ar = Area(stage0)
        h_all = ar("h_all", [P, NF, T])
        h_hi = ar("h_hi", [P, 4, T], F32R)
        d_raw = ar("d_raw", [P, 4, 2, WB])
        assert ar.at <= dense_end
        h_lo = place("h_lo", [P, 4, T], F32R, on_y_conv)
        down_tmp = place("down_tmp", [P, 2, WB], F32, y_s_at)
        ar = Area(queries_at)
        d_hi = ar("d_hi", [P, 4, WB], F32R)
        d_lo = ar("d_lo", [P, 4, WB], F32R)
        assert ar.at <= queries_end
        down_quads = place("down_quads", [P, D], F32, gate_p_at)
        ln2_rows = place("ln2_rows", [P, 2, D], F32, stage0)
        o_t_sq = place("o_t_sq", [P, B * H * S], F32, h_t_s_at)

        q_store = nc.dram_tensor("q_store", (T, AW), F32, kind="Internal").ap()
        y_conv_store = nc.dram_tensor("y_conv_store", (CC, T), F32, kind="Internal").ap()
        u_ext = nc.dram_tensor("u_ext", (B, S + 2, CC), F32, kind="Internal").ap()
        h_store = nc.dram_tensor("h_store", (F, T), F32, kind="Internal").ap()
        k_out = io["new_k_prompt"].rearrange("l b t h d -> (l b t) (h d)")
        v_out = io["new_v_prompt"].rearrange("l b t h d -> (l b t) (h d)")
        k_pages = io["cache_k"].rearrange("l n p h d -> (l n) p (h d)")
        v_pages = io["cache_v"].rearrange("l n p h d -> (l n) p (h d)")
        x_dram = io["x_prompt"].rearrange("b t d -> (b t) d")
        y_dram = io["y_prompt"].rearrange("b t d -> (b t) d")
        xs_dram = io["x_sample"].rearrange("b t d -> (b t) d")
        ys_dram = io["y_sample"].rearrange("b t d -> (b t) d")
        by_rows = lambda w: w[0].rearrange("(k p) n -> p k n", p=P)
        w_ada, w_in, w_out = by_rows(io["w_ada"]), by_rows(io["w_in"]), by_rows(io["w_out"])
        w_gate, w_up, w_down = by_rows(io["w_gate"]), by_rows(io["w_up"]), by_rows(io["w_down"])
        row_of = lambda name: io[name].rearrange("l d -> (l d)")

        stage_done = sem("stage_done")
        dve_step = sem("dve_step")
        consts_in, c_in, vectors_in, bias_in = sem("consts_in"), sem("c_in"), sem("vectors_in"), sem("bias_in")
        bias_zeroed, silu_zeroed, c_turned, silu_ready = (
            sem("bias_zeroed"), sem("silu_zeroed"), sem("c_turned"), sem("silu_ready"))
        ada_in = [sem("ada_in0"), sem("ada_in1")]
        ada_done, ada_banks_free = sem("ada_done"), sem("ada_banks_free")
        mod_done, mod_kept, gates_done, gates_kept = (
            sem("mod_done"), sem("mod_kept"), sem("gates_done"), sem("gates_kept"))
        lam_sums, lam_exps = sem("lam_sums"), sem("lam_exps")
        xs_in, x_in = sem("xs_in"), [sem(f"x_in{c}") for c in range(NCH)]
        x_turned, x_banks_free, x_hi_done, x_split = sem("x_turned"), sem("x_banks_free"), sem("x_hi_done"), sem("x_split")
        xs_turned, xs_ready = sem("xs_turned"), sem("xs_ready")
        w_in_sem = [sem("w_landed0"), sem("w_landed1")]
        w_hi_done, w_lo_done = sem("w_hi_done"), sem("w_lo_done")
        s_done, s_quads_free, s_folded, s_fold_free = (
            sem("s_done"), sem("s_quads_free"), sem("s_folded"), sem("s_fold_free"))
        fm_done, fm_free, tm_done, tm_free = sem("fm_done"), sem("fm_free"), sem("tm_done"), sem("tm_free")
        conv_ready, conv_stored, roped, z_stored = (
            sem("conv_ready"), sem("conv_stored"), sem("roped"), [sem("z_stored0"), sem("z_stored1")])
        s_conv_ready, s_roped, s_stored, u_ext_in = (
            sem("s_conv_ready"), sem("s_roped"), sem("s_stored"), sem("u_ext_in"))
        q_wide_ready, q_all_done, q_all_kept = sem("q_wide_ready"), sem("q_all_done"), sem("q_all_kept")
        conv_s_in, v_in_rows, qk_in = sem("conv_s_in"), sem("v_in_rows"), sem("qk_in")
        y_conv_kept, y_conv_in, k_rows_turned, k_t_ready = (
            sem("y_conv_kept"), sem("y_conv_in"), sem("k_rows_turned"), sem("k_t_ready"))
        q_zeroed, rows_turned, head_ready = sem("q_zeroed"), sem("rows_turned"), sem("head_ready")
        scores_done, neg_max, score_banks_free = sem("scores_done"), sem("neg_max"), sem("score_banks_free")
        a_ready, a_turned, a_t_ready = sem("a_ready"), sem("a_turned"), sem("a_t_ready")
        pv_done, o_free = sem("pv_done"), sem("o_free")
        k_in = [sem(f"k_in{g}") for g in range(RING)]
        v_in = [sem(f"v_in{g}") for g in range(RING)]
        pages_in = sem("pages_in")
        k_free, v_free, scored, s_bank_free = sem("k_free"), sem("v_free"), sem("scored"), sem("s_bank_free")
        q_ready, new_scored, max_ready, max_turned = (
            sem("q_ready"), sem("new_scored"), sem("max_ready"), sem("max_turned"))
        max_spread, max_back, negmax_ready, exp_done = (
            sem("max_spread"), sem("max_back"), sem("negmax_ready"), sem("exp_done"))
        p_turned, p_by_act, p_by_dve = sem("p_turned"), sem("p_by_act"), sem("p_by_dve")
        o_scaled_ready, o_t_done, o_t_kept = (
            sem("o_scaled_ready"), sem("o_t_done"), sem("o_t_kept"))
        sq_ready, sq_root, o_normed, o_turned, o_hi_done, o_banks_free = (
            sem("sq_ready"), sem("sq_root"), sem("o_normed"), sem("o_turned"), sem("o_hi_done"), sem("o_banks_free"))
        ys_ready, o_aggregated = sem("ys_ready"), sem("o_aggregated")
        os_sq, os_mean, os_root, ys_turned = sem("os_sq"), sem("os_mean"), sem("os_root"), sem("ys_turned")
        y_hi_done = sem("y_hi_done")
        x1_in, ln_in, var_ready, root_ready, norm_ready, x1_ready, x1_scaled, moments_in, x1_odd_ready, xs_normed = (
            sem("x1_in"), sem("ln_in"), sem("var_ready"), sem("root_ready"), sem("norm_ready"), sem("x1_ready"),
            sem("x1_scaled"), sem("moments_in"), sem("x1_odd_ready"), sem("xs_normed"))
        gate_free, up_free, gs_taken, hs_ready, hs_turned, us_taken = (
            sem("gate_free"), sem("up_free"), sem("gs_taken"), sem("hs_ready"), sem("hs_turned"), sem("us_taken"))
        h_stored, x1_times_g = sem("h_stored"), sem("x1_times_g")
        h_in = [sem(f"h_in{j}") for j in range(NF // 2)]
        d_in = [sem(f"d_in{j}") for j in range(4)]
        d_hi_done, d_split, d_used, down_done, down_free = (
            sem("d_hi_done"), sem("d_split"), sem("d_used"), sem("down_done"), sem("down_free"))
        down_quads_in, down_folded, down_s_free = sem("down_quads_in"), sem("down_folded"), sem("down_s_free")
        y_ready, y_stored = sem("y_ready"), sem("y_stored")

        TILES = ([i for i in range(NT) if i % 4 in (0, 3)], [i for i in range(NT) if i % 4 in (1, 2)])
        assert 2 * H == B and NT == 2 * REVS and RING == 4 and REVS <= 4
        MISC, ROWS, OUT = 4, 5, 7
        down_bank = lambda par, pair: 0 if pair == DB - 1 else (1, 5)[par] + pair
        TPC = CH // P
        UNITS = NCH * KC
        PAIRS = NF // 2
        TB = min(4, NT)
        DB = NT // 2
        MIX0, FF0 = NB_IN, NB_IN + NB_OUT

        PART_ORDER = (0, 1, 3, 4, 2, 5)
        cols_of = "cchhbb"
        in_cols = [2 * CC, 2 * CC + WB, 0, WB, CC, CC + WB] + [3 * CC + WB * j for j in range(6)]

        def stage_end(eng, n):
            eng.drain().then_inc(stage_done, 1)
            eng.wait_ge(stage_done, 4 * n)

        def chain(eng, steps):
            count = [0, 0]

            def link(ins):
                count[1] += 1
                ins.then_inc(steps, 1)
                eng.wait_ge(steps, count[0] + count[1])

            @contextmanager
            def loop(turns, links):
                first = count[0] + count[1]
                with eng.Fori(0, turns) as i:
                    count[0], count[1] = first + i * links, 0
                    yield i
                    assert count[1] == links, (count[1], links)
                count[0], count[1] = first + turns * links, 0

            return link, loop

        def regroup(copy, j):
            got = psum[QUAD * j:QUAD * (j + 1), 0:REVS, :].rearrange("p r n -> p (r n)").rearrange(
                "p (g h a q) -> p g h a q", h=H, a=4, q=8)
            to = p_t[:].rearrange("p (g j) (h q) -> p g j h q", j=4, q=8)
            for a in range(4):
                last = copy(to[QUAD * a:QUAD * (a + 1), :, j], got[:, :, :, a, :])
            return last

        def rope(x1_, x2_, cos, sin, tmp, link, done):
            v = nc.vector
            v.tensor_tensor(tmp[0], x1_, cos, ALU.mult)
            v.tensor_tensor(tmp[1], x2_, sin, ALU.mult)
            v.tensor_tensor(tmp[2], x2_, cos, ALU.mult)
            link(v.tensor_tensor(tmp[3], x1_, sin, ALU.mult))
            v.tensor_tensor(x1_, tmp[0], tmp[1], ALU.subtract)
            v.tensor_tensor(x2_, tmp[2], tmp[3], ALU.add).then_inc(done, 1)

        block = ctx.enter_context(nc.Block())

        def load_pages(eng, par):
            def group(pages, ring, landed, free, b, r, g):
                for j in range(GP):
                    page = eng.value_load(page_row[0:1, ds((b * REVS + r) * (RING * GP) + (g * GP + j), 1)],
                                          min_val=0, max_val=z.POOL - 1)
                    if j == 0:
                        eng.wait_ge(free, (b * REVS + r) * RING + g + 1)
                    eng.dma_start(ring[:, g, j, :], pages[ds(page, 1)].rearrange("o p d -> p (o d)")
                                  ).then_inc(landed[g], 16)

            keys, values = (k_pages, k_ring, k_in, k_free), (v_pages, v_ring, v_in, v_free)
            with eng.Fori(0, REVS) as r:
                for g in range(par, RING, 2):
                    group(*keys, 0, r, g)
            with eng.Fori(0, B - 1) as b:
                with eng.Fori(0, REVS) as r:
                    for g in range(par, RING, 2):
                        group(*keys, b + 1, r, g)
                        group(*values, b, r, g)
            with eng.Fori(0, REVS) as r:
                for g in range(par, RING, 2):
                    group(*values, B - 1, r, g)

        def fetch_head(eng, h):
            for rows, src in ((k_rows, k_out), (q_rows, q_store)):
                eng.dma_start(rows[:], src[:, ds(h * HD, HD)].rearrange("(t p) n -> p t n", p=P)).then_inc(qk_in, 16)

        @block.sync
        def _(sp):
            sp.dma_start(consts[:], io["consts"]).then_inc(consts_in, 16)
            sp.dma_start(c_rows[0:1, :], io["c_prompt"]).then_inc(c_in, 16)
            sp.dma_start(c_rows[1:1 + B, :], io["c_sample"]).then_inc(c_in, 16)

            def load_ada(s, n):
                sp.dma_start(ada_w[:, s], w_ada[:, :, ds(n * BANK, BANK)]).then_inc(ada_in[s], 16)

            load_ada(0, 2 * PART_ORDER[0])
            load_ada(1, 2 * PART_ORDER[0] + 1)
            for j, name in enumerate(("lambda_q1", "lambda_k1", "lambda_q2", "lambda_k2")):
                sp.dma_start(lam_rows[:, j, :], row_of(name).partition_broadcast(P)).then_inc(vectors_in, 16)
            with nc.allow_non_contiguous_dma(reason="a few vectors by feature"):
                sp.dma_start(g_attn[:], io["subln_g"].rearrange("l d -> d l")).then_inc(vectors_in, 16)
                for j, name in enumerate(("ln1_g", "ln1_b")):
                    sp.dma_start(ln1_t[:, j, :], row_of(name).rearrange("(k p) -> p k", p=P)).then_inc(vectors_in, 16)
                for j in range(3):
                    sp.dma_start(conv_w_t[:, j, :], io["conv_w"][0, j].rearrange("(f p) -> p f", p=P)).then_inc(vectors_in, 16)
            sp.wait_ge(bias_zeroed, 1)
            sp.dma_start(ada_bias[0:QUAD, :], row_of("b_ada").partition_broadcast(QUAD)).then_inc(bias_in, 16)
            for i in range(1, z.MODS):
                for s in range(2):
                    sp.wait_ge(ada_done, 2 * i + s - 1)
                    load_ada(s, 2 * PART_ORDER[i] + s)

            def load_w(n, w, col):
                if not isinstance(n, int) or n >= 2:
                    sp.wait_ge(s_folded, n - 1)
                s = n % 2
                sp.dma_start(w_raw[:, s], w[:, :, ds(col, WB)]).then_inc(w_in_sem[s], 16)

            for c in range(NCH):
                sp.dma_start(x_rows[:, c * TPC:(c + 1) * TPC, :], x_dram[c * CH:(c + 1) * CH, :].rearrange("(t p) d -> p t d", p=P)
                             ).then_inc(x_in[c], 16)
            sp.dma_start(xs_rows[:], xs_dram).then_inc(xs_in, 16)
            for n in range(2):
                load_w(n, w_in, in_cols[n])
            stage_end(sp, 1)

            def store_z(m):
                if m < 4:
                    sp.wait_ge(roped, m + 1)
                else:
                    sp.wait_ge(tm_free, TB + NT * (m + 1))
                to = (q_store, k_out, v_out)[m // 2]
                sp.dma_start(to[:, (m % 2) * WB:(m % 2 + 1) * WB].rearrange("(t p) n -> p t n", p=P),
                             z_rows[:, m % 2]).then_inc(z_stored[m % 2], 16)

            for n in range(2, NB_IN):
                load_w(n, w_in, in_cols[n])
                if n == 6:
                    sp.wait_ge(conv_ready, 1)
                    with nc.allow_non_contiguous_dma(reason="two tokens' rows by feature"):
                        for f in range(CC // P):
                            sp.dma_start(io["new_conv_prompt"][0, 0][:, f * P:(f + 1) * P].rearrange("j p -> p j"),
                                         u_conv[:, f, T:T + 2]).then_inc(conv_stored, 16)
                if n - 2 >= 6:
                    store_z(n - 8)
            sp.wait_ge(fm_free, 2 + 6 * FT)
            sp.dma_start(y_conv_store.rearrange("(f p) t -> p f t", p=P), y_conv[:]).then_inc(y_conv_kept, 16)
            store_z(4)
            store_z(5)
            sp.wait_ge(s_conv_ready, 1)
            sp.dma_start(u_ext[:, 2:2 + S, :].rearrange("b t c -> b t c"), u_s[:]).then_inc(u_ext_in, 16)
            sp.dma_start(u_ext[:, 0:2, :], io["state_conv"][0]).then_inc(u_ext_in, 16)
            sp.wait_ge(s_roped, 1)
            sp.dma_start(io["new_k_sample"].rearrange("l b t h d -> (l b t) (h d)"), z_s[:, 3 * CC + AW:3 * CC + 2 * AW]).then_inc(s_stored, 16)
            sp.dma_start(io["new_v_sample"].rearrange("l b t h d -> (l b t) (h d)"), z_s[:, 3 * CC + 2 * AW:]).then_inc(s_stored, 16)
            sp.wait_ge(u_ext_in, 32)
            sp.dma_start(io["new_conv_sample"][0], u_ext[:, S:S + 2, :]).then_inc(s_stored, 16)
            sp.wait_ge(s_stored, 48)
            sp.wait_ge(conv_stored, 16 * (CC // P))
            for s in range(2):
                sp.wait_ge(z_stored[s], 48)
            sp.wait_ge(y_conv_kept, 16)
            stage_end(sp, 2)

            for j in range(3):
                sp.dma_start(conv_s[:, j, :], u_ext[:, j:j + S, :]).then_inc(conv_s_in, 16)
            for j in range(3):
                sp.dma_start(conv_s[:, 4 + j, :], io["conv_w"][0, j].partition_broadcast(QUAD)).then_inc(conv_s_in, 16)
            sp.dma_start(page_row[:], io["page_table"].rearrange("b n -> (b n)").rearrange("(o n) -> o n", o=1)).then_inc(pages_in, 16)
            sp.wait_ge(pages_in, 16)
            load_pages(sp, 0)
            stage_end(sp, 3)
            sp.dma_start(y_conv[:], y_conv_store.rearrange("(f p) t -> p f t", p=P)).then_inc(y_conv_in, 16)
            for j in range(2):
                load_w(MIX0 + j, w_out, j * WB)

            sp.wait_ge(o_turned, NT)
            sp.dma_start(x1[:], x_dram.rearrange("(t p) d -> p t d", p=P)).then_inc(x1_in, 16)
            sp.wait_ge(o_banks_free, 1)
            for j, name in enumerate(("ln1_g", "ln1_b")):
                sp.dma_start(ln_rows[:, j, :], row_of(name).partition_broadcast(P)).then_inc(ln_in, 16)
            for j in range(2, NB_OUT):
                load_w(MIX0 + j, w_out, j * WB)

            def load_ff(i, which):
                sp.wait_ge(s_folded, FF0 - 1 + which + 2 * i)
                sp.dma_start(w_raw[:, which], (w_gate, w_up)[which][:, :, ds(i * WB, WB)]).then_inc(w_in_sem[which], 16)

            sp.sem_inc(h_stored, 16)
            load_ff(0, 0)
            load_ff(0, 1)

            def store_h(i):
                sp.wait_ge(up_free, 2 + FT + i * FT)
                sp.dma_start(h_store[ds(i * WB, WB), :].rearrange("(f p) t -> p f t", p=P), h_out[:]).then_inc(h_stored, 16)

            with sp.Fori(0, NG - 1) as i:
                load_ff(i + 1, 0)
                load_ff(i + 1, 1)
                store_h(i)
            store_h(NG - 1)
            sp.wait_ge(h_stored, 16 * (NG + 1))
            sp.wait_ge(x1_scaled, NT + 1)
            stage_end(sp, 4)

            def load_d(nb, pp):
                if pp >= 4:
                    sp.wait_ge(d_used, nb * NF + 4 + 2 * (pp - 3))
                elif not isinstance(nb, int):
                    before = max(p for p in range(PAIRS) if p % 4 == pp)
                    sp.wait_ge(d_used, nb * NF - NF + 4 + 2 * (before + 1))
                sp.dma_start(d_raw[:, pp % 4], w_down[:, 2 * pp:2 * pp + 2, ds(nb * WB, WB)]).then_inc(d_in[pp % 4], 16)

            h_view = h_store.rearrange("(k p) t -> p k t", p=P)
            for pp in range(PAIRS):
                sp.dma_start(h_all[:, 2 * pp:2 * pp + 2, :], h_view[:, 2 * pp:2 * pp + 2, :]).then_inc(h_in[pp], 16)
                load_d(0, pp)
            with sp.Fori(1, D // WB) as nb:
                for pp in range(PAIRS):
                    load_d(nb, pp)
            sp.wait_ge(d_used, 4 + (D // WB) * NF)
            for j, name in enumerate(("ln2_g", "ln2_b")):
                sp.dma_start(ln2_rows[:, j, :], row_of(name).partition_broadcast(P)).then_inc(ln_in, 16)
            for t in range(NT):
                sp.wait_ge(y_ready, t + 1)
                sp.dma_start(y_dram[t * P:(t + 1) * P, :], x1[:, t, :]).then_inc(y_stored, 16)
            sp.wait_ge(y_ready, NT + 1)
            sp.dma_start(ys_dram, xs_rows[:]).then_inc(y_stored, 16)
            sp.wait_ge(y_stored, 16 * (NT + 1))

        @block.gpsimd
        def _(pool):
            pool.wait_ge(stage_done, 8)
            pool.dma_start(v_rows[:], v_out.rearrange("(t p) n -> p t n", p=P)).then_inc(v_in_rows, 16)
            pool.wait_ge(pages_in, 16)
            load_pages(pool, 1)

            pool.wait_ge(xs_turned, 2)
            pool.wait_ge(ln_in, 32)
            for t in range(NT + 1):
                x, g, b = ((x1[:, t, :], ln_rows[:, 0, :], ln_rows[:, 1, :]) if t < NT
                           else (xs_rows[:], ln_rows[0:QUAD, 0, :], ln_rows[0:QUAD, 1, :]))
                nc.gpsimd.tensor_tensor(x, x, g, ALU.mult).then_inc(x1_times_g, 1)
                pool.wait_ge(x1_times_g, t + 1)
                nc.gpsimd.tensor_tensor(x, x, b, ALU.add).then_inc(x1_scaled, 1)

        @block.tensor
        def _(pe):
            mm, turn = nc.tensor.matmul, nc.tensor.transpose

            pe.wait_ge(consts_in, 16)
            pe.wait_ge(c_in, 32)
            for k in range(KC):
                last = turn(psum[:, 0, 16 * k:16 * k + 1 + B], c_rows[0:1 + B, k * P:(k + 1) * P], ident[0:1 + B, 0:1 + B])
            last.then_inc(c_turned, 1)
            pe.wait_ge(silu_ready, 1)
            def ada_fold(i):
                part = PART_ORDER[i]
                pe.wait_ge(ada_banks_free, 2 + 2 * i + 2)
                if i < 4:
                    for k in range(KC):
                        at = part * D + k * P
                        last = mm(psum[:, 3 + i // 2, (i % 2) * 256 + k * QUAD:(i % 2) * 256 + (k + 1) * QUAD],
                                  ada_out[:, at:at + P], C("quad_fold"), start=True, stop=True)
                    last.then_inc(mod_done, 1)
                    return
                for who, rows in (("pick_prompt", P), ("pick_sample", QUAD)):
                    for j in range(D // BANK):
                        pe.wait_ge(gates_kept, 1 + len(gate_folds))
                        mm(psum[0:rows, 5 + j, :], C(who), ada_out[:, part * D + j * BANK:part * D + (j + 1) * BANK],
                           start=True, stop=True).then_inc(gates_done, 1)
                        gate_folds.append(1)

            gate_folds = []
            for i in range(z.MODS):
                for s in range(2):
                    pe.wait_ge(ada_in[s], 16 * i + 16)
                    pe.wait_ge(ada_banks_free, 2 * i + s + 1)
                    for k in range(KC):
                        q = QUAD * (k % 4)
                        last = mm(psum[q:q + QUAD, 1 + s, :], silu_t[:, k, :], ada_w[:, s, k, :],
                                  start=k < 4, stop=k >= KC - 4)
                    last.then_inc(ada_done, 1)
                if i:
                    ada_fold(i - 1)
            ada_fold(z.MODS - 1)
            stage_end(pe, 1)

            def turn_unit(rows, u, c, k):
                pe.wait_ge(x_banks_free, u + 1)
                for t in range(TPC):
                    last = turn(psum[:, u % 4, t * P:(t + 1) * P], rows[:, c * TPC + t, k * P:(k + 1) * P], ident)
                last.then_inc(x_turned, 1)

            for c in range(NCH):
                pe.wait_ge(x_in[c], 16)
                for k in range(KC):
                    turn_unit(x_rows, c * KC + k, c, k)

            def turn_sample():
                for k in range(KC):
                    last = turn(psum[:, 4, k * QUAD:(k + 1) * QUAD], xs_rows[:, k * P:(k + 1) * P], ident[0:QUAD, 0:QUAD])
                last.then_inc(xs_turned, 1)

            pe.wait_ge(xs_in, 16)
            turn_sample()
            pe.wait_ge(x_split, 2 + UNITS)
            pe.wait_ge(xs_ready, 1)

            def sample_product(n, s):
                pe.wait_ge(w_lo_done, n + 1)
                pe.wait_ge(s_quads_free, n + 1)
                for k in range(KC):
                    q = QUAD * (k % 4)
                    last = mm(psum[q:q + QUAD, 4 + s, 0:WB], x_t_s[:, k, :], w_raw[:, s, k, :],
                              start=k < 4, stop=k >= KC - 4)
                last.then_inc(s_done, 1)

            def sample_fold(n, s, free, value):
                pe.wait_ge(s_quads_free, n + 3)
                pe.wait_ge(free, value)
                mm(psum[0:QUAD, 6 + s, 0:WB], C("quad_fold"), s_quads[:, s, :],
                   start=True, stop=True).then_inc(s_folded, 1)

            PARTS = ((w_hi, x_hi), (w_hi, x_lo), (w_lo, x_hi))

            def by_feature(s, ft):
                for k in range(KC):
                    for j, (w, x) in enumerate(PARTS):
                        for c in range(NCH):
                            last = mm(psum[:, 2 * ft + c, 0:CH], w[:, s, k, ft * P:(ft + 1) * P], x[:, k, c * CH:(c + 1) * CH],
                                      start=k == 0 and j == 0, stop=k == KC - 1 and j == 2)
                return last

            def by_token(s, t):
                for k in range(KC):
                    for j, (w, x) in enumerate(PARTS):
                        last = mm(psum[:, t % TB, 0:WB], x[:, k, t * P:(t + 1) * P], w[:, s, k, :],
                                  start=k == 0 and j == 0, stop=k == KC - 1 and j == 2)
                return last

            with pe.Fori(0, 3) as i:
                for s in range(2):
                    n = 2 * i + s
                    sample_product(n, s)
                    for ft in range(FT):
                        pe.wait_ge(fm_free, FT * n + ft + 1)
                        by_feature(s, ft).then_inc(fm_done, 1)
                    sample_fold(n, s, s_fold_free, n + 1)

            def token_blocks(first, count, tm_before):
                with pe.Fori(0, count // 2) as i:
                    for s in range(2):
                        n = first + 2 * i + s
                        sample_product(n, s)
                        for t in range(NT):
                            pe.wait_ge(tm_free, tm_before + (2 * i + s) * NT + t + 1)
                            by_token(s, t).then_inc(tm_done, 1)
                        sample_fold(n, s, s_fold_free, n + 1)

            pe.wait_ge(fm_free, 2 + 6 * FT)
            token_blocks(6, 6, 0)
            pe.wait_ge(q_wide_ready, 1)
            for hb in range(4 * H):
                last = mm(psum[:, 7, hb * BS:(hb + 1) * BS], q_wide[:, hb].rearrange("p a j -> p (a j)"),
                          ident[0:QUAD, 0:QUAD], start=True, stop=True)
            last.then_inc(q_all_done, 1)
            stage_end(pe, 2)

            pe.sem_inc(v_free, RING)

            def head_start(h):
                pe.wait_ge(qk_in, 32 * h + 32)
                pe.wait_ge(a_t_ready, h * NT + 1)
                for t in range(NT):
                    last = turn(psum[:, ROWS + t // 4, (t % 4) * P:(t % 4 + 1) * P], k_rows[:, t, :], ident)
                last.then_inc(k_rows_turned, 1)
                pe.wait_ge(k_t_ready, h + 1)
                for t in range(NT):
                    last = turn(psum[:, ROWS + t // 4, (t % 4) * P:(t % 4 + 1) * P], q_rows[:, t, :], ident)
                last.then_inc(rows_turned, 1)
                pe.wait_ge(head_ready, h + 1)

            def scores(n, i, c):
                pe.wait_ge(score_banks_free, 2 * n + c + 1)
                pe.wait_ge(a_t_ready, n + 1)
                for k0 in range(0, (i + 1) * P, BANK):
                    w = min(BANK, (i + 1) * P - k0)
                    last = mm(psum[:, ROWS + k0 // BANK, 0:w], q_zero[:, c, i * P:(i + 1) * P], k_t[:, k0:k0 + w],
                              start=True, stop=True)
                last.then_inc(scores_done, 1)

            def turn_rows(n, i):
                pe.wait_ge(a_ready, n + 2)
                for j in range(i + 1):
                    last = turn(psum[:, ROWS + j // 4, (j % 4) * P:(j % 4 + 1) * P], a_rows[:, j * P:(j + 1) * P], ident)
                last.then_inc(a_turned, 1)

            def weigh_rows(h, n, i):
                pe.wait_ge(a_t_ready, n + 2)
                pe.wait_ge(o_free, n + 1)
                for j in range(i + 1):
                    last = mm(psum[:, OUT, 0:P], a_t[:, j * P:(j + 1) * P],
                              v_rows[:, j, ds(h * HD, HD)], start=j == 0, stop=j == i)
                last.then_inc(pv_done, 1)

            def new_keys(b):
                pe.wait_ge(q_ready, b + 1)
                for h in range(H):
                    for d in range(4):
                        last = mm(psum[QUAD * h:QUAD * (h + 1), MISC, 416:416 + QUAD], q_blocks[:, h, d, :],
                                  k_new_t[:, h * HD + d * QUAD:h * HD + (d + 1) * QUAD], start=d == 0, stop=d == 3)
                last.then_inc(new_scored, 1)

            def key_group(b, r, g):
                n = (b * REVS + r) * RING + g
                pe.wait_ge(k_free, RING + 1 + n)
                pe.wait_ge(s_bank_free, n + 1)
                for h in range(H):
                    for d in range(4):
                        last = mm(psum[QUAD * h:QUAD * (h + 1), g % 2, 0:GP * QUAD], q_blocks[:, h, d, :],
                                  k_turned[:, g % 2, :, h * HD + d * QUAD:h * HD + (d + 1) * QUAD],
                                  start=d == 0, stop=d == 3)
                last.then_inc(scored, 1)

            def value_group(b, r, g, stop):
                pe.wait_ge(v_in[g], (b * REVS + r + 1) * (16 * GP))
                for j in range(GP):
                    for h in range(H):
                        last = mm(psum[QUAD * h:QUAD * (h + 1), 2, 0:P], p_t[:, (r * RING + g) * GP + j, :],
                                  v_ring[:, g, j, h * HD:(h + 1) * HD], start=False, stop=stop and j == GP - 1)
                last.then_inc(v_free, 1)

            def softmax(b):
                pe.wait_ge(max_ready, b + 1)
                pe.wait_ge(o_t_kept, b + 1)
                turn(psum[0:1, MISC, 0:P], dec[:, 0:1], ident).then_inc(max_turned, 1)
                pe.wait_ge(max_spread, b + 1)
                mm(psum[:, MISC, 256:257], max_row[0:1, 1, :], ident[0:1, 0:1], start=True, stop=True).then_inc(max_back, 1)
                for r in range(REVS):
                    pe.wait_ge(exp_done, b * (REVS + 1) + r + 1)
                    for g in range(4):
                        last = turn(psum[:, r, g * P:(g + 1) * P], s_rows[:, r * BANK + g * P:r * BANK + (g + 1) * P], ident)
                pe.wait_ge(exp_done, (b + 1) * (REVS + 1))
                mm(psum[:, MISC, 384:384 + REVS + 1], C("head_fold"), dec[:, 2:3 + REVS], start=True, stop=True)
                turn(psum[0:QUAD, MISC, P:2 * P], s_rows[:, NEW0:SC], ident).then_inc(p_turned, 1)
                pe.wait_ge(p_by_act, b + 1)
                pe.wait_ge(p_by_dve, b + 1)
                for h in range(H):
                    mm(psum[QUAD * h:QUAD * (h + 1), 2, 0:P], p_new[:], v_new[:, h * HD:(h + 1) * HD], start=True, stop=False)

            def by_query(b):
                pe.wait_ge(o_scaled_ready, b + 1)
                mm(psum[:, MISC, 448:448 + H * S], o_scaled[:], C("own_head"), start=True, stop=True).then_inc(o_t_done, 1)

            def step(b, h, half, first=False):
                if half == 0:
                    pe.wait_ge(v_in_rows, 16)
                    head_start(h)
                if not first:
                    softmax(b - 1)
                new_keys(b)
                for r in range(REVS):
                    n, i = b * REVS + r, TILES[half][r]
                    for g in range(RING):
                        if g < 2:
                            scores(n, i, g)
                        if g == 3:
                            turn_rows(n, i)
                        key_group(b, r, g)
                        if not first:
                            value_group(b - 1, r, g, (r, g) == (REVS - 1, RING - 1))
                    weigh_rows(h, n, i)
                if not first:
                    by_query(b - 1)

            step(0, 0, 0, first=True)
            with pe.Fori(0, H - 1) as i:
                step(2 * i + 1, i, 1)
                step(2 * i + 2, i + 1, 0)
            step(B - 1, H - 1, 1)
            softmax(B - 1)
            for r in range(REVS):
                for g in range(RING):
                    value_group(B - 1, r, g, (r, g) == (REVS - 1, RING - 1))
            by_query(B - 1)
            stage_end(pe, 3)

            for t in range(NT):
                pe.wait_ge(o_normed, t + 1)
                if t >= 4:
                    pe.wait_ge(o_banks_free, t - 3)
                for h in range(H):
                    last = turn(psum[:, t % 4, h * P:(h + 1) * P], o_rows[:, t, h * HD:(h + 1) * HD], ident)
                last.then_inc(o_turned, 1)
            pe.wait_ge(os_sq, 1)
            mm(psum[:, 4, 0:B * H * S], C("mean"), o_t_sq[:], start=True, stop=True).then_inc(os_mean, 1)
            for k in range(CC // P):
                last = turn(psum[:, 5, k * QUAD:(k + 1) * QUAD], y_s[:, k * P:(k + 1) * P], ident[0:QUAD, 0:QUAD])
            last.then_inc(ys_turned, 1)
            pe.wait_ge(o_banks_free, NT)
            pe.wait_ge(ys_ready, 1)
            token_blocks(MIX0, NB_OUT, 6 * NT)
            for c in range(NCH):
                pe.wait_ge(x1_ready, (c + 1) * TPC // 2)
                pe.wait_ge(x1_odd_ready, (c + 1) * TPC // 2)
                for k in range(KC):
                    turn_unit(x1, UNITS + c * KC + k, c, k)
            pe.wait_ge(xs_normed, 1)
            turn_sample()
            pe.wait_ge(x_split, 2 + 2 * UNITS)
            pe.wait_ge(xs_ready, 2)

            with pe.Fori(0, NG) as i:
                for s in range(2):
                    n = FF0 + 2 * i + s
                    sample_product(n, s)
                    for ft in range(FT):
                        if s == 0:
                            pe.wait_ge(up_free, i * FT + ft + 1)
                        else:
                            pe.wait_ge(gate_free, i * FT + ft + 1)
                        by_feature(s, ft).then_inc(fm_done, 1)
                    sample_fold(n, s, (gs_taken, us_taken)[s], i + 1)
                pe.wait_ge(consts_in, 16)
                pe.wait_ge(hs_ready, i + 1)
                for ft in range(FT):
                    last = turn(psum[:, 7, WB + ft * QUAD:WB + (ft + 1) * QUAD], h_s[:, ft * P:(ft + 1) * P], ident[0:QUAD, 0:QUAD])
                last.then_inc(hs_turned, 1)
            stage_end(pe, 4)

            with pe.Fori(0, D // WB // 2) as i:
                for par in range(2):
                    nb = 2 * i + par
                    for k in range(NF):
                        pe.wait_ge(d_split, nb * NF + (k + 3))
                        s = (par * NF + k) % 4
                        for t in range(NT):
                            pair = t // 2
                            if k == 0 and t % 2 == 0:
                                pe.wait_ge(down_free, nb * DB + (DB + 1 if pair == DB - 1 else pair + 2))
                            for j, (x, w) in enumerate(((h_hi, d_hi), (h_hi, d_lo), (h_lo, d_hi))):
                                last = mm(psum[:, down_bank(par, pair), (t % 2) * WB:(t % 2 + 1) * WB],
                                          x[:, s, t * P:(t + 1) * P], w[:, s, :],
                                          start=k == 0 and j == 0 and t % 2 == 0, stop=k == NF - 1 and j == 2,
                                          skip_group_check=True)
                        if k == 0:
                            pe.wait_ge(down_quads_in, nb + 1)
                        q = QUAD * (k % 4)
                        last = mm(psum[q:q + QUAD, 4, 0:WB], h_t_s[:, k, :], d_raw[:, (k // 2) % 4, k % 2, :],
                                  start=k < 4, stop=k >= NF - 4)
                        last.then_inc(d_used, 1)
            pe.wait_ge(down_quads_in, 1 + D // WB)
            pe.wait_ge(down_free, 2 * DB + DB * (D // WB - 1))
            for j in range(D // BANK):
                last = mm(psum[0:QUAD, 1 + j, :], C("quad_fold"), down_quads[:, j * BANK:(j + 1) * BANK], start=True, stop=True)
            last.then_inc(down_folded, 1)

        @block.scalar
        def _(act):
            go, copy = nc.scalar.activation, nc.scalar.copy

            act.sem_inc(gates_kept, 2)
            act.wait_ge(c_turned, 1)
            act.wait_ge(silu_zeroed, 1)
            go(silu_t[:, :, 0:1 + B], psum[:, 0, 0:16 * KC].rearrange("p (k c) -> p k c", c=16)[:, :, 0:1 + B],
               ACT.Silu).then_inc(silu_ready, 1)
            act.wait_ge(lam_sums, 1)
            go(small[:, 2:4], small[:, 0:2], ACT.Exp).then_inc(lam_exps, 1)
            for n in range(8):
                gate, who, j = n // 4, n // 2 % 2, n % 2
                gates = (gate_p, gate_s)[who]
                act.wait_ge(gates_done, n + 1)
                copy(gates[:, gate, j * BANK:(j + 1) * BANK], psum[0:(P, QUAD)[who], 5 + j, :]).then_inc(gates_kept, 1)
            stage_end(act, 1)

            act.sem_inc(x_banks_free, 4)

            def modulate(u, c, k, x, shift, scale):
                act.wait_ge(x_turned, u + 1)
                act.wait_ge(x_split, u + 1)
                go(x[:, u % 2, :], psum[:, u % 4, 0:CH], ACT.Identity, bias=mod_t[:, shift, k, 0:1],
                   scale=mod_t[:, scale, k, 0:1]).then_inc(x_banks_free, 1)

            for c in range(NCH):
                for k in range(KC):
                    modulate(c * KC + k, c, k, x_mod, 0, 1)

            def w_high(n, s, fills):
                act.wait_ge(w_in_sem[s], 16 * fills)
                if not isinstance(n, int) or n >= 2:
                    act.wait_ge(s_folded, n - 1)
                copy(w_hi[:, s], w_raw[:, s]).then_inc(w_hi_done, 1)

            w_high(0, 0, 1)
            for n in range(NB_IN):
                if n + 1 < NB_IN:
                    w_high(n + 1, (n + 1) % 2, (n + 1) // 2 + 1)
                if n >= 6:
                    m = n - 6
                    if m == 0:
                        act.wait_ge(fm_free, 2 + 6 * FT)
                        act.wait_ge(conv_stored, 16 * (CC // P))
                    if m >= 2:
                        act.wait_ge(z_stored[m % 2], 16 * (m // 2))
                    for t in range(NT):
                        act.wait_ge(tm_done, m * NT + t + 1)
                        copy(z_rows[:, m % 2, t, :], psum[:, t % TB, 0:WB]).then_inc(tm_free, 1)
            act.wait_ge(q_all_done, 1)
            copy(q_all[:].rearrange("p h b -> p (h b)"), psum[:, 7, :]).then_inc(q_all_kept, 1)
            stage_end(act, 2)

            fetch_head(act, 0)
            act.sem_inc(score_banks_free, 1)
            act.sem_inc(a_t_ready, 1)
            act.sem_inc(s_bank_free, 2)
            act.sem_inc(o_t_kept, 1)
            act.wait_ge(q_zeroed, 1)

            def head_start(h):
                both = psum[:, ROWS:ROWS + -(-T // BANK), 0:CH]
                act.wait_ge(k_rows_turned, h + 1)
                copy(k_t[:], both.rearrange("p c n -> p (c n)")).then_inc(k_t_ready, 1)
                act.wait_ge(rows_turned, h + 1)
                for c in range(2):
                    r = slice(c * QK, (c + 1) * QK)
                    last = nc.scalar.mul(q_zero[r, c, :], both[r].rearrange("p c n -> p (c n)"), SCORE_SCALE)
                last.then_inc(head_ready, 1)

            def exps(n, i, c):
                act.wait_ge(neg_max, 2 * n + c + 1)
                act.wait_ge(a_ready, n + 1)
                w = (i + 1) * P
                go(e_rows[:, c, 0:w], psum[:, ROWS:ROWS + 2, :].rearrange("p c n -> p (c n)")[:, 0:w], ACT.Exp,
                   bias=soft[:, 2 + c:3 + c], accum_out=soft[:, 4 + c:5 + c]).then_inc(score_banks_free, 1)

            def keep_turned(n, i):
                act.wait_ge(a_turned, n + 2)
                act.wait_ge(pv_done, n + 1)
                w = (i + 1) * P
                copy(a_t[:, 0:w], psum[:, ROWS:ROWS + 2, :].rearrange("p c n -> p (c n)")[:, 0:w]).then_inc(a_t_ready, 1)

            def take_scores(b, r, g):
                n = (b * REVS + r) * RING + g
                act.wait_ge(scored, 3 + n)
                copy(s_rows[:, (r * RING + g) * (GP * QUAD):(r * RING + g + 1) * (GP * QUAD)], psum[:, g % 2, 0:GP * QUAD]
                     ).then_inc(s_bank_free, 1)

            def softmax(b):
                act.wait_ge(negmax_ready, b + 1)
                for r in range(REVS + 1):
                    part = s_rows[:, r * BANK:(r + 1) * BANK] if r < REVS else s_rows[:, NEW0:SC]
                    go(part, part, ACT.Exp, bias=dec[:, 1:2], accum_out=dec[:, 2 + r:3 + r]).then_inc(exp_done, 1)
                act.wait_ge(p_turned, b + 1)
                for j in range(0, 2):
                    last = regroup(copy, j)
                last.then_inc(p_by_act, 1)

            def keep_output(b):
                act.wait_ge(o_t_done, b + 1)
                copy(o_t_all[:, ds(b, 1), :], psum[:, MISC, 448:448 + H * S].rearrange("p (o n) -> p o n", o=1)).then_inc(o_t_kept, 1)

            def step(b, h, half, first=False):
                if half == 0:
                    head_start(h)
                if not first:
                    softmax(b - 1)
                for r in range(REVS):
                    n, i = b * REVS + r, TILES[half][r]
                    for g in range(RING):
                        if g == 3:
                            keep_turned(n, i)
                        take_scores(b, r, g)
                        if g < 2:
                            exps(n, i, g)
                if not first:
                    keep_output(b - 1)

            step(0, 0, 0, first=True)
            with act.Fori(0, H - 1) as i:
                fetch_head(act, i + 1)
                step(2 * i + 1, i, 1)
                step(2 * i + 2, i + 1, 0)
            step(B - 1, H - 1, 1)
            softmax(B - 1)
            keep_output(B - 1)
            stage_end(act, 3)

            act.wait_ge(sq_ready, 1)
            go(o_moments[:, :, 1], o_moments[:, :, 1], ACT.Sqrt, bias=eps_col[:]).then_inc(sq_root, 1)
            w_high(MIX0, 0, NB_IN // 2 + 1)
            act.wait_ge(y_conv_in, 16)
            copy(x_hi[:, 0:CC // P, :], y_conv[:]).then_inc(y_hi_done, 1)
            for t in range(NT):
                act.wait_ge(o_turned, t + 1)
                go(x_hi[:, CC // P:, t * P:(t + 1) * P], psum[:, t % 4, :].rearrange("p (h n) -> p h n", n=P), ACT.Copy,
                   scale=g_attn[:, 0:1]).then_inc(o_hi_done, 1)
            act.wait_ge(os_mean, 1)
            go(o_t_sq[:], psum[:, 4, 0:B * H * S], ACT.Sqrt, bias=eps_col[:]).then_inc(os_root, 1)
            FILLS = NB_IN // 2
            for j in range(NB_OUT - 1):
                w_high(MIX0 + j + 1, (j + 1) % 2, FILLS + (j + 1) // 2 + 1)

            def roots(count):
                act.wait_ge(var_ready, count)
                var = rstd[:, 0:2 * NT].rearrange("p (t j) -> p t j", j=2)[:, :, 1]
                go(var, var, ACT.Sqrt, bias=eps_col[:])
                var = rstd[0:QUAD, 2 * NT + 1:2 * NT + 2]
                go(var, var, ACT.Sqrt, bias=eps_col[0:QUAD]).then_inc(root_ready, 1)

            def normalise(t, x, done):
                rows = x.shape[0]
                go(x, x, ACT.Identity, bias=rstd[0:rows, 48 + t:49 + t], scale=rstd[0:rows, 32 + t:33 + t]).then_inc(done, 1)

            roots(1)
            act.wait_ge(norm_ready, 1)
            for c in range(NCH):
                for t in range(c * TPC, (c + 1) * TPC, 2):
                    normalise(t, x1[:, t, :], x1_ready)
                for k in range(KC):
                    modulate(UNITS + c * KC + k, c, k, x1_mod, 2, 3)
                if c == 0:
                    normalise(NT, xs_rows[:], xs_normed)

            act.wait_ge(x_split, 2 + 2 * UNITS)
            FILLS = (NB_IN + NB_OUT) // 2
            w_high(FF0, 0, FILLS + 1)

            def gate_up(i, more):
                w_high(FF0 + 1 + 2 * i, 1, FILLS + 1 + i)
                act.wait_ge(h_stored, 16 * i + 16)
                for ft in range(FT):
                    act.wait_ge(fm_done, 6 * FT + 2 * FT * i + ft + 1)
                    go(h_out[:, ft, :], psum[:, 2 * ft:2 * ft + NCH, 0:CH].rearrange("p c n -> p (c n)"), ACT.Silu).then_inc(gate_free, 1)
                act.wait_ge(s_folded, FF0 + 1 + 2 * i)
                act.wait_ge(us_taken, i + 1)
                go(gate_act_s[:], psum[0:QUAD, 6, 0:WB], ACT.Silu).then_inc(gs_taken, 1)
                if more:
                    w_high(FF0 + 2 + 2 * i, 0, FILLS + 2 + i)

            with act.Fori(0, NG - 1) as i:
                gate_up(i, True)
            gate_up(NG - 1, False)
            stage_end(act, 4)

            with act.Fori(0, D // WB // 2) as i:
                for par in range(2):
                    nb = 2 * i + par
                    for k in range(NF):
                        pp, s = k // 2, (par * NF + k) % 4
                        if k % 2 == 0:
                            fills = (PAIRS - pp % 4 + 3) // 4
                            act.wait_ge(d_in[pp % 4], 16 * (nb * fills + (pp // 4 + 1)))
                            if par == 0:
                                act.wait_ge(h_in[pp], 16)
                        act.wait_ge(d_used, nb * NF + (k + 1))
                        copy(h_hi[:, s, :], h_all[:, k, :])
                        copy(d_hi[:, s, :], d_raw[:, pp % 4, k % 2, :]).then_inc(d_hi_done, 1)
            roots(2)
            act.wait_ge(norm_ready, 2)
            for t in range(0, NT, 2):
                normalise(t, x1[:, t, :], x1_ready)
            normalise(NT, xs_rows[:], xs_normed)

        @block.vector
        def _(dve):
            v = nc.vector
            link, linked_loop = chain(dve, dve_step)

            v.memset(ada_bias[:], 0.0).then_inc(bias_zeroed, 1)
            v.memset(silu_t[:], 0.0).then_inc(silu_zeroed, 1)
            dve.sem_inc(ada_banks_free, 2)
            v.memset(k_new_t[:], 0.0)
            v.memset(v_new[:], 0.0)
            v.memset(q_blocks[:], 0.0)
            link(v.memset(eps_col[:], LN_EPS))
            dve.wait_ge(vectors_in, 16 * 10)
            for j in range(2):
                link(v.tensor_tensor(lam_rows[:, 2 * j, :], lam_rows[:, 2 * j, :], lam_rows[:, 2 * j + 1, :], ALU.mult))
            link(v.tensor_reduce(small[:, 0:1], lam_rows[:, 0, :], AX_X, ALU.add))
            v.tensor_reduce(small[:, 1:2], lam_rows[:, 2, :], AX_X, ALU.add).then_inc(lam_sums, 1)
            dve.wait_ge(lam_exps, 1)
            link(v.tensor_tensor(small[:, 5:6], small[:, 3:4], small[:, 2:3], ALU.subtract))
            link(v.tensor_scalar(NEG_LAM, small[:, 5:6], -lam_init, None, ALU.add))
            dve.wait_ge(consts_in, 16)
            link(v.tensor_scalar(small[:, 7:8], C("comp1"), NEG_LAM, None, ALU.mult))
            link(v.tensor_tensor(COEF, small[:, 7:8], C("comp0"), ALU.add))
            link(v.tensor_scalar(g_attn[:], g_attn[:], 1.0 - lam_init, None, ALU.mult))
            dve.wait_ge(bias_in, 16)
            for i in range(z.MODS):
                for s in range(2):
                    dve.wait_ge(ada_done, 2 * i + s + 1)
                    at = ds((2 * PART_ORDER[i] + s) * BANK, BANK)
                    v.tensor_tensor(ada_out[:, at], psum[:, 1 + s, :], ada_bias[:, at], ALU.add).then_inc(ada_banks_free, 1)
            dve.wait_ge(mod_done, 4)
            for m in range(4):
                last = v.tensor_scalar(mod_t[:, m].rearrange("p k c -> p (k c)"), psum[:, 3 + m // 2, (m % 2) * 256:(m % 2) * 256 + KC * QUAD],
                                       float(m % 2), None, ALU.add)
            link(last)
            wide = lambda j: ln1_t[:, j, :].unsqueeze(2).to_broadcast([P, KC, QUAD])
            link(v.tensor_tensor(silu_t[:], mod_t[:, 3], wide(1), ALU.mult))
            link(v.tensor_tensor(mod_t[:, 2], mod_t[:, 2], silu_t[:], ALU.add))
            link(v.tensor_tensor(mod_t[:, 3], mod_t[:, 3], wide(0), ALU.mult))
            stage_end(dve, 1)

            dve.sem_inc(x_split, 2)
            dve.sem_inc(s_quads_free, 2)
            dve.sem_inc(s_fold_free, 2)
            dve.sem_inc(fm_free, 2)
            dve.sem_inc(tm_free, TB)

            def split(u, c, k, x):
                at = slice(c * CH, (c + 1) * CH)
                dve.wait_ge(x_banks_free, u + 5)
                v.tensor_copy(x_hi[:, k, at], x[:, u % 2, :]).then_inc(x_hi_done, 1)
                dve.wait_ge(x_hi_done, u + 1)
                v.tensor_tensor(x_lo[:, k, at], x[:, u % 2, :], x_hi[:, k, at], ALU.subtract).then_inc(x_split, 1)

            def modulate_sample(shift, scale):
                per_token = lambda m: mod_t[:, m, :, 1:1 + B].unsqueeze(3).to_broadcast([P, KC, B, S])
                out = x_t_s[:].rearrange("p k (b t) -> p k b t", t=S)
                link(v.tensor_tensor(out, psum[:, 4, 0:KC * QUAD].rearrange("p (k b t) -> p k b t", b=B, t=S), per_token(scale), ALU.mult))
                v.tensor_tensor(out, out, per_token(shift), ALU.add).then_inc(xs_ready, 1)

            for c in range(NCH):
                for k in range(KC):
                    split(c * KC + k, c, k, x_mod)
            dve.wait_ge(x_split, 2 + UNITS)
            link(v.memset(u_conv[:, :, 0:2], 0.0))
            dve.wait_ge(xs_turned, 1)
            modulate_sample(0, 1)

            def w_low(n, s):
                dve.wait_ge(w_hi_done, n + 1)
                v.tensor_tensor(w_lo[:, s], w_raw[:, s], w_hi[:, s], ALU.subtract).then_inc(w_lo_done, 1)

            def take_quads(n, s):
                dve.wait_ge(s_done, n + 1)
                v.tensor_copy(s_quads[:, s, :], psum[:, 4 + s, 0:WB]).then_inc(s_quads_free, 1)

            w_low(0, 0)
            for n in range(NB_IN):
                s = n % 2
                if n + 1 < NB_IN:
                    w_low(n + 1, 1 - s)
                take_quads(n, s)
                for ft in range(FT):
                    if n >= 6:
                        break
                    f = (n % 2) * FT + ft
                    dve.wait_ge(fm_done, FT * n + ft + 1)
                    got = psum[:, 2 * ft:2 * ft + NCH, 0:CH].rearrange("p c n -> p (c n)")
                    u = u_conv[:, f, 2:2 + T]
                    y = y_conv[:, f, :]
                    if cols_of[n] == "c":
                        v.tensor_copy(u, got).then_inc(fm_free, 1)
                    elif cols_of[n] == "h":
                        v.tensor_tensor(u, got, u, ALU.mult).then_inc(fm_free, 1)
                        dve.wait_ge(fm_free, 3 + FT * n + ft)
                        link(v.tensor_scalar(y, u_conv[:, f, 0:T], conv_w_t[:, 0, f:f + 1], None, ALU.mult))
                        link(v.scalar_tensor_tensor(y, u_conv[:, f, 1:1 + T], conv_w_t[:, 1, f:f + 1], y, ALU.mult, ALU.add))
                        if f == CC // P - 1:
                            v.scalar_tensor_tensor(y, u, conv_w_t[:, 2, f:f + 1], y, ALU.mult, ALU.add).then_inc(conv_ready, 1)
                            dve.wait_ge(conv_ready, 1)
                        else:
                            link(v.scalar_tensor_tensor(y, u, conv_w_t[:, 2, f:f + 1], y, ALU.mult, ALU.add))
                    else:
                        v.tensor_tensor(y, got, y, ALU.mult).then_inc(fm_free, 1)
                if 6 <= n < 10:
                    m = n - 6
                    dve.wait_ge(tm_free, TB + (m + 1) * NT)
                    pair = z_rows[:, m % 2].rearrange("p t (g d) -> p t g d", d=QK)
                    cos = C("cos_p").rearrange("p (t d) -> p t d", d=8).unsqueeze(2).to_broadcast([P, NT, 4, 8])
                    sin = C("sin_p").rearrange("p (t d) -> p t d", d=8).unsqueeze(2).to_broadcast([P, NT, 4, 8])
                    rope(pair[:, :, :, 0:8], pair[:, :, :, 8:16], cos, sin,
                         [rope_p[:, j, :].rearrange("p (t g d) -> p t g d", g=4, d=8) for j in range(4)], link, roped)
                    dve.wait_ge(roped, m + 1)
                dve.wait_ge(s_folded, n + 1)
                v.tensor_copy(z_s[:, in_cols[n]:in_cols[n] + WB], psum[0:QUAD, 6 + s, 0:WB]).then_inc(s_fold_free, 1)
            dve.wait_ge(s_fold_free, 2 + NB_IN)
            for s in range(2):
                dve.wait_ge(z_stored[s], 48)
            v.tensor_copy(y_s[:], z_s[:, CC:2 * CC])
            v.tensor_tensor(u_s[:], z_s[:, 2 * CC:3 * CC], z_s[:, 0:CC], ALU.mult).then_inc(s_conv_ready, 1)
            qk = z_s[:, 3 * CC:3 * CC + 2 * AW].rearrange("p (g d) -> p g d", d=QK)
            cos = C("cos_s")[0:QUAD].unsqueeze(1).to_broadcast([QUAD, 4 * H, 8])
            sin = C("sin_s")[0:QUAD].unsqueeze(1).to_broadcast([QUAD, 4 * H, 8])
            rope(qk[:, :, 0:8], qk[:, :, 8:16], cos, sin,
                 [rope_s[:, j, :].rearrange("p (g d) -> p g d", d=8) for j in range(4)], link, s_roped)
            dve.wait_ge(s_roped, 1)
            v.transpose(k_new_t[0:QUAD, :], z_s[:, 3 * CC + AW:3 * CC + 2 * AW])
            link(v.tensor_copy(v_new[0:QUAD, :], z_s[:, 3 * CC + 2 * AW:]))
            v.tensor_scalar(q_wide[:], z_s[:, 3 * CC:3 * CC + AW].rearrange("p (g j) -> p g j", j=QUAD).unsqueeze(2)
                            .to_broadcast([QUAD, 4 * H, 4, QUAD]), SCORE_SCALE, None, ALU.mult).then_inc(q_wide_ready, 1)
            stage_end(dve, 2)

            dve.sem_inc(k_free, RING)
            dve.sem_inc(a_ready, 1)
            dve.sem_inc(a_turned, 1)
            dve.sem_inc(pv_done, 1)
            dve.sem_inc(o_free, 1)
            dve.sem_inc(scored, 2)
            v.memset(q_zero[:], 0.0).then_inc(q_zeroed, 1)
            dve.wait_ge(conv_s_in, 96)
            for j in range(3):
                link(v.tensor_tensor(conv_s[:, j, :], conv_s[:, j, :], conv_s[:, 4 + j, :], ALU.mult))
            link(v.tensor_tensor(conv_s[:, 0, :], conv_s[:, 0, :], conv_s[:, 1, :], ALU.add))
            link(v.tensor_tensor(conv_s[:, 0, :], conv_s[:, 0, :], conv_s[:, 2, :], ALU.add))
            link(v.tensor_tensor(y_s[:], y_s[:], conv_s[:, 0, :], ALU.mult))
            link(v.memset(p_new[:], 0.0))

            def maxima(n, i, c):
                w = (i + 1) * P
                dve.wait_ge(scores_done, 2 * n + c + 1)
                diag = psum[:, ROWS + i // 4, (i % 4) * P:(i % 4 + 1) * P]
                link(v.tensor_tensor(diag, diag, C("causal"), ALU.add))
                link(v.tensor_reduce(soft[:, c:c + 1], psum[:, ROWS:ROWS + 2, :].rearrange("p c n -> p (c n)")[:, 0:w], AX_X, ALU.max))
                v.tensor_scalar(soft[:, 2 + c:3 + c], soft[:, c:c + 1], -1.0, None, ALU.mult).then_inc(neg_max, 1)

            def combine(n, i):
                w = (i + 1) * P
                dve.wait_ge(score_banks_free, 2 * n + 3)
                link(v.reciprocal(soft[:, 6:8], soft[:, 4:6]))
                link(v.tensor_scalar(soft[:, 7:8], soft[:, 7:8], NEG_LAM, None, ALU.mult))
                dve.wait_ge(a_turned, n + 1)
                link(v.tensor_scalar(a_rows[:, 0:w], e_rows[:, 0, 0:w], soft[:, 6:7], None, ALU.mult))
                v.scalar_tensor_tensor(a_rows[:, 0:w], e_rows[:, 1, 0:w], soft[:, 7:8], a_rows[:, 0:w], ALU.mult, ALU.add
                                       ).then_inc(a_ready, 1)

            def take_rows(h, n, i):
                dve.wait_ge(pv_done, n + 2)
                v.bn_stats(o_stats[:, ds((i * H + h) * 6, 6)], psum[:, OUT, 0:P])
                v.tensor_copy(o_rows[:, i, ds(h * HD, HD)], psum[:, OUT, 0:P]).then_inc(o_free, 1)

            q_rows_of = q_all[:].rearrange("p (h d) n -> p h d n", d=4)

            def queries(b):
                dve.wait_ge(scored, 2 + b * (REVS * RING))
                for a in range(4):
                    for c in range(2):
                        r = slice(QUAD * a, QUAD * (a + 1))
                        last = v.tensor_copy(q_blocks[r, :, 2 * c:2 * c + 2, a * 8 + c * S:a * 8 + (c + 1) * S],
                                             q_rows_of[r, :, 2 * c:2 * c + 2, ds(b * S, S)])
                last.then_inc(q_ready, 1)
                dve.wait_ge(new_scored, b + 1)
                v.tensor_tensor(s_rows[:, NEW0:SC].rearrange("p (o n) -> p o n", o=1), psum[:, MISC, 416:416 + QUAD].rearrange("p (o n) -> p o n", o=1),
                                C("new_mask").rearrange("p (b n) -> p b n", n=QUAD)[:, ds(b, 1), :], ALU.add)

            def turn_keys(b, r, g):
                n = (b * REVS + r) * RING + g
                dve.wait_ge(k_in[g], (b * REVS + r + 1) * (16 * GP))
                dve.wait_ge(scored, n + 1)
                v.transpose(k_turned[:, g % 2].rearrange("p j n -> p (j n)"), k_ring[:, g].rearrange("p j n -> p (j n)")
                            ).then_inc(k_free, 1)

            def softmax(b):
                dve.wait_ge(s_bank_free, 2 + (b + 1) * (REVS * RING))
                v.tensor_reduce(dec[:, 0:1], s_rows[:], AX_X, ALU.max).then_inc(max_ready, 1)
                dve.wait_ge(max_turned, b + 1)
                link(v.tensor_reduce(max_row[0:1, 0, 0:QUAD].rearrange("p (h q) -> p h q", q=8),
                                     psum[0:1, MISC, 0:P].rearrange("p (h a q) -> p h q a", a=4, q=8), AX_X, ALU.max))
                v.tensor_scalar(max_row[0:1, 1, :].rearrange("p (h a q) -> p h a q", a=4, q=8),
                                max_row[0:1, 0, 0:QUAD].rearrange("p (h q) -> p h q", q=8).unsqueeze(2).to_broadcast([1, H, 4, 8]),
                                -1.0, None, ALU.mult).then_inc(max_spread, 1)
                dve.wait_ge(max_back, b + 1)
                v.tensor_copy(dec[:, 1:2], psum[:, MISC, 256:257]).then_inc(negmax_ready, 1)
                dve.wait_ge(p_turned, b + 1)
                for j in range(2, 4):
                    regroup(v.tensor_copy, j)
                v.tensor_copy(p_new[0:QUAD, :].rearrange("p (h q) -> p h q", q=8),
                              psum[0:QUAD, MISC, P:2 * P].rearrange("p (h a q) -> p h a q", a=4, q=8)[:, :, 0, :]).then_inc(p_by_dve, 1)
                link(v.tensor_reduce(dec[:, 12:13], psum[:, MISC, 384:384 + REVS + 1], AX_X, ALU.add))
                link(v.reciprocal(dec[:, 13:14], dec[:, 12:13]))
                link(v.tensor_tensor(dec[:, 14:15], dec[:, 13:14], COEF, ALU.mult))

            def scale_output(b):
                dve.wait_ge(v_free, RING + (b + 1) * (REVS * RING))
                v.tensor_scalar(o_scaled[:], psum[:, 2, 0:P], dec[:, 14:15], None, ALU.mult).then_inc(o_scaled_ready, 1)

            def step(b, h, half, first=False):
                if not first:
                    softmax(b - 1)
                queries(b)
                for r in range(REVS):
                    n, i = b * REVS + r, TILES[half][r]
                    for g in range(RING):
                        turn_keys(b, r, g)
                        if g < 2:
                            maxima(n, i, g)
                        elif g == 2:
                            combine(n, i)
                        else:
                            take_rows(h, n, i)
                if not first:
                    scale_output(b - 1)

            step(0, 0, 0, first=True)
            with linked_loop(H - 1, 2 * (4 + 7 * REVS)) as i:
                step(2 * i + 1, i, 1)
                step(2 * i + 2, i + 1, 0)
            step(B - 1, H - 1, 1)
            softmax(B - 1)
            scale_output(B - 1)
            stage_end(dve, 3)

            for n in range(NT * H):
                v.bn_aggr(o_moments[:, n, :], o_stats[:, 6 * n:6 * n + 6])
            dve.drain().then_inc(o_aggregated, 1)
            dve.wait_ge(o_aggregated, 1)
            o_mean, o_var = o_moments[:, :, 0], o_moments[:, :, 1]
            link(v.tensor_tensor(o_mean, o_mean, o_mean, ALU.mult))
            v.tensor_tensor(o_var, o_var, o_mean, ALU.add).then_inc(sq_ready, 1)
            o_t = o_t_all[:].rearrange("p b n -> p (b n)")
            v.tensor_tensor(o_t_sq[:], o_t, o_t, ALU.mult).then_inc(os_sq, 1)
            dve.wait_ge(sq_root, 1)
            link(v.reciprocal(o_var, o_var))
            for t in range(NT):
                rows = o_rows[:, t, :].rearrange("p (h d) -> p h d", d=HD)
                v.tensor_tensor(rows, rows, o_moments[:, t * H:(t + 1) * H, 1:2].to_broadcast([P, H, HD]), ALU.mult).then_inc(o_normed, 1)
            w_low(MIX0, 0)
            dve.wait_ge(y_hi_done, 1)
            link(v.tensor_tensor(x_lo[:, 0:CC // P, :], y_conv[:], x_hi[:, 0:CC // P, :], ALU.subtract))
            for t in range(NT):
                dve.wait_ge(o_hi_done, t + 1)
                at = slice(t * P, (t + 1) * P)
                for h in range(H):
                    k = CC // P + h
                    last = v.scalar_tensor_tensor(x_lo[:, k, at], psum[:, t % 4, h * P:(h + 1) * P], g_attn[:, 0:1], x_hi[:, k, at],
                                                  ALU.mult, ALU.subtract)
                last.then_inc(o_banks_free, 1)
            dve.wait_ge(os_root, 1)
            link(v.reciprocal(o_t_sq[:], o_t_sq[:]))
            link(v.tensor_tensor(o_t, o_t, o_t_sq[:], ALU.mult))
            v.tensor_scalar(x_t_s[:, CC // P:, :].rearrange("p h (b t) -> p b h t", t=S), o_t_all[:].rearrange("p b (h t) -> p b h t", t=S),
                            g_attn[:, 0:1], None, ALU.mult)
            dve.wait_ge(ys_turned, 1)
            v.tensor_copy(x_t_s[:, 0:CC // P, :].rearrange("p k n -> p (k n)"), psum[:, 5, 0:(CC // P) * QUAD]).then_inc(ys_ready, 1)

            def residual(x, got, gate, tmp, free, t, j):
                ins = v.tensor_tensor(tmp, got, gate, ALU.mult)
                ins.then_inc(free[0], 1)
                dve.wait_ge(free[0], free[1])
                link(v.scalar_tensor_tensor(x, x, z.ALPHA, tmp, ALU.mult, ALU.add))
                rows = x.shape[0]
                for i in range(x.shape[1] if len(x.shape) == 3 else 1):
                    at = (t + i) * 6 * NB_OUT + 6 * j
                    v.bn_stats(stats[0:rows, ds(at, 6)], x[:, i, :] if len(x.shape) == 3 else x)

            dve.wait_ge(x1_in, 16)
            for j in range(NB_OUT):
                n, s = MIX0 + j, j % 2
                if j + 1 < NB_OUT:
                    w_low(n + 1, 1 - s)
                take_quads(n, s)
                cols = slice(j * WB, (j + 1) * WB)
                for t in range(NT):
                    dve.wait_ge(tm_done, (6 + j) * NT + t + 1)
                    residual(x1[:, t, cols], psum[:, t % TB, 0:WB], gate_p[:, 0, cols], row_tmp[:, 0, :],
                             (tm_free, TB + (6 + j) * NT + t + 1), t, j)
                dve.wait_ge(s_folded, n + 1)
                residual(xs_rows[:, cols], psum[0:QUAD, 6 + s, 0:WB], gate_s[:, 0, cols], row_tmp[0:QUAD, 1, :],
                         (s_fold_free, 3 + n), NT, j)

            def moments(count):
                dve.drain().then_inc(moments_in, 1)
                dve.wait_ge(moments_in, count)
                for t in range(NT + 1):
                    rows = P if t < NT else QUAD
                    v.bn_aggr(rstd[0:rows, 2 * t:2 * t + 2], stats[0:rows, 6 * NB_OUT * t:6 * NB_OUT * (t + 1)])
                dve.drain().then_inc(var_ready, 1)
                dve.wait_ge(root_ready, count)
                pairs = rstd[:, 0:2 * NT].rearrange("p (t j) -> p t j", j=2)
                link(v.reciprocal(rstd[:, 32:32 + NT], pairs[:, :, 1]))
                link(v.reciprocal(rstd[0:QUAD, 32 + NT:33 + NT], rstd[0:QUAD, 2 * NT + 1:2 * NT + 2]))
                link(v.scalar_tensor_tensor(rstd[:, 48:48 + NT], pairs[:, :, 0], -1.0, rstd[:, 32:32 + NT], ALU.mult, ALU.mult))
                v.scalar_tensor_tensor(rstd[0:QUAD, 48 + NT:49 + NT], rstd[0:QUAD, 2 * NT:2 * NT + 1], -1.0,
                                       rstd[0:QUAD, 32 + NT:33 + NT], ALU.mult, ALU.mult).then_inc(norm_ready, 1)

            def normalise(t):
                return v.tensor_scalar(x1[:, t, :], x1[:, t, :], rstd[:, 2 * t:2 * t + 1], rstd[:, 32 + t:33 + t], ALU.subtract, ALU.mult)

            moments(1)
            for c in range(NCH):
                for t in range(c * TPC + 1, (c + 1) * TPC, 2):
                    normalise(t).then_inc(x1_odd_ready, 1)
                for k in range(KC):
                    split(UNITS + c * KC + k, c, k, x1_mod)
            dve.wait_ge(xs_turned, 2)
            modulate_sample(2, 3)

            dve.sem_inc(up_free, 2)
            dve.sem_inc(us_taken, 1)
            dve.sem_inc(gs_taken, 1)
            w_low(FF0, 0)

            def gate_up(i, more):
                w_low(FF0 + 1 + 2 * i, 1)
                take_quads(FF0 + 2 * i, 0)
                if more:
                    w_low(FF0 + 2 + 2 * i, 0)
                take_quads(FF0 + 1 + 2 * i, 1)
                for ft in range(FT):
                    dve.wait_ge(fm_done, 6 * FT + 2 * FT * i + (FT + ft + 1))
                    dve.wait_ge(gate_free, FT * i + ft + 1)
                    h = h_out[:, ft, :]
                    v.tensor_tensor(h, psum[:, 2 * ft:2 * ft + NCH, 0:CH].rearrange("p c n -> p (c n)"), h, ALU.mult).then_inc(up_free, 1)
                dve.wait_ge(s_folded, FF0 + 2 + 2 * i)
                dve.wait_ge(gs_taken, i + 2)
                v.tensor_tensor(h_s[:], psum[0:QUAD, 7, 0:WB], gate_act_s[:], ALU.mult).then_inc(us_taken, 1)
                dve.wait_ge(us_taken, i + 2)
                dve.sem_inc(hs_ready, 1)
                dve.wait_ge(hs_turned, i + 1)
                v.tensor_copy(h_t_s[:, ds(FT * i, FT), :], psum[:, 7, WB:WB + FT * QUAD].rearrange("p (f n) -> p f n", n=QUAD))

            with dve.Fori(0, NG - 1) as i:
                gate_up(i, True)
            gate_up(NG - 1, False)
            stage_end(dve, 4)

            dve.sem_inc(d_used, 4)
            dve.sem_inc(d_split, 2)
            dve.sem_inc(down_free, 2 * DB)
            dve.sem_inc(down_quads_in, 1)

            def take_pair(nb, turn):
                j = (DB - 1 + turn) % DB
                cols = slice(nb * WB, (nb + 1) * WB)
                got = psum[:, down_bank(nb % 2, j), 0:2 * WB].rearrange("p (t n) -> p t n", n=WB)
                gate = gate_p[:, 1, cols].unsqueeze(1).to_broadcast([P, 2, WB])
                residual(x1[:, 2 * j:2 * j + 2, cols], got, gate, down_tmp[:], (down_free, 2 * DB + nb * DB + turn + 1), 2 * j, nb)

            def take_quads_of(nb):
                dve.wait_ge(d_used, 4 + (nb + 1) * NF)
                v.tensor_copy(down_quads[:, nb * WB:(nb + 1) * WB], psum[:, 4, 0:WB]).then_inc(down_quads_in, 1)

            for nb in range(D // WB):
                for k in range(NF):
                    m, s = nb * NF + k, (nb * NF + k) % 4
                    dve.wait_ge(d_hi_done, m + 1)
                    v.tensor_tensor(h_lo[:, s, :], h_all[:, k, :], h_hi[:, s, :], ALU.subtract)
                    v.tensor_tensor(d_lo[:, s, :], d_raw[:, (k // 2) % 4, k % 2, :], d_hi[:, s, :], ALU.subtract).then_inc(d_split, 1)
                    if nb and k == 1:
                        take_quads_of(nb - 1)
                    if nb and k % 2 == 1 and k // 2 < min(DB, PAIRS):
                        take_pair(nb - 1, k // 2)
                for turn in range(PAIRS, DB if nb else 0):
                    take_pair(nb - 1, turn)
            take_quads_of(D // WB - 1)
            for turn in range(DB):
                take_pair(D // WB - 1, turn)
            dve.wait_ge(down_folded, 1)
            for nb in range(D // WB):
                cols = slice(nb * WB, (nb + 1) * WB)
                residual(xs_rows[:, cols], psum[0:QUAD, 1 + nb // 2, (nb % 2) * WB:(nb % 2 + 1) * WB], gate_s[:, 1, cols],
                         down_tmp[0:QUAD, 0, :], (down_s_free, nb + 1), NT, nb)
            moments(2)
            dve.wait_ge(ln_in, 64)
            for t in range(NT + 1):
                rows = P if t < NT else QUAD
                x = x1[:, t, :] if t < NT else xs_rows[:]
                if t == NT:
                    dve.wait_ge(xs_normed, 2)
                elif t % 2 == 0:
                    dve.wait_ge(x1_ready, NT // 2 + t // 2 + 1)
                else:
                    link(normalise(t))
                link(v.tensor_tensor(x, x, ln2_rows[0:rows, 0, :], ALU.mult))
                v.tensor_tensor(x, x, ln2_rows[0:rows, 1, :], ALU.add).then_inc(y_ready, 1)


_NAMES = ["x_prompt", "x_sample", "c_prompt", "c_sample", "cache_k", "cache_v", "state_conv", "page_table",
          "w_ada", "b_ada", "w_in", "conv_w", "lambda_q1", "lambda_k1", "lambda_q2", "lambda_k2", "subln_g",
          "w_out", "ln1_g", "ln1_b", "w_gate", "w_up", "w_down", "ln2_g", "ln2_b"]


def kernel(**inputs):
    import concourse.bacc as bacc
    from concourse.bass_utils import run_bass_kernel_spmd

    nc = bacc.Bacc("TRN2", target_bir_lowering=False, num_devices=1)
    arrays = {n: np.ascontiguousarray(inputs[n]) for n in _NAMES}
    z = Shapes({n: a.shape for n, a in arrays.items()})
    arrays["consts"], const_at = constants(z)
    io = {n: nc.dram_tensor(n, a.shape, mybir.dt.from_np(a.dtype), kind="ExternalInput").ap() for n, a in arrays.items()}
    outs = [("y_prompt", (1, z.T, z.D)), ("y_sample", (z.B, z.S, z.D)),
            ("new_k_prompt", (1, 1, z.T, z.H, z.HD)), ("new_v_prompt", (1, 1, z.T, z.H, z.HD)),
            ("new_conv_prompt", (1, 1, 2, z.CC)),
            ("new_k_sample", (1, z.B, z.S, z.H, z.HD)), ("new_v_sample", (1, z.B, z.S, z.H, z.HD)),
            ("new_conv_sample", (1, z.B, 2, z.CC))]
    for n, shape in outs:
        io[n] = nc.dram_tensor(n, shape, F32, kind="ExternalOutput").ap()
    build(nc, z, io, const_at, arrays["consts"].shape[1])
    r = run_bass_kernel_spmd(nc, [arrays], core_ids=[0])
    return tuple(r.results[0][n] for n, _ in outs)
```
